# Optimizing a Trainium2 kernel written in Bass

```python
import math
import jax, jax.numpy as jnp
from jax import lax
import numpy as np

D_MODEL = 1024
BATCH = 1
SEQ = 256
DEPTH = 1

HEAD_DIM = 64
DSWA_PATTERNS = ((128, 1), (512, 4), (2048, 16))
DSWA_HEADS_PER_GROUP = 4
DSWA_GROUPS = len(DSWA_PATTERNS)
DSWA_HEADS = DSWA_GROUPS * DSWA_HEADS_PER_GROUP
FOX_HEADS = 8
ATTN_BLOCK = 128
NUM_BUCKETS = 32
MAX_DISTANCE = 2048
N_EXPERTS = 32
TOP_K = 4
D_FF_EXPERT = D_MODEL
SWIGLU_LIMIT = 7.0
SWIGLU_ALPHA = 1.702
EXPERT_BLOCK = 256
RMS_EPS = 1e-6
NEG_INF = -1e30

DSWA_WIDTH = DSWA_HEADS * HEAD_DIM
DSWA_OUT_WIDTH = DSWA_HEADS_PER_GROUP * HEAD_DIM
FOX_WIDTH = FOX_HEADS * HEAD_DIM
IN_PROJ_WIDTH = 3 * DSWA_WIDTH + 3 * FOX_WIDTH + FOX_HEADS + 2 * D_MODEL

kernel_name = "hybrid_dilated_fox_moe_layer"

def rmsnorm(x, g):
    xf = x.astype(jnp.float32)
    y = xf * lax.rsqrt(jnp.mean(xf * xf, axis=-1, keepdims=True) + RMS_EPS)
    return (y * g.astype(jnp.float32)).astype(x.dtype)

def t5_bucket(n):
    max_exact = NUM_BUCKETS // 2
    n_safe = np.maximum(n, 1).astype(np.float64)
    large = max_exact + (np.log(n_safe / max_exact) / np.log(MAX_DISTANCE / max_exact)
                         * (NUM_BUCKETS - max_exact)).astype(np.int64)
    large = np.minimum(large, NUM_BUCKETS - 1)
    return np.where(n < max_exact, n, large).astype(np.int32)

def dilated_window_attention(q, k, v, bias_table, window, dilation):
    B, S, H, Dh = q.shape
    steps = window // dilation
    L = S // dilation
    c = math.gcd(L, ATTN_BLOCK)
    nblk = L // c
    span = c + steps

    def by_residue(t):
        return t.reshape(B, L, dilation, H, Dh).transpose(0, 2, 3, 1, 4)

    qs = by_residue(q).reshape(B, dilation, H, nblk, c, Dh)
    pad = ((0, 0), (0, 0), (0, 0), (steps, 0), (0, 0))
    kp = jnp.pad(by_residue(k), pad)
    vp = jnp.pad(by_residue(v), pad)
    key_idx = np.arange(nblk)[:, None] * c + np.arange(span)[None, :]
    kblk = kp[:, :, :, key_idx]
    vblk = vp[:, :, :, key_idx]
    back = np.arange(c)[:, None] + steps - np.arange(span)[None, :]
    valid = ((back >= 0) & (back <= steps))[None] & ((key_idx - steps)[:, None, :] >= 0)
    bucket = t5_bucket(np.clip(back, 0, steps) * dilation)
    bias = jnp.transpose(bias_table[bucket], (2, 0, 1)).astype(jnp.float32)
    s = jnp.einsum('bzhnqd,bzhnkd->bzhnqk', qs, kblk).astype(jnp.float32) * (Dh ** -0.5) + bias[:, None]
    s = jnp.where(valid, s, NEG_INF)
    m = jnp.max(s, axis=-1, keepdims=True)
    p = jnp.exp(s - m)
    den = jnp.sum(p, axis=-1, keepdims=True)
    o = jnp.einsum('bzhnqk,bzhnkd->bzhnqd', p.astype(v.dtype), vblk).astype(jnp.float32) / den
    lse = (m + jnp.log(den))[..., 0]
    o = o.reshape(B, dilation, H, L, Dh).transpose(0, 3, 1, 2, 4).reshape(B, S, H, Dh)
    lse = lse.reshape(B, dilation, H, L).transpose(0, 3, 1, 2).reshape(B, S, H)
    return o, lse

def forgetting_attention(q, k, v, log_f):
    B, S, H, Dh = q.shape
    nq = S // ATTN_BLOCK
    c = jnp.cumsum(log_f, axis=1)
    ck = c.transpose(0, 2, 1)
    qblk = q.reshape(B, nq, ATTN_BLOCK, H, Dh).transpose(1, 0, 2, 3, 4)
    cblk = c.reshape(B, nq, ATTN_BLOCK, H).transpose(1, 0, 3, 2)
    kpos = jnp.arange(S)

    def one_block(args):
        qb, cq, i = args
        s = jnp.einsum('bqhd,bkhd->bhqk', qb, k).astype(jnp.float32) * (Dh ** -0.5)
        s = s + cq[..., None] - ck[:, :, None, :]
        qpos = i * ATTN_BLOCK + jnp.arange(ATTN_BLOCK)
        s = jnp.where(qpos[:, None] >= kpos[None, :], s, NEG_INF)
        p = jax.nn.softmax(s, axis=-1)
        return jnp.einsum('bhqk,bkhd->bqhd', p.astype(v.dtype), v)

    o = lax.map(one_block, (qblk, cblk, jnp.arange(nq)))
    return o.transpose(1, 0, 2, 3, 4).reshape(B, S, H * Dh)

def routed_ffn(h, w_router, b_router, w_gate_up, b_gate_up, w_down, b_down):
    B, S, D = h.shape
    N = B * S
    xt = h.reshape(N, D)
    logits = (xt @ w_router + b_router).astype(jnp.float32)
    top_v, top_i = lax.top_k(logits, TOP_K)
    gate = jax.nn.softmax(top_v, axis=-1)
    A = N * TOP_K
    flat_e = top_i.reshape(-1)
    flat_tok = jnp.arange(A, dtype=jnp.int32) // TOP_K
    order = jnp.argsort(flat_e)
    se = flat_e[order]
    stok = flat_tok[order]
    sgate = gate.reshape(-1)[order]
    counts = jnp.zeros((N_EXPERTS,), jnp.int32).at[flat_e].add(1)
    starts = jnp.cumsum(counts) - counts
    pcounts = ((counts + EXPERT_BLOCK - 1) // EXPERT_BLOCK) * EXPERT_BLOCK
    pends = jnp.cumsum(pcounts)
    pstarts = pends - pcounts
    dest = pstarts[se] + jnp.arange(A, dtype=jnp.int32) - starts[se]
    P = A + N_EXPERTS * EXPERT_BLOCK
    nblk = P // EXPERT_BLOCK
    row_tok = jnp.full((P,), N, jnp.int32).at[dest].set(stok)
    row_gate = jnp.zeros((P,), jnp.float32).at[dest].set(sgate)
    blk_e = jnp.minimum(jnp.searchsorted(pends, jnp.arange(nblk) * EXPERT_BLOCK, side='right'),
                        N_EXPERTS - 1)
    x_pad = jnp.concatenate([xt, jnp.zeros((1, D), xt.dtype)], axis=0)

    def expert_block(args):
        tok, e = args
        xb = x_pad[tok]
        gu = xb @ w_gate_up[e] + b_gate_up[e]
        g, u = gu[:, :D_FF_EXPERT], gu[:, D_FF_EXPERT:]
        g = jnp.minimum(g, SWIGLU_LIMIT)
        u = jnp.clip(u, -SWIGLU_LIMIT, SWIGLU_LIMIT)
        mid = (u + 1) * (g * jax.nn.sigmoid(SWIGLU_ALPHA * g))
        return mid @ w_down[e] + b_down[e]

    yb = lax.map(expert_block, (row_tok.reshape(nblk, EXPERT_BLOCK), blk_e)).reshape(P, D)
    y = jnp.zeros((N + 1, D), h.dtype).at[row_tok].add(yb * row_gate[:, None].astype(yb.dtype))
    return y[:N].reshape(B, S, D)

def hybrid_layer(x, ln1_g, w_in, b_forget, b_gate, q_norm_a, k_norm_a, q_norm_b, k_norm_b, rel_bias,
                 w_branch_a, w_branch_b, w_out, ln2_g, w_router, b_router, w_gate_up, b_gate_up,
                 w_down, b_down):
    B, S, D = x.shape
    h = rmsnorm(x, ln1_g)
    proj = h @ w_in
    o0 = 0
    qa = proj[..., o0:o0 + DSWA_WIDTH]; o0 += DSWA_WIDTH
    ka = proj[..., o0:o0 + DSWA_WIDTH]; o0 += DSWA_WIDTH
    va = proj[..., o0:o0 + DSWA_WIDTH]; o0 += DSWA_WIDTH
    qb = proj[..., o0:o0 + FOX_WIDTH]; o0 += FOX_WIDTH
    kb = proj[..., o0:o0 + FOX_WIDTH]; o0 += FOX_WIDTH
    vb = proj[..., o0:o0 + FOX_WIDTH]; o0 += FOX_WIDTH
    f_logit = proj[..., o0:o0 + FOX_HEADS]; o0 += FOX_HEADS
    g_logit = proj[..., o0:o0 + 2 * D]

    shp_a = (B, S, DSWA_GROUPS, DSWA_HEADS_PER_GROUP, HEAD_DIM)
    qa = rmsnorm(qa.reshape(shp_a), q_norm_a)
    ka = rmsnorm(ka.reshape(shp_a), k_norm_a)
    va = va.reshape(shp_a)
    outs, lses = [], []
    for g, (window, dilation) in enumerate(DSWA_PATTERNS):
        cols = rel_bias[:, g * DSWA_HEADS_PER_GROUP:(g + 1) * DSWA_HEADS_PER_GROUP]
        o, l = dilated_window_attention(qa[:, :, g], ka[:, :, g], va[:, :, g], cols, window, dilation)
        outs.append(o)
        lses.append(l)
    mix = jax.nn.softmax(jnp.stack(lses, axis=0), axis=0)
    o_a = jnp.sum(mix[..., None] * jnp.stack(outs, axis=0), axis=0).astype(x.dtype)
    o_a = o_a.reshape(B, S, DSWA_OUT_WIDTH)

    shp_b = (B, S, FOX_HEADS, HEAD_DIM)
    qb = rmsnorm(qb.reshape(shp_b), q_norm_b)
    kb = rmsnorm(kb.reshape(shp_b), k_norm_b)
    log_f = jax.nn.log_sigmoid((f_logit + b_forget).astype(jnp.float32))
    o_b = forgetting_attention(qb, kb, vb.reshape(shp_b), log_f)

    gate = jax.nn.sigmoid((g_logit + b_gate).astype(jnp.float32)).astype(x.dtype)
    merged = gate[..., :D] * (o_a @ w_branch_a) + gate[..., D:] * (o_b @ w_branch_b)
    x = x + merged @ w_out
    x = x + routed_ffn(rmsnorm(x, ln2_g), w_router, b_router, w_gate_up, b_gate_up, w_down, b_down)
    return x

def setup_inputs(seed: int = 0) -> dict:
    key = jax.random.key(seed)
    ks = jax.random.split(key, 20)
    f32 = jnp.float32
    nrm = lambda k, shape, s: jax.random.normal(k, shape, f32) * s
    return {
        "x": nrm(ks[0], (BATCH, SEQ, D_MODEL), 1.0),
        "ln1_g": 1.0 + nrm(ks[1], (DEPTH, D_MODEL), 0.02),
        "w_in": nrm(ks[2], (DEPTH, D_MODEL, IN_PROJ_WIDTH), D_MODEL ** -0.5),
        "b_forget": jnp.linspace(1.0, 6.0, FOX_HEADS, dtype=f32)[None, :] + nrm(ks[3], (DEPTH, FOX_HEADS), 0.1),
        "b_gate": nrm(ks[4], (DEPTH, 2 * D_MODEL), 0.1),
        "q_norm_a": 1.0 + nrm(ks[5], (DEPTH, HEAD_DIM), 0.02),
        "k_norm_a": 1.0 + nrm(ks[6], (DEPTH, HEAD_DIM), 0.02),
        "q_norm_b": 1.0 + nrm(ks[7], (DEPTH, HEAD_DIM), 0.02),
        "k_norm_b": 1.0 + nrm(ks[8], (DEPTH, HEAD_DIM), 0.02),
        "rel_bias": nrm(ks[9], (NUM_BUCKETS, DSWA_HEADS), 0.5),
        "w_branch_a": nrm(ks[10], (DEPTH, DSWA_OUT_WIDTH, D_MODEL), DSWA_OUT_WIDTH ** -0.5),
        "w_branch_b": nrm(ks[11], (DEPTH, FOX_WIDTH, D_MODEL), FOX_WIDTH ** -0.5),
        "w_out": nrm(ks[12], (DEPTH, D_MODEL, D_MODEL), D_MODEL ** -0.5),
        "ln2_g": 1.0 + nrm(ks[13], (DEPTH, D_MODEL), 0.02),
        "w_router": nrm(ks[14], (DEPTH, D_MODEL, N_EXPERTS), D_MODEL ** -0.5),
        "b_router": nrm(ks[15], (DEPTH, N_EXPERTS), 0.01),
        "w_gate_up": nrm(ks[16], (DEPTH, N_EXPERTS, D_MODEL, 2 * D_FF_EXPERT), D_MODEL ** -0.5),
        "b_gate_up": nrm(ks[17], (DEPTH, N_EXPERTS, 2 * D_FF_EXPERT), 0.01),
        "w_down": nrm(ks[18], (DEPTH, N_EXPERTS, D_FF_EXPERT, D_MODEL), D_FF_EXPERT ** -0.5),
        "b_down": nrm(ks[19], (DEPTH, N_EXPERTS, D_MODEL), 0.01),
    }

def reference(x, ln1_g, w_in, b_forget, b_gate, q_norm_a, k_norm_a, q_norm_b, k_norm_b, rel_bias,
              w_branch_a, w_branch_b, w_out, ln2_g, w_router, b_router, w_gate_up, b_gate_up,
              w_down, b_down):
    for layer in range(DEPTH):
        x = hybrid_layer(x, ln1_g[layer], w_in[layer], b_forget[layer], b_gate[layer],
                         q_norm_a[layer], k_norm_a[layer], q_norm_b[layer], k_norm_b[layer], rel_bias,
                         w_branch_a[layer], w_branch_b[layer], w_out[layer], ln2_g[layer],
                         w_router[layer], b_router[layer], w_gate_up[layer], b_gate_up[layer],
                         w_down[layer], b_down[layer])
    return x


_drawn_inputs = setup_inputs


def setup_inputs(seed=0):
    import zlib

    import numpy as np

    out = dict(_drawn_inputs(seed))
    spreads = {}
    factors = {'ln1_g': 2.784,
     'b_gate': 2.881,
     'q_norm_a': 6.904,
     'k_norm_a': 4.896,
     'q_norm_b': 7.674,
     'k_norm_b': 3.592,
     'b_gate_up': 23.79,
     'b_down': 27.471,
     'ln2_g': 2.683,
     'b_router': 4.064}
    for name, (base, spread) in spreads.items():
        noise = np.random.default_rng([zlib.crc32(name.encode()), seed]).standard_normal(out[name].shape)
        drawn = base * np.exp(spread * noise) if base else spread * noise
        out[name] = __import__('jax').numpy.asarray(drawn.astype(out[name].dtype))
    for name, factor in factors.items():
        out[name] = (out[name] * factor).astype(out[name].dtype)
    return out
```

```python
from contextlib import ExitStack

import numpy as np

import concourse.bass as bass
from concourse import mybir

F32 = mybir.dt.float32
I32 = mybir.dt.int32
U32 = mybir.dt.uint32
ALU = mybir.AluOpType
ACT = mybir.ActivationFunctionType
AX_X = mybir.AxisListType.X

P = 128
D = 1024
SEQ = 256
TT = SEQ // P
KB = D // P
HD = 64
GROUPS, SLOTHEADS = 3, 4
AH = GROUPS * SLOTHEADS
AW = AH * HD
FH = 8
FW = FH * HD
EPS = 1e-6
NEG = -1e30
NB = 32
NE = 32
TOPK = 4
LIMIT, ALPHA = 7.0, 1.702
SLOTS = 64
MAXPASS = SEQ // SLOTS
BIG = 10000.0

RING = 6
SLOT = 4096
BANK = 512

QKW = 2 * AW + 2 * FW
VW = AW + FW
IN_CHUNKS = [
    (0, 512, [(0, 512, "qk", 0)]),
    (512, 512, [(0, 512, "qk", 512)]),
    (1024, 512, [(0, 512, "qk", 1024)]),
    (1536, 512, [(0, 512, "v", 0)]),
    (2048, 512, [(0, 256, "v", 512), (256, 256, "qk", 1536)]),
    (2560, 512, [(0, 512, "qk", 1792)]),
    (3072, 512, [(0, 256, "qk", 2304), (256, 256, "v", 768)]),
    (3584, 264, [(0, 256, "v", 1024), (256, 8, "f", 0)]),
    (3848, 512, [(0, 512, "g", 0)]),
    (4360, 512, [(0, 512, "g", 512)]),
    (4872, 512, [(0, 512, "g", 1024)]),
    (5384, 512, [(0, 512, "g", 1536)]),
]
NIN = len(IN_CHUNKS)
GATE0 = 8
QK_BATCHES = [(0, 4, 0), (4, 2, 0), (6, 4, 1), (10, 2, 1), (12, 4, 2), (16, 4, 3)]
FLIP_AT = 2
TOEP = 2 * P + P

UNITS = ([("a", t, s) for t in range(TT) for s in range(SLOTHEADS)]
         + [("b", t, h) for t in range(TT) for h in range(FH)])
NU = len(UNITS)
NUA = TT * SLOTHEADS


def unit_blocks(u):
    kind, t, _ = UNITS[u]
    if kind == "a" and t == 1:
        return [[(g, k) for g, k in ((0, 0), (0, 1), (1, 0))], [(g, k) for g, k in ((1, 1), (2, 0), (2, 1))]]
    if kind == "a":
        return [[(0, 0), (1, 0), (2, 0)]]
    return [[(0, k) for k in range(t + 1)]]


PIECES = [(u, piece) for u in range(NU) for piece in unit_blocks(u)]
LAST_PIECE = [max(i for i, (v, _) in enumerate(PIECES) if v == u) for u in range(NU)]


def build(nc, a, out):
    with ExitStack() as ctx:
        def sb(name, shape, dt=F32):
            return ctx.enter_context(nc.sbuf_tensor(name, shape, dt))

        def sem(name):
            return ctx.enter_context(nc.semaphore(name))

        ring = [sb(f"ring{i}", [P, SLOT]) for i in range(RING)]
        ps = [ctx.enter_context(nc.psum_tensor(f"ps{i}", [P, 2 * BANK], F32)) for i in range(4)]

        def bank(i):
            return ps[i // 2][:, (i % 2) * BANK:(i % 2 + 1) * BANK]

        xres = sb("xres", [P, TT, D])
        reg_n = sb("reg_n", [P, TT * D])
        reg_t = sb("reg_t", [P, KB * SEQ])
        reg_a = sb("reg_a", [P, TT * QKW])
        reg_b = sb("reg_b", [P, TT * QKW])
        vals = sb("vals", [P, TT, VW])
        gates = sb("gates", [P, TT, 2 * D])
        reg_r = sb("reg_r", [P, AH * SEQ])

        h = reg_n[:, :].rearrange("p (t d) -> p t d", t=TT)
        gate_bias = reg_n[:, :]
        merged = h
        hn = h
        hT = reg_t[:, :].rearrange("p (k s) -> p k s", k=KB)
        oT = reg_t[:, 0:6 * SEQ].rearrange("p (k s) -> p k s", k=6)
        qk = reg_a[:, :].rearrange("p (t d) -> p t d", t=TT)
        sq = reg_b[:, :].rearrange("p (t d) -> p t d", t=TT)
        qkT = reg_b[:, :].rearrange("p (k s) -> p k s", k=QKW // P)
        mT = reg_b[:, 0:KB * SEQ].rearrange("p (k s) -> p k s", k=KB)
        bgu = reg_b[:, 2048:4096]
        bdown = reg_b[:, 4096:5120]
        toep = reg_r[:, :].rearrange("p (h c) -> p h c", h=AH)
        prod = reg_r[:, 0:2048].rearrange("p (i b c) -> p i b c", i=2, b=2)

        onehot = reg_b[0:NB, 0:TOEP]
        rmask = reg_b[0:AH, TOEP:2 * TOEP]
        rrow = reg_b[0:AH, 2 * TOEP:3 * TOEP]
        rel = reg_b[0:NB, 3 * TOEP:3 * TOEP + AH]
        vflat = vals[:, :, :].rearrange("p t d -> p (t d)")
        hw = TT * TOPK * NE
        hit = vflat[:, 0:hw].rearrange("p (t k e) -> p t k e", t=TT, k=TOPK)
        ghit = vflat[:, hw:2 * hw].rearrange("p (t k e) -> p t k e", t=TT, k=TOPK)
        GT = vflat[0:NE, 2 * hw:2 * hw + SEQ]
        logits, mask, G, posm = (vflat[:, 3 * hw + i * TT * NE:3 * hw + (i + 1) * TT * NE]
                                 .rearrange("p (t e) -> p t e", t=TT) for i in range(4))

        at = [0]

        def take(n):
            at[0] += n
            assert at[0] <= TT * QKW
            return reg_a[:, at[0] - n:at[0]]

        probs = [take(3 * SEQ) for _ in range(2)]
        probsT = [take(3 * SEQ) for _ in range(2)]
        o_a = take(TT * SLOTHEADS * HD).rearrange("p (t d) -> p t d", t=TT)
        o_b = take(TT * FW).rearrange("p (t d) -> p t d", t=TT)
        at[0] = 0
        xT = take(KB * SLOTS).rearrange("p (k s) -> p k s", k=KB)
        glu_g, glu_u, glu_s, mid = [take(2 * P) for _ in range(4)]
        midT = take(4 * P).rearrange("p (j b s) -> p j b s", j=2, b=2)
        yb = take(BANK)
        pick = take(TT * SLOTS).rearrange("p (t s) -> p t s", t=TT)
        gpick = take(TT * P).rearrange("p (t s) -> p t s", t=TT)
        gpickT = take(TT * P)
        sel_e = take(SLOTS)
        cols = take(5)
        take(3)
        table = take(5 * (MAXPASS * NE + 1)).rearrange("p (e c) -> p e c", c=5)

        zeros = h[:, 0, 0:SEQ]
        ident = sb("ident", [P, P])
        anti = sb("anti", [P, P])
        ones = sb("ones", [P, P])
        tri_le = sb("tri_le", [P, P])
        tri_lt = sb("tri_lt", [P, P])
        causal = sb("causal", [P, SEQ])
        iota_i = sb("iota_i", [P, P], I32)
        slot_no = sb("slot_no", [P, P])
        exp_i = sb("exp_i", [P, NE], I32)
        exp_no = sb("exp_no", [P, NE])
        thr_i = sb("thr_i", [P, MAXPASS - 1], I32)
        thr = sb("thr", [P, MAXPASS - 1])
        g1 = sb("g1", [P, KB])
        g2 = sb("g2", [P, KB])
        gain = sb("gain", [P, 4])
        fbias = sb("fbias", [P, FH])
        rbias = sb("rbias", [P, NE])
        wr = sb("wr", [P, KB, NE])
        stat = sb("stat", [P, 4, TT])
        qstat = sb("qstat", [P, 2, TT, QKW // HD])
        fz = sb("fz", [P, TT, FH])
        fw = sb("fw", [P, 3, TT, FH])
        logf = sb("logf", [P, TT, FH])
        cum = sb("cum", [P, TT, FH])
        negcT = sb("negcT", [FH, SEQ])
        amax = sb("amax", [P, NU])
        nmax = sb("nmax", [P, NU])
        den = sb("den", [P, NU])
        rden = sb("rden", [P, NU])
        top = sb("top", [P, TT, 8])
        topi = sb("topi", [P, TT, 8], U32)
        topf = sb("topf", [P, TT, TOPK])
        ntop = sb("ntop", [P, TT])
        egate = sb("egate", [P, TT, TOPK])
        esum = sb("esum", [P, TT])
        ersum = sb("ersum", [P, TT])
        cmax = sb("cmax", [P, 1])
        over = sb("over", [P, MAXPASS - 1])
        more = sb("more", [P, 1])
        counts = sb("counts", [P, 2], I32)

        scratch = nc.dram_tensor("rel_rows", [AH * TOEP], F32, kind="Internal")

        landed = [sem(f"landed{i}") for i in range(RING)]
        used = sem("used")
        x_in, small_in, gbias_in, ebias_in = sem("x_in"), sem("small_in"), sem("gbias_in"), sem("ebias_in")
        consts = sem("consts")
        sq1, var1, std1, rstd1, h_ok, hT_ps, hT_ok = (sem(n) for n in (
            "sq1", "var1", "std1", "rstd1", "h_ok", "hT_ps", "hT_ok"))
        flip_ps, flip_ok = sem("flip_ps"), sem("flip_ok")
        gain_ok, rel_ps, rel_ok, rel_out, rel_in = (sem(n) for n in ("gain_ok", "rel_ps", "rel_ok", "rel_out", "rel_in"))
        proj, ev_act, ev_dve = sem("proj"), sem("ev_act"), sem("ev_dve")
        gexp, gone, gate_ok = sem("gexp"), sem("gone"), sem("gate_ok")
        qsq, qsum, qvar, qstd, qrstd, qn = (sem(n) for n in ("qsq", "qsum", "qvar", "qstd", "qrstd", "qn"))
        qT_ps, qT_ok = sem("qT_ps"), sem("qT_ok")
        fstep, fexp, fln, logf_ok, cum_ps, cum_ok = (sem(n) for n in (
            "fstep", "fexp", "fln", "logf_ok", "cum_ps", "cum_ok"))
        sc_ps, sc_add, mx, nmx, pr_ok = (sem(n) for n in ("sc_ps", "sc_add", "mx", "nmx", "pr_ok"))
        pT_ps, pT_act, pT_dve, pv, rden_ok, o_ok = (sem(n) for n in ("pT_ps", "pT_act", "pT_dve", "pv", "rden_ok", "o_ok"))
        oT_ps, oT_act, oT_dve, br_ps, br_mul, merged_ok = (sem(n) for n in (
            "oT_ps", "oT_act", "oT_dve", "br_ps", "br_mul", "merged_ok"))
        mT_ps, mT_ok, wo_ps, x1_ok = (sem(n) for n in ("mT_ps", "mT_ok", "wo_ps", "x1_ok"))
        sq2, var2, std2, rstd2, hn_ok, h2_ps, h2_ok = (sem(n) for n in (
            "sq2", "var2", "std2", "rstd2", "hn_ok", "h2_ps", "h2_ok"))
        lg_ps, lg_ok, tops, topm, gexp2, rt, mask_ok = (sem(n) for n in (
            "lg_ps", "lg_ok", "tops", "topm", "gexp2", "rt", "mask_ok"))
        pos_ps, GT_ps, GT_ok, tab_ok, cnt_ok = (sem(n) for n in ("pos_ps", "GT_ps", "GT_ok", "tab_ok", "cnt_ok"))
        zero_ok = sem("zero_ok")
        col_ok, pick_ok, xg_ps, xg_ok, gp_ps, gp_ok = (sem(n) for n in (
            "col_ok", "pick_ok", "xg_ps", "xg_ok", "gp_ps", "gp_ok"))
        gu_ps, g_ok, sig_ok, u_ok, ug_ok, mid_ok, midT_ps, midT_ok = (sem(n) for n in (
            "gu_ps", "g_ok", "sig_ok", "u_ok", "ug_ok", "mid_ok", "midT_ps", "midT_ok"))
        dn_ps, yb_ok, scat = sem("dn_ps"), sem("yb_ok"), sem("scat")
        fin, stored = sem("fin"), sem("stored")

        n_pre = NIN + 4
        lands = [[16 * (i // RING + 1)] for i in range(n_pre)]
        extra = {NIN % RING: NIN}

        def landing(n):
            s = n % RING
            return 16 * (n // RING + 1) + (16 if s in extra and n >= extra[s] else 0)

        pre_land = [max([landing(n) for n in range(n_pre) if n % RING == s]) for s in range(RING)]
        PER = 6

        def eslot(c):
            return (n_pre + c) % RING

        w_in = a["w_in"][0]

        def expert_load(eng, e, c):
            slot = ring[eslot(c)]
            if c < 4:
                j, kh = c // 2, c % 2
                src = a["w_gate_up"][0][bass.ds(e, 1)].rearrange(
                    "o (p k) (w j c) -> p (o k) w j c", k=KB, w=2, j=2)[:, kh * 4:kh * 4 + 4, :, j, :]
                dst = slot[:, :].rearrange("p (k w c) -> p k w c", k=4, w=2)
                for w in range(2):
                    eng.dma_start(dst[:, :, w, :], src[:, :, w, :]).then_inc(landed[eslot(c)], 16)
            else:
                kh = c - 4
                src = a["w_down"][0][bass.ds(e, 1)].rearrange("o (k p) c -> p (o k) c", p=P)[:, kh * 4:kh * 4 + 4, :]
                eng.dma_start(slot[:, :].rearrange("p (k c) -> p k c", k=4), src).then_inc(landed[eslot(c)], 16)

        def eland(c):
            return 32 if c < 4 else 16

        block = ctx.enter_context(nc.Block())

        @block.sync
        def _(sp):
            for t in range(TT):
                sp.dma_start(xres[:, t, :], a["x"][0, t * P:(t + 1) * P, :]).then_inc(x_in, 16)
            for n, (c0, w, _) in enumerate(IN_CHUNKS):
                if n >= RING:
                    sp.wait_ge(used, n - RING + 1)
                sp.dma_start(ring[n % RING][:, 0:KB * w].rearrange("p (k c) -> p k c", k=KB),
                             w_in.rearrange("(p k) c -> p k c", k=KB)[:, :, c0:c0 + w]).then_inc(landed[n % RING], 16)
            wbr = [(NIN, 0, a["w_branch_a"][0], 0, 2), (NIN, 2, a["w_branch_b"][0], 0, 2),
                   (NIN + 1, 0, a["w_branch_b"][0], 2, 2), (NIN + 2, 0, a["w_out"][0], 0, 4),
                   (NIN + 3, 0, a["w_out"][0], 4, 4)]
            for n, k0, w, b0, nb in wbr:
                sp.wait_ge(used, n - RING + 1)
                sp.dma_start(ring[n % RING][:, k0 * D:(k0 + nb) * D].rearrange("p (k c) -> p k c", k=nb),
                             w.rearrange("(k p) c -> p k c", p=P)[:, b0:b0 + nb, :]).then_inc(landed[n % RING], 16)
            with sp.Fori(0, NE) as e:
                for c in range(PER):
                    sp.wait_ge(used, e * PER + (n_pre + c - RING + 1))
                    expert_load(sp, e, c)
            sp.wait_ge(cnt_ok, 3)
            passes = sp.value_load(counts[0:1, 1:2], min_val=1, max_val=MAXPASS)
            with sp.If(passes > 1):
                with sp.Fori(1, passes) as q:
                    with sp.Fori(0, NE) as e:
                        for c in range(PER):
                            sp.wait_ge(used, (q * NE + e) * PER + (n_pre + c - RING + 1))
                            expert_load(sp, e, c)
            for t in range(TT):
                sp.wait_ge(fin, t + 1)
                sp.dma_start(out[0, t * P:(t + 1) * P, :], xres[:, t, :]).then_inc(stored, 16)
            sp.wait_ge(stored, 16 * TT)

        @block.gpsimd
        def _(pool):
            pool.memset(ones[:, :], 1.0).then_inc(consts, 1)
            pool.memset(zeros, 0.0).then_inc(consts, 1)
            pool.wait_ge(consts, 2)
            pool.affine_select(out=ident[:, :], in_=zeros[:, 0:P], compare_op=ALU.not_equal, fill=1.0, base=0,
                               pattern=[[-1, P]], channel_multiplier=1).then_inc(consts, 1)
            pool.affine_select(out=tri_le[:, :], in_=ones[:, :], compare_op=ALU.is_ge, fill=0.0, base=0,
                               pattern=[[1, P]], channel_multiplier=-1).then_inc(consts, 1)
            pool.affine_select(out=tri_lt[:, :], in_=ones[:, :], compare_op=ALU.is_gt, fill=0.0, base=0,
                               pattern=[[1, P]], channel_multiplier=-1).then_inc(consts, 1)
            pool.affine_select(out=causal[:, :], in_=zeros, compare_op=ALU.is_ge, fill=NEG, base=P,
                               pattern=[[-1, SEQ]], channel_multiplier=1).then_inc(consts, 1)
            pool.iota(iota_i[:, :], pattern=[[0, 2], [1, SLOTS]], base=0, channel_multiplier=0).then_inc(consts, 1)
            pool.iota(exp_i[:, :], pattern=[[1, NE]], base=0, channel_multiplier=0).then_inc(consts, 1)
            pool.iota(thr_i[:, :], pattern=[[SLOTS, MAXPASS - 1]], base=SLOTS, channel_multiplier=0).then_inc(consts, 1)
            pool.wait_ge(consts, 9)
            pool.tensor_copy(slot_no[:, :], iota_i[:, :]).then_inc(consts, 1)
            pool.tensor_copy(exp_no[:, :], exp_i[:, :]).then_inc(consts, 1)
            pool.tensor_copy(thr[:, :], thr_i[:, :]).then_inc(consts, 1)
            pool.affine_select(out=anti[:, :], in_=zeros[:, 0:P], compare_op=ALU.not_equal, fill=1.0, base=1 - P,
                               pattern=[[1, P]], channel_multiplier=1).then_inc(consts, 1)
            for t in range(TT):
                pool.wait_ge(ev_act, 7)
                pool.wait_ge(ev_dve, 7)
                pool.wait_ge(rel_in, 16)
                pool.tensor_tensor(sq[:, t, :], qk[:, t, :], qk[:, t, :], ALU.mult).then_inc(qsq, 1)
            pool.wait_ge(tab_ok, 1)
            pool.wait_ge(cnt_ok, 3)
            steps = pool.value_load(counts[0:1, 0:1], min_val=NE, max_val=MAXPASS * NE)

            def select(t, first):
                pool.tensor_copy(cols, table[:, bass.ds(t, 1), :].rearrange("p o c -> p (o c)")).then_inc(col_ok, 1)
                pool.wait_ge(col_ok, t + 1)
                if not first:
                    pool.wait_ge(xg_ps, t)
                    pool.wait_ge(gp_ps, t)
                    pool.wait_ge(gu_ps, 2 * t)
                pool.tensor_tensor(sel_e, ones[:, 0:SLOTS], cols[:, 4:5].to_broadcast([P, SLOTS]), ALU.mult)
                for tt in range(TT):
                    pool.tensor_scalar(pick[:, tt, :], slot_no[:, 0:SLOTS], cols[:, tt:tt + 1], None, ALU.is_equal)
                for tt in range(TT):
                    last = pool.tensor_scalar(gpick[:, tt, :], slot_no[:, :], cols[:, tt:tt + 1],
                                              cols[:, 2 + tt:3 + tt], ALU.is_equal, ALU.mult)
                last.then_inc(pick_ok, 1)

            select(0, True)
            with pool.Fori(0, steps) as t:
                pool.wait_ge(pick_ok, t + 1)
                select(t + 1, False)

        @block.scalar
        def _(act):
            small = [
                (g1[:, :], a["ln1_g"][0].rearrange("(p k) -> p k", k=KB)),
                (g2[:, :], a["ln2_g"][0].rearrange("(p k) -> p k", k=KB)),
                (fbias[:, :], a["b_forget"][0:1, :].to_broadcast([P, FH])),
                (rbias[:, :], a["b_router"][0:1, :].to_broadcast([P, NE])),
                (wr[:, :, :], a["w_router"][0].rearrange("(p k) e -> p k e", k=KB)),
                (rel, a["rel_bias"]),
                (onehot, a["bucket_onehot"]),
                (rmask, a["reach_mask"]),
            ]
            for i, n in enumerate(("q_norm_a", "k_norm_a", "q_norm_b", "k_norm_b")):
                for half in range(2):
                    small.append((gain[half * HD:(half + 1) * HD, i:i + 1], a[n].rearrange("o d -> d o")))
            for dst, src in small:
                act.dma_start(dst, src).then_inc(small_in, 16)
            for t in range(TT):
                act.wait_ge(x_in, 16 * TT)
                act.activation(hT[:, 0:4, :].rearrange("p k s -> p (k s)"), xres[:, t, :], ACT.Square,
                               accum_out=stat[:, 0, t:t + 1]).then_inc(sq1, 1)
                act.wait_ge(sq1, t + 1)
            act.wait_ge(var1, 1)
            act.activation(stat[:, 2, :], stat[:, 1, :], ACT.Sqrt).then_inc(std1, 1)
            act.wait_ge(rel_ok, 1)
            act.dma_start(scratch.ap().rearrange("(h c) -> h c", h=AH), rrow).then_inc(rel_out, 16)
            act.wait_ge(rel_out, 16)
            act.dma_start(toep, bass.AP(scratch, 0, [[1, P], [TOEP, AH], [1, SEQ]])).then_inc(rel_in, 16)
            act.wait_ge(hT_ps, 4)
            act.dma_start(gate_bias, a["b_gate"][0:1, :].to_broadcast([P, 2 * D])).then_inc(gbias_in, 16)
            for c in range(GATE0):
                act.wait_ge(proj, 2 * c + 1)
                for s0, w, kind, d0 in IN_CHUNKS[c][2]:
                    dst = {"qk": qk, "v": vals, "f": fz}[kind]
                    last = act.activation(dst[:, 0, d0:d0 + w], bank((2 * c) % 4)[:, s0:s0 + w], ACT.Copy)
                last.then_inc(ev_act, 1)
                if c == FLIP_AT:
                    for i in range(AH // 2):
                        act.wait_ge(flip_ps, i + 1)
                        act.activation(reg_r[:, i * BANK:(i + 1) * BANK], bank(4 + i % 4), ACT.Copy).then_inc(flip_ok, 1)
            for t in range(TT):
                act.wait_ge(qvar, t + 1)
                act.activation(qstat[:, 1, t, :], qstat[:, 0, t, :], ACT.Sqrt).then_inc(qstd, 1)
            act.wait_ge(fstep, 2)
            act.activation(fw[:, 1, :, :], fw[:, 0, :, :], ACT.Exp).then_inc(fexp, 1)
            act.wait_ge(fstep, 3)
            act.activation(fw[:, 2, :, :], fw[:, 1, :, :], ACT.Ln).then_inc(fln, 1)
            for c in range(GATE0, NIN):
                for t in range(TT):
                    act.wait_ge(ev_dve, GATE0 + 2 * (c - GATE0) + t + 1)
                    g = gates[:, t, (c - GATE0) * BANK:(c - GATE0 + 1) * BANK]
                    act.activation(g, g, ACT.Exp, scale=-1.0).then_inc(gexp, 1)

            def soft(u):
                kind, t, _ = UNITS[u]
                nk = (t + 1) * P
                w = 3 * nk if kind == "a" else nk
                act.wait_ge(nmx, u + 1)
                act.activation(probs[u % 2][:, 0:w], probs[u % 2][:, 0:w], ACT.Exp, bias=nmax[:, u:u + 1],
                               accum_out=den[:, u:u + 1]).then_inc(pr_ok, 1)

            soft(0)
            for u in range(NU):
                if u + 1 < NU:
                    soft(u + 1)
                for i, (v, blocks) in enumerate(PIECES):
                    if v == u and i % 2 == 0:
                        act.wait_ge(pT_ps, i + 1)
                        if u >= 2:
                            act.wait_ge(pv, u - 1)
                        o = sum(len(b) for b in unit_blocks(u)[:0 if i == LAST_PIECE[u] - len(unit_blocks(u)) + 1 else 1]) * P
                        act.activation(probsT[u % 2][:, o:o + len(blocks) * P],
                                       bank(4 + i % 2)[:, 0:len(blocks) * P], ACT.Copy).then_inc(pT_act, 1)
            act.wait_ge(zero_ok, 1)
            act.dma_start(bgu[0:NE, :], a["b_gate_up"][0]).then_inc(ebias_in, 16)
            act.dma_start(bdown[0:NE, :], a["b_down"][0]).then_inc(ebias_in, 16)
            act.wait_ge(oT_ps, 1)
            act.activation(oT[:, :, 0:P], ps[0][:, 0:6 * P].rearrange("p (k s) -> p k s", k=6), ACT.Copy).then_inc(oT_act, 1)
            for t in range(TT):
                act.wait_ge(mT_ps, t + 1)
                act.activation(mT[:, :, t * P:(t + 1) * P], ps[t][:, :].rearrange("p (k s) -> p k s", k=KB),
                               ACT.Copy).then_inc(mT_ok, 1)
            for t in range(TT):
                act.wait_ge(x1_ok, 2 * (t + 1))
                act.activation(merged[:, t, :], xres[:, t, :], ACT.Square, accum_out=stat[:, 0, t:t + 1]).then_inc(sq2, 1)
            act.wait_ge(var2, 1)
            act.activation(stat[:, 2, :], stat[:, 1, :], ACT.Sqrt).then_inc(std2, 1)
            act.wait_ge(topm, 1)
            for t in range(TT):
                act.activation(egate[:, t, :], top[:, t, 0:TOPK], ACT.Exp, bias=ntop[:, t:t + 1],
                               accum_out=esum[:, t:t + 1]).then_inc(gexp2, 1)
            act.wait_ge(GT_ps, 1)
            act.activation(GT, bank(5)[0:NE, 0:SEQ], ACT.Copy).then_inc(GT_ok, 1)

            def gathered():
                pass

            act.wait_ge(cnt_ok, 3)
            steps = act.value_load(counts[0:1, 0:1], min_val=NE, max_val=MAXPASS * NE)
            act.wait_ge(gp_ps, 1)
            act.activation(gpickT, bank(7)[:, 0:TT * P], ACT.Copy).then_inc(gp_ok, 1)
            with act.Fori(0, steps) as t:
                for j in range(2):
                    act.wait_ge(g_ok, 2 * t + j + 1)
                    act.activation(glu_s, glu_g, ACT.Sigmoid, scale=ALPHA).then_inc(sig_ok, 1)
                for j in range(2):
                    act.wait_ge(midT_ps, 2 * t + j + 1)
                    act.activation(midT[:, j, :, :].rearrange("p b s -> p (b s)"), bank(7)[:, 0:2 * P],
                                   ACT.Copy).then_inc(midT_ok, 1)
                act.wait_ge(dn_ps, t + 1)
                act.activation(yb, bank(6), ACT.Copy).then_inc(yb_ok, 1)
                act.wait_ge(gp_ps, t + 2)
                act.wait_ge(scat, t + 1)
                act.activation(gpickT, bank(7)[:, 0:TT * P], ACT.Copy).then_inc(gp_ok, 1)

        @block.vector
        def _(dve):
            dve.memset(bdown[:, :], 0.0)
            dve.wait_ge(sq1, TT)
            dve.tensor_scalar(stat[:, 1, :], stat[:, 0, :], 1.0 / D, EPS, ALU.mult, ALU.add).then_inc(var1, 1)
            dve.wait_ge(std1, 1)
            dve.reciprocal(stat[:, 3, :], stat[:, 2, :]).then_inc(rstd1, 1)
            dve.wait_ge(rstd1, 1)
            for t in range(TT):
                dve.wait_ge(consts, 13)
                dve.tensor_scalar(h[:, t, :], xres[:, t, :], stat[:, 3, t:t + 1], None, ALU.mult).then_inc(h_ok, 1)
            dve.wait_ge(small_in, 16 * 16)
            for i in range(4):
                t, half = i // 2, i % 2
                dve.wait_ge(hT_ps, i + 1)
                dve.tensor_tensor(hT[:, 4 * half:4 * half + 4, t * P:(t + 1) * P],
                                  bank(i).rearrange("p (k s) -> p k s", k=4),
                                  g1[:, 4 * half:4 * half + 4].unsqueeze(2).to_broadcast([P, 4, P]),
                                  ALU.mult).then_inc(hT_ok, 1)
            dve.wait_ge(rel_ps, 1)
            dve.tensor_tensor(rrow, bank(4)[0:AH, 0:TOEP], rmask, ALU.add).then_inc(rel_ok, 1)
            for i in (0, 2):
                dve.tensor_scalar(gain[:, i:i + 1], gain[:, i:i + 1], HD ** -0.5, None, ALU.mult).then_inc(gain_ok, 1)
            for c in range(GATE0):
                dve.wait_ge(proj, 2 * c + 2)
                for s0, w, kind, d0 in IN_CHUNKS[c][2]:
                    dst = {"qk": qk, "v": vals, "f": fz}[kind]
                    last = dve.tensor_copy(dst[:, 1, d0:d0 + w], bank((2 * c + 1) % 4)[:, s0:s0 + w])
                last.then_inc(ev_dve, 1)
            for t in range(TT):
                dve.wait_ge(qsq, t + 1)
                dve.tensor_reduce(qstat[:, 0, t, :], sq[:, t, :].rearrange("p (h d) -> p h d", d=HD), AX_X,
                                  ALU.add).then_inc(qsum, 1)
                dve.wait_ge(qsum, t + 1)
                dve.tensor_scalar(qstat[:, 0, t, :], qstat[:, 0, t, :], 1.0 / HD, EPS, ALU.mult,
                                  ALU.add).then_inc(qvar, 1)
            for t in range(TT):
                dve.wait_ge(qstd, t + 1)
                dve.reciprocal(qstat[:, 0, t, :], qstat[:, 1, t, :]).then_inc(qrstd, 1)
                dve.wait_ge(qrstd, t + 1)
                q = qk[:, t, :].rearrange("p (h d) -> p h d", d=HD)
                dve.tensor_tensor(q, q, qstat[:, 0, t, :].unsqueeze(2).to_broadcast([P, QKW // HD, HD]),
                                  ALU.mult).then_inc(qn, 1)
            dve.wait_ge(ev_act, GATE0)
            dve.wait_ge(ev_dve, GATE0)
            dve.tensor_tensor(fz[:, :, :], fz[:, :, :], fbias[:, :].unsqueeze(1).to_broadcast([P, TT, FH]),
                              ALU.add).then_inc(fstep, 1)
            dve.wait_ge(fstep, 1)
            dve.scalar_tensor_tensor(out=fw[:, 0, :, :], in0=fz[:, :, :], scalar=-1.0, in1=fz[:, :, :], op0=ALU.mult,
                                     op1=ALU.min).then_inc(fstep, 1)
            dve.wait_ge(fexp, 1)
            dve.tensor_scalar(fw[:, 1, :, :], fw[:, 1, :, :], 1.0, None, ALU.add).then_inc(fstep, 1)
            dve.wait_ge(fln, 1)
            dve.scalar_tensor_tensor(out=logf[:, :, :], in0=fz[:, :, :], scalar=0.0, in1=fw[:, 2, :, :], op0=ALU.min,
                                     op1=ALU.subtract).then_inc(logf_ok, 1)

            def gate_evac(c):
                for t in range(TT):
                    dve.wait_ge(proj, 2 * c + t + 1)
                    o = (c - GATE0) * BANK
                    dve.tensor_tensor(gates[:, t, o:o + BANK], bank((2 * c + t) % 4), gate_bias[:, o:o + BANK],
                                      ALU.add).then_inc(ev_dve, 1)

            dve.wait_ge(gbias_in, 16)
            gate_evac(GATE0)
            gate_evac(GATE0 + 1)
            dve.wait_ge(gain_ok, 2)
            for i in range(len(QK_BATCHES) * TT):
                t, (b0, nb, gi) = i // len(QK_BATCHES), QK_BATCHES[i % len(QK_BATCHES)]
                dve.wait_ge(qT_ps, i + 1)
                if i == 0:
                    dve.wait_ge(qsum, TT)
                dve.tensor_scalar(qkT[:, b0:b0 + nb, t * P:(t + 1) * P],
                                  bank(4 + i % 4)[:, 0:nb * P].rearrange("p (k s) -> p k s", k=nb),
                                  gain[:, gi:gi + 1], None, ALU.mult).then_inc(qT_ok, 1)
            dve.wait_ge(cum_ps, 1)
            dve.tensor_copy(cum[:, :, :], bank(4)[:, 0:TT * FH].rearrange("p (t h) -> p t h", t=TT)).then_inc(cum_ok, 1)
            dve.tensor_scalar(negcT[:, :], bank(5)[0:FH, 0:SEQ], -1.0, None, ALU.mult).then_inc(cum_ok, 1)
            gate_evac(GATE0 + 2)
            gate_evac(GATE0 + 3)
            ng = TT * (NIN - GATE0)
            for i in range(ng):
                dve.wait_ge(gexp, i + 1)
                g = gates[:, i % TT, (i // TT) * BANK:(i // TT + 1) * BANK]
                dve.tensor_scalar(g, g, 1.0, None, ALU.add).then_inc(gone, 1)
            for i in range(ng):
                dve.wait_ge(gone, i + 1)
                g = gates[:, i % TT, (i // TT) * BANK:(i // TT + 1) * BANK]
                dve.reciprocal(g, g).then_inc(gate_ok, 1)

            def bias_max(u):
                kind, t, s = UNITS[u]
                nk = (t + 1) * P
                dve.wait_ge(sc_ps, u + 1)
                if u >= 2:
                    dve.wait_ge(pT_ps, LAST_PIECE[u - 2] + 1)
                if kind == "a":
                    if u == 0:
                        dve.wait_ge(flip_ok, AH // 2)
                    pr = probs[u % 2][:, 0:3 * nk].rearrange("p (g c) -> p g c", g=3)
                    src = ps[u % 2][:, 0:3 * SEQ].rearrange("p (g c) -> p g c", g=3)[:, :, 0:nk]
                    b = toep[:, :, :].rearrange("p (g s) c -> p g s c", g=3)[:, :, s, SEQ - nk:SEQ]
                    dve.tensor_tensor(pr, src, b, ALU.add).then_inc(sc_add, 1)
                    w = 3 * nk
                else:
                    if u == NUA:
                        dve.wait_ge(cum_ok, 2)
                    dve.scalar_tensor_tensor(out=probs[u % 2][:, 0:nk], in0=ps[u % 2][:, 0:nk],
                                             scalar=cum[:, t, s:s + 1], in1=causal[:, SEQ - nk:SEQ], op0=ALU.add,
                                             op1=ALU.add).then_inc(sc_add, 1)
                    w = nk
                dve.wait_ge(sc_add, u + 1)
                dve.tensor_reduce(amax[:, u:u + 1], probs[u % 2][:, 0:w], AX_X, ALU.max).then_inc(mx, 1)
                dve.wait_ge(mx, u + 1)
                dve.tensor_scalar(nmax[:, u:u + 1], amax[:, u:u + 1], -1.0, None, ALU.mult).then_inc(nmx, 1)

            def attn_out(n, u0, u1, src, dst):
                dve.wait_ge(pr_ok, u1)
                dve.reciprocal(rden[:, u0:u1], den[:, u0:u1]).then_inc(rden_ok, 1)
                dve.wait_ge(rden_ok, n)
                dve.wait_ge(pv, u1)
                dve.tensor_tensor(dst.rearrange("p (u d) -> p u d", d=HD), src.rearrange("p (u d) -> p u d", d=HD),
                                  rden[:, u0:u1].unsqueeze(2).to_broadcast([P, u1 - u0, HD]), ALU.mult).then_inc(o_ok, 1)

            dve.wait_ge(consts, 12)
            bias_max(0)
            for u in range(NU):
                if u + 1 < NU:
                    bias_max(u + 1)
                for i, (v, blocks) in enumerate(PIECES):
                    if v == u and i % 2 == 1:
                        dve.wait_ge(pT_ps, i + 1)
                        if u >= 2:
                            dve.wait_ge(pv, u - 1)
                        o = sum(len(b) for b in unit_blocks(u)[:0 if i == LAST_PIECE[u] - len(unit_blocks(u)) + 1 else 1]) * P
                        dve.tensor_copy(probsT[u % 2][:, o:o + len(blocks) * P],
                                        bank(4 + i % 2)[:, 0:len(blocks) * P]).then_inc(pT_dve, 1)
                if u == NUA:
                    attn_out(1, 0, NUA, bank(6), o_a.rearrange("p t d -> p (t d)"))
                if u == NUA + FH:
                    attn_out(2, NUA, NUA + FH, bank(7), o_b[:, 0, :])
            attn_out(3, NUA + FH, NU, bank(6), o_b[:, 1, :])
            dve.memset(bgu[:, :], 0.0).then_inc(zero_ok, 1)
            dve.wait_ge(oT_ps, 2)
            dve.tensor_copy(oT[:, :, P:SEQ], ps[1][:, 0:6 * P].rearrange("p (k s) -> p k s", k=6)).then_inc(oT_dve, 1)
            dve.wait_ge(gate_ok, ng)
            for i in range(2 * TT):
                t, n = i // 2, i % 2
                dve.wait_ge(br_ps, i + 1)
                for b in range(2):
                    dve.tensor_tensor(prod[:, i % 2, b, :], bank(4 + 2 * (i % 2) + b),
                                      gates[:, t, b * D + n * BANK:b * D + (n + 1) * BANK], ALU.mult).then_inc(br_mul, 1)
                dve.wait_ge(br_mul, 2 * i + 2)
                dve.tensor_tensor(merged[:, t, n * BANK:(n + 1) * BANK], prod[:, i % 2, 0, :], prod[:, i % 2, 1, :],
                                  ALU.add).then_inc(merged_ok, 1)
            for i in range(2 * TT):
                t, n = i // 2, i % 2
                dve.wait_ge(wo_ps, i + 1)
                xs = xres[:, t, n * BANK:(n + 1) * BANK]
                dve.tensor_tensor(xs, bank(4 + i), xs, ALU.add).then_inc(x1_ok, 1)
            dve.wait_ge(sq2, TT)
            dve.tensor_scalar(stat[:, 1, :], stat[:, 0, :], 1.0 / D, EPS, ALU.mult, ALU.add).then_inc(var2, 1)
            dve.wait_ge(std2, 1)
            dve.reciprocal(stat[:, 3, :], stat[:, 2, :]).then_inc(rstd2, 1)
            dve.wait_ge(rstd2, 1)
            for t in range(TT):
                dve.tensor_scalar(hn[:, t, :], xres[:, t, :], stat[:, 3, t:t + 1], None, ALU.mult).then_inc(hn_ok, 1)
            for i in range(4):
                t, half = i // 2, i % 2
                dve.wait_ge(h2_ps, i + 1)
                dve.tensor_tensor(hT[:, 4 * half:4 * half + 4, t * P:(t + 1) * P],
                                  bank(i).rearrange("p (k s) -> p k s", k=4),
                                  g2[:, 4 * half:4 * half + 4].unsqueeze(2).to_broadcast([P, 4, P]),
                                  ALU.mult).then_inc(h2_ok, 1)
            dve.wait_ge(lg_ps, 1)
            dve.tensor_tensor(logits[:, :, :], bank(4)[:, 0:TT * NE].rearrange("p (t e) -> p t e", t=TT),
                              rbias[:, :].unsqueeze(1).to_broadcast([P, TT, NE]), ALU.add).then_inc(lg_ok, 1)
            dve.wait_ge(lg_ok, 1)
            for t in range(TT):
                dve.max(top[:, t, :], logits[:, t, :]).then_inc(tops, 1)
            dve.wait_ge(tops, TT)
            for t in range(TT):
                dve.max_index(topi[:, t, :], top[:, t, :], logits[:, t, :]).then_inc(tops, 1)
            dve.tensor_scalar(ntop[:, :], top[:, :, 0], -1.0, None, ALU.mult).then_inc(topm, 1)
            dve.wait_ge(tops, 2 * TT)
            dve.tensor_copy(topf[:, :, :], topi[:, :, 0:TOPK]).then_inc(rt, 1)
            dve.wait_ge(rt, 1)
            hs = [P, TT, TOPK, NE]
            dve.tensor_tensor(hit, exp_no[:, :].unsqueeze(1).unsqueeze(1).to_broadcast(hs),
                              topf[:, :, :].unsqueeze(3).to_broadcast(hs), ALU.is_equal).then_inc(rt, 1)
            dve.wait_ge(rt, 2)
            dve.tensor_reduce(mask[:, :, :], hit.rearrange("p t k e -> p t e k"), AX_X,
                              ALU.add).then_inc(mask_ok, 1)
            dve.memset(table[:, :, :], BIG).then_inc(rt, 1)
            dve.wait_ge(gexp2, TT)
            dve.reciprocal(ersum[:, :], esum[:, :]).then_inc(rt, 1)
            dve.wait_ge(rt, 4)
            dve.tensor_tensor(egate[:, :, :], egate[:, :, :], ersum[:, :].unsqueeze(2).to_broadcast([P, TT, TOPK]),
                              ALU.mult).then_inc(rt, 1)
            dve.wait_ge(rt, 5)
            dve.tensor_tensor(ghit, hit, egate[:, :, :].unsqueeze(3).to_broadcast(hs),
                              ALU.mult).then_inc(rt, 1)
            dve.wait_ge(rt, 6)
            dve.tensor_reduce(G[:, :, :], ghit.rearrange("p t k e -> p t e k"), AX_X,
                              ALU.add).then_inc(rt, 1)
            dve.wait_ge(pos_ps, 1)
            dve.scalar_tensor_tensor(out=posm[:, :, :], in0=mask[:, :, :], scalar=-BIG,
                                     in1=bank(4)[:, 0:TT * NE].rearrange("p (t e) -> p t e", t=TT), op0=ALU.mult,
                                     op1=ALU.add).then_inc(rt, 1)
            dve.tensor_reduce(cmax[:, :], bank(4)[:, TT * NE:(TT + 1) * NE], AX_X, ALU.max).then_inc(cnt_ok, 1)
            dve.wait_ge(rt, 8)
            for q in range(MAXPASS):
                for t in range(TT):
                    dve.tensor_scalar(table[:, q * NE:(q + 1) * NE, t], posm[:, t, :], BIG - SLOTS * q, None,
                                      ALU.add)
                    dve.tensor_copy(table[:, q * NE:(q + 1) * NE, 2 + t], G[:, t, :])
                last = dve.tensor_copy(table[:, q * NE:(q + 1) * NE, 4], ident[:, 0:NE])
            last.then_inc(tab_ok, 1)
            dve.wait_ge(cnt_ok, 1)
            dve.tensor_scalar(over[:, :], thr[:, :], cmax[:, 0:1], None, ALU.is_lt).then_inc(rt, 1)
            dve.wait_ge(rt, 9)
            dve.tensor_reduce(more[:, :], over[:, :], AX_X, ALU.add).then_inc(rt, 1)
            dve.wait_ge(rt, 10)
            dve.tensor_scalar(counts[:, 0:1], more[:, :], float(NE), float(NE), ALU.mult, ALU.add).then_inc(cnt_ok, 1)
            dve.tensor_scalar(counts[:, 1:2], more[:, :], 1.0, None, ALU.add).then_inc(cnt_ok, 1)

            def gathered(t):
                dve.wait_ge(xg_ps, t + 1)
                dve.tensor_tensor(xT, bank(7).rearrange("p (k s) -> p k s", k=KB),
                                  g2[:, :].unsqueeze(2).to_broadcast([P, KB, SLOTS]), ALU.mult).then_inc(xg_ok, 1)

            dve.wait_ge(cnt_ok, 3)
            steps = dve.value_load(counts[0:1, 0:1], min_val=NE, max_val=MAXPASS * NE)
            gathered(0)
            with dve.Fori(0, steps) as t:
                for j in range(2):
                    dve.wait_ge(gu_ps, 2 * t + j + 1)
                    if j:
                        dve.wait_ge(mid_ok, 2 * t + 1)
                    dve.tensor_scalar(glu_g, bank(4 + j)[:, 0:2 * P], LIMIT, None, ALU.min).then_inc(g_ok, 1)
                    dve.tensor_scalar(glu_u, bank(4 + j)[:, 2 * P:4 * P], LIMIT, -LIMIT, ALU.min, ALU.max).then_inc(u_ok, 1)
                    dve.wait_ge(u_ok, 2 * t + j + 1)
                    dve.wait_ge(g_ok, 2 * t + j + 1)
                    dve.scalar_tensor_tensor(out=glu_u, in0=glu_u, scalar=1.0, in1=glu_g, op0=ALU.add,
                                             op1=ALU.mult).then_inc(ug_ok, 1)
                    dve.wait_ge(ug_ok, 2 * t + j + 1)
                    dve.wait_ge(sig_ok, 2 * t + j + 1)
                    if j:
                        dve.wait_ge(midT_ps, 2 * t + 1)
                    dve.tensor_tensor(mid, glu_u, glu_s, ALU.mult).then_inc(mid_ok, 1)
                gathered(t + 1)
            dve.wait_ge(scat, steps)
            for t in range(TT):
                dve.tensor_tensor(xres[:, t, :], ps[t][:, :], xres[:, t, :], ALU.add).then_inc(fin, 1)

        @block.tensor
        def _(pe):
            dma_done = lambda n: pe.wait_ge(landed[n % RING], landing(n))
            pe.wait_ge(consts, 3)
            for i in range(4):
                t, half = i // 2, i % 2
                pe.wait_ge(h_ok, t + 1)
                for k in range(4):
                    last = pe.transpose(bank(i)[:, k * P:(k + 1) * P],
                                        h[:, t, :].rearrange("p (q k) -> p k q", k=KB)[:, 4 * half + k, :], ident[:, :])
                last.then_inc(hT_ps, 1)
            pe.wait_ge(small_in, 16 * 16)
            pe.matmul(bank(4)[0:AH, 0:TOEP], rel, onehot, start=True, stop=True).then_inc(rel_ps, 1)

            def project(c):
                w = IN_CHUNKS[c][1]
                wt = ring[c % RING][:, 0:KB * w].rearrange("p (k c) -> p k c", k=KB)
                dma_done(c)
                for t in range(TT):
                    if c >= 2:
                        if t == 0 and c - 2 < GATE0:
                            pe.wait_ge(ev_act, c - 1)
                        elif c - 2 < GATE0:
                            pe.wait_ge(ev_dve, c - 1)
                        else:
                            pe.wait_ge(ev_dve, GATE0 + 2 * (c - 2 - GATE0) + t + 1)
                    for k in range(KB):
                        last = pe.matmul(bank((2 * c + t) % 4)[:, 0:w], hT[:, k, t * P:(t + 1) * P], wt[:, k, :],
                                         start=(k == 0), stop=(k == KB - 1))
                    last.then_inc(proj, 1)
                    if t == TT - 1:
                        pe.wait_ge(proj, 2 * c + 2)
                        pe.sem_inc(used, 1)

            pe.wait_ge(hT_ok, 4)
            for c in range(GATE0 + 2):
                project(c)
                if c == FLIP_AT:
                    pe.wait_ge(rel_in, 16)
                    pe.wait_ge(consts, 13)
                    for i in range(AH // 2):
                        if i >= 4:
                            pe.wait_ge(flip_ok, i - 3)
                        pe.matmul(bank(4 + i % 4), anti[:, :], reg_r[:, i * BANK:(i + 1) * BANK], start=True,
                                  stop=True).then_inc(flip_ps, 1)
            pe.wait_ge(flip_ok, AH // 2)
            for i in range(len(QK_BATCHES) * TT):
                t, (b0, nb, _) = i // len(QK_BATCHES), QK_BATCHES[i % len(QK_BATCHES)]
                pe.wait_ge(qn, t + 1)
                if i >= 4:
                    pe.wait_ge(qT_ok, i - 3)
                for k in range(nb):
                    last = pe.transpose(bank(4 + i % 4)[:, k * P:(k + 1) * P], qk[:, t, (b0 + k) * P:(b0 + k + 1) * P],
                                        ident[:, :])
                last.then_inc(qT_ps, 1)
            pe.wait_ge(logf_ok, 1)
            pe.wait_ge(consts, 12)
            pe.wait_ge(qT_ok, len(QK_BATCHES) * TT)
            pe.matmul(bank(4)[:, 0:FH], tri_le[:, :], logf[:, 0, :], start=True, stop=True)
            pe.matmul(bank(4)[:, FH:2 * FH], ones[:, :], logf[:, 0, :], start=True, stop=False)
            pe.matmul(bank(4)[:, FH:2 * FH], tri_le[:, :], logf[:, 1, :], start=False, stop=True)
            pe.matmul(bank(5)[0:FH, 0:P], logf[:, 0, :], tri_le[:, :], start=True, stop=True)
            pe.matmul(bank(5)[0:FH, P:SEQ], logf[:, 0, :], ones[:, :], start=True, stop=False)
            pe.matmul(bank(5)[0:FH, P:SEQ], logf[:, 1, :], tri_le[:, :], start=False, stop=True).then_inc(cum_ps, 1)
            for c in range(GATE0 + 2, NIN):
                project(c)

            def scores(u):
                kind, t, s = UNITS[u]
                nk = (t + 1) * P
                if u >= 2:
                    pe.wait_ge(sc_add, u - 1)
                for g in range(3 if kind == "a" else 1):
                    hd = g * SLOTHEADS + s if kind == "a" else s
                    qb, kb = (hd // 2, AH // 2 + hd // 2) if kind == "a" else (AH + hd // 2, AH + FH // 2 + hd // 2)
                    r = HD * (hd % 2)
                    last = pe.matmul(ps[u % 2][:, g * SEQ:g * SEQ + nk], qkT[r:r + HD, qb, t * P:(t + 1) * P],
                                     qkT[r:r + HD, kb, 0:nk], start=True, stop=(kind == "a"))
                if kind == "b":
                    last = pe.matmul(ps[u % 2][:, 0:nk], ident[0:FH, s:s + 1].to_broadcast([FH, P]), negcT[:, 0:nk], start=False, stop=True)
                last.then_inc(sc_ps, 1)

            def turn(u):
                pe.wait_ge(pr_ok, u + 1)
                nk = (UNITS[u][1] + 1) * P
                for i, (v, blocks) in enumerate(PIECES):
                    if v == u:
                        if i >= 2:
                            pe.wait_ge(pT_act if i % 2 == 0 else pT_dve, i // 2)
                        for n, (g, k) in enumerate(blocks):
                            last = pe.transpose(bank(4 + i % 2)[:, n * P:(n + 1) * P],
                                                probs[u % 2][:, g * nk + k * P:g * nk + (k + 1) * P], ident[:, :])
                        last.then_inc(pT_ps, 1)

            def values(u):
                kind, t, s = UNITS[u]
                i = LAST_PIECE[u]
                pe.wait_ge(pT_act, i // 2 + 1)
                pe.wait_ge(pT_dve, (i + 1) // 2)
                if u == NUA + FH:
                    pe.wait_ge(o_ok, 1)
                blocks = [b for piece in unit_blocks(u) for b in piece]
                ob = bank(6) if kind == "a" or t == 1 else bank(7)
                o = (t * SLOTHEADS + s if kind == "a" else s) * HD
                for n, (g, k) in enumerate(blocks):
                    v0 = (g * SLOTHEADS + s) * HD if kind == "a" else AW + s * HD
                    last = pe.matmul(ob[:, o:o + HD], probsT[u % 2][:, n * P:(n + 1) * P], vals[:, k, v0:v0 + HD],
                                     start=(n == 0), stop=(n == len(blocks) - 1))
                last.then_inc(pv, 1)

            pe.wait_ge(cum_ok, 2)
            pe.wait_ge(ev_dve, GATE0 + 2 * (NIN - GATE0))
            scores(0)
            for u in range(NU):
                if u + 1 < NU:
                    scores(u + 1)
                turn(u)
                if u:
                    values(u - 1)
            values(NU - 1)
            pe.wait_ge(o_ok, 3)
            for t in range(TT):
                for b in range(6):
                    src = o_a[:, t, b * P:(b + 1) * P] if b < 2 else o_b[:, t, (b - 2) * P:(b - 1) * P]
                    last = pe.transpose(ps[t][:, b * P:(b + 1) * P], src, ident[:, :])
                last.then_inc(oT_ps, 1)
            dma_done(NIN)
            dma_done(NIN + 1)
            pe.wait_ge(oT_act, 1)
            pe.wait_ge(oT_dve, 1)
            for i in range(2 * TT):
                t, n = i // 2, i % 2
                if i >= 2:
                    pe.wait_ge(br_mul, 2 * (i - 1))
                for b, ks in ((0, range(0, 2)), (1, range(2, 6))):
                    for k in ks:
                        w = ring[(NIN + k // 4) % RING]
                        last = pe.matmul(bank(4 + 2 * (i % 2) + b), oT[:, k, t * P:(t + 1) * P],
                                         w[:, (k % 4) * D + n * BANK:(k % 4) * D + (n + 1) * BANK],
                                         start=(k == ks[0]), stop=(k == ks[-1]))
                last.then_inc(br_ps, 1)
            pe.wait_ge(br_ps, 2 * TT)
            pe.sem_inc(used, 2)
            for t in range(TT):
                pe.wait_ge(merged_ok, 2 * (t + 1))
                for k in range(KB):
                    last = pe.transpose(ps[t][:, k * P:(k + 1) * P], merged[:, t, k * P:(k + 1) * P], ident[:, :])
                last.then_inc(mT_ps, 1)
            dma_done(NIN + 2)
            dma_done(NIN + 3)
            for i in range(2 * TT):
                t, n = i // 2, i % 2
                pe.wait_ge(mT_ok, t + 1)
                for k in range(KB):
                    w = ring[(NIN + 2 + k // 4) % RING]
                    last = pe.matmul(bank(4 + i), mT[:, k, t * P:(t + 1) * P],
                                     w[:, (k % 4) * D + n * BANK:(k % 4) * D + (n + 1) * BANK],
                                     start=(k == 0), stop=(k == KB - 1))
                last.then_inc(wo_ps, 1)
            pe.wait_ge(wo_ps, 2 * TT)
            pe.sem_inc(used, 2)
            for i in range(4):
                t, half = i // 2, i % 2
                pe.wait_ge(hn_ok, t + 1)
                for k in range(4):
                    last = pe.transpose(bank(i)[:, k * P:(k + 1) * P],
                                        hn[:, t, :].rearrange("p (q k) -> p k q", k=KB)[:, 4 * half + k, :], ident[:, :])
                last.then_inc(h2_ps, 1)
            pe.wait_ge(h2_ok, 4)
            for t in range(TT):
                for k in range(KB):
                    last = pe.matmul(bank(4)[:, t * NE:(t + 1) * NE], hT[:, k, t * P:(t + 1) * P], wr[:, k, :],
                                     start=(k == 0), stop=(k == KB - 1))
            last.then_inc(lg_ps, 1)
            pe.wait_ge(mask_ok, 1)
            pe.matmul(bank(4)[:, 0:NE], tri_lt[:, :], mask[:, 0, :], start=True, stop=True)
            pe.matmul(bank(4)[:, NE:2 * NE], ones[:, :], mask[:, 0, :], start=True, stop=False)
            pe.matmul(bank(4)[:, NE:2 * NE], tri_lt[:, :], mask[:, 1, :], start=False, stop=True)
            pe.matmul(bank(4)[:, 2 * NE:3 * NE], ones[:, :], mask[:, 0, :], start=True, stop=False)
            pe.matmul(bank(4)[:, 2 * NE:3 * NE], ones[:, :], mask[:, 1, :], start=False, stop=True).then_inc(pos_ps, 1)
            pe.wait_ge(rt, 7)
            for t in range(TT):
                last = pe.transpose(bank(5)[0:NE, t * P:(t + 1) * P], G[:, t, :], ident[:, :])
            last.then_inc(GT_ps, 1)
            pe.wait_ge(GT_ok, 1)
            pe.wait_ge(ebias_in, 32)
            for t in range(TT):
                for n in range(2):
                    pe.matmul(bank(2 * t + n), GT[:, t * P:(t + 1) * P], bdown[0:NE, n * BANK:(n + 1) * BANK],
                              start=True, stop=False, skip_group_check=True)

            def gather(t):
                pe.wait_ge(pick_ok, t + 1)
                for k in range(KB):
                    for tt in range(TT):
                        last = pe.matmul(bank(7)[:, k * SLOTS:(k + 1) * SLOTS],
                                         hn[:, tt, :].rearrange("p (q k) -> p k q", k=KB)[:, k, :], pick[:, tt, :],
                                         start=(tt == 0), stop=(tt == TT - 1))
                last.then_inc(xg_ps, 1)

            def turn_gates(t):
                pe.wait_ge(xg_ok, t + 1)
                for tt in range(TT):
                    last = pe.transpose(bank(7)[:, tt * P:(tt + 1) * P], gpick[:, tt, :], ident[:, :])
                last.then_inc(gp_ps, 1)

            def turn_mid(t, j):
                pe.wait_ge(mid_ok, 2 * t + j + 1)
                if j:
                    pe.wait_ge(midT_ok, 2 * t + 1)
                for b in range(2):
                    last = pe.transpose(bank(7)[:, b * P:(b + 1) * P], mid[:, b * P:(b + 1) * P], ident[:, :])
                last.then_inc(midT_ps, 1)

            def chunk(t, c):
                pe.wait_ge(landed[eslot(c)], t * eland(c) + (pre_land[eslot(c)] + eland(c)))

            def down(t, half):
                chunk(t, 4 + half)
                pe.wait_ge(midT_ok, 2 * t + half + 1)
                w = ring[eslot(4 + half)]
                for k in range(4):
                    for n in range(2):
                        last = pe.matmul(bank(6)[n * SLOTS:(n + 1) * SLOTS, :],
                                         midT[:, half, k % 2, (k // 2) * SLOTS:(k // 2 + 1) * SLOTS],
                                         w[:, k * D + n * BANK:k * D + (n + 1) * BANK],
                                         start=(half == 0 and k == 0), stop=(half == 1 and k == 3))
                last.then_inc(used, 1)

            pe.wait_ge(cnt_ok, 3)
            steps = pe.value_load(counts[0:1, 0:1], min_val=NE, max_val=MAXPASS * NE)
            gather(0)
            turn_gates(0)
            with pe.Fori(0, steps) as t:
                pe.wait_ge(xg_ok, t + 1)
                for j in range(2):
                    gu = bank(4 + j)
                    for n in range(2):
                        pe.matmul(gu[n * SLOTS:(n + 1) * SLOTS, :], sel_e,
                                  bgu.rearrange("p (w j n c) -> p w j n c", w=2, j=2, n=2)[:, :, j, n, :],
                                  start=True, stop=False)
                    for kh in range(2):
                        chunk(t, 2 * j + kh)
                        w = ring[eslot(2 * j + kh)][:, :].rearrange("p (k w n c) -> p k w n c", k=4, w=2, n=2)
                        for k in range(4):
                            for n in range(2):
                                last = pe.matmul(gu[n * SLOTS:(n + 1) * SLOTS, :], xT[:, 4 * kh + k, :],
                                                 w[:, k, :, n, :], start=False, stop=(kh == 1 and k == 3))
                        if kh == 0:
                            last.then_inc(used, 1)
                    last.then_inc(gu_ps, 1)
                    pe.wait_ge(gu_ps, 2 * t + j + 1)
                    pe.sem_inc(used, 1)
                pe.wait_ge(gp_ok, t + 1)
                turn_mid(t, 0)
                down(t, 0)
                turn_mid(t, 1)
                down(t, 1)
                pe.wait_ge(used, t * PER + (n_pre + PER))
                pe.sem_inc(dn_ps, 1)
                pe.wait_ge(midT_ok, 2 * t + 2)
                gather(t + 1)
                pe.wait_ge(yb_ok, t + 1)
                for tt in range(TT):
                    for n in range(2):
                        last = pe.matmul(bank(2 * tt + n), gpickT[n * SLOTS:(n + 1) * SLOTS, tt * P:(tt + 1) * P],
                                         yb[n * SLOTS:(n + 1) * SLOTS, :], start=False, stop=False,
                                         skip_group_check=True)
                last.then_inc(scat, 1)
                turn_gates(t + 1)


def _tables():
    max_exact, max_distance = NB // 2, 2048
    dist = 2 * P - 1 - np.arange(TOEP)
    n = np.maximum(dist, 0)
    large = max_exact + (np.log(np.maximum(n, 1).astype(np.float64) / max_exact) / np.log(max_distance / max_exact)
                         * (NB - max_exact)).astype(np.int64)
    bucket = np.where(n < max_exact, n, np.minimum(large, NB - 1))
    onehot = ((np.arange(NB)[:, None] == bucket[None, :]) & (dist >= 0)[None, :]).astype(np.float32)
    reach = np.zeros((AH, TOEP), np.float32)
    for g, (window, dilation) in enumerate(((128, 1), (512, 4), (2048, 16))):
        ok = (dist >= 0) & (dist % dilation == 0) & (dist <= window)
        reach[g * SLOTHEADS:(g + 1) * SLOTHEADS] = np.where(ok, 0.0, NEG)
    return onehot, reach


_INS = ["x", "ln1_g", "w_in", "b_forget", "b_gate", "q_norm_a", "k_norm_a", "q_norm_b", "k_norm_b", "rel_bias",
        "w_branch_a", "w_branch_b", "w_out", "ln2_g", "w_router", "b_router", "w_gate_up", "b_gate_up", "w_down",
        "b_down"]


def kernel(**inputs):
    import numpy as _np
    import concourse.bacc as _bacc
    from concourse import mybir as _mybir
    from concourse.bass_utils import run_bass_kernel_spmd as _run

    nc = _bacc.Bacc("TRN2", target_bir_lowering=False, num_devices=1)
    arrays, args = {}, {}
    given = {n: _np.ascontiguousarray(inputs[n]) for n in _INS}
    given["bucket_onehot"], given["reach_mask"] = _tables()
    for name, v in given.items():
        arrays[f"in_{name}"] = v
        args[name] = nc.dram_tensor(f"in_{name}", v.shape, _mybir.dt.from_np(v.dtype), kind="ExternalInput").ap()
    out = nc.dram_tensor("out_0", (1, SEQ, D), F32, kind="ExternalOutput").ap()
    build(nc, args, out)
    r = _run(nc, [arrays], core_ids=[0])
    return r.results[0]["out_0"]
```

```python
from contextlib import ExitStack

import numpy as np

import concourse.bass as bass
from concourse import mybir

F32 = mybir.dt.float32
I32 = mybir.dt.int32
U32 = mybir.dt.uint32
ALU = mybir.AluOpType
ACT = mybir.ActivationFunctionType
AX_X = mybir.AxisListType.X

P = 128
D = 1024
SEQ = 256
TT = SEQ // P
KB = D // P
HD = 64
GROUPS, SLOTHEADS = 3, 4
AH = GROUPS * SLOTHEADS
AW = AH * HD
FH = 8
FW = FH * HD
EPS = 1e-6
NEG = -1e30
NB = 32
NE = 32
TOPK = 4
LIMIT, ALPHA = 7.0, 1.702
SLOTS = 64
MAXPASS = SEQ // SLOTS
BIG = 10000.0

RING = 6
SLOT = 4096
BANK = 512

QKW = 2 * AW + 2 * FW
VW = AW + FW
IN_CHUNKS = [
    (0, 512, [(0, 512, "qk", 0)]),
    (512, 512, [(0, 512, "qk", 512)]),
    (1024, 512, [(0, 512, "qk", 1024)]),
    (2048, 512, [(0, 256, "v", 512), (256, 256, "qk", 1536)]),
    (2560, 512, [(0, 512, "qk", 1792)]),
    (3072, 512, [(0, 256, "qk", 2304), (256, 256, "v", 768)]),
    (3584, 264, [(0, 256, "v", 1024), (256, 8, "f", 0)]),
    (1536, 512, [(0, 512, "v", 0)]),
    (3848, 512, [(0, 512, "g", 0)]),
    (4360, 512, [(0, 512, "g", 512)]),
    (4872, 512, [(0, 512, "g", 1024)]),
    (5384, 512, [(0, 512, "g", 1536)]),
]
NQK = 6
NIN = len(IN_CHUNKS)
NSMALL = 12
GATE0 = 8
QK_BATCHES = [(0, 4, 0), (4, 2, 0), (6, 4, 1), (10, 2, 1), (12, 4, 2), (16, 4, 3)]
FLIP_AT = 2
TOEP = 2 * P + P

PAIRS = ([("a", t, s) for t in range(TT) for s in (0, 2)]
         + [("b", t, s) for t in range(TT) for s in (0, 2, 4, 6)])
NPAIR = len(PAIRS)
NPA = 2 * TT
NU = 2 * NPAIR
NUA = 2 * NPA


def keys(p):
    return (PAIRS[p][1] + 1) * P


def width(p):
    return keys(p) * (GROUPS if PAIRS[p][0] == "a" else 1)


def blocks(p):
    kind, t, _ = PAIRS[p]
    return [(i, g, k) for i in range(2) for g in range(GROUPS if kind == "a" else 1) for k in range(t + 1)]


PIECES = [(p, blocks(p)[n:n + 4]) for p in range(NPAIR) for n in range(0, len(blocks(p)), 4)]
NGATE = TT * (NIN - GATE0)


def attention_order():
    order, filled = [], 0

    def fill(count):
        nonlocal filled
        for _ in range(min(count, NGATE * KB - filled)):
            order.append(("fill", filled))
            filled += 1

    fill(KB)
    order.append(("scores", 0))
    fill(5)
    order.append(("soft", 0))
    for p in range(NPAIR):
        if p + 1 < NPAIR:
            order.append(("scores", p + 1))
            fill(3)
        for i, (v, _) in enumerate(PIECES):
            if v == p:
                order.append(("turn", i))
                fill(1)
                order.append(("values", i))
        if p + 1 < NPAIR:
            order.append(("soft", p + 1))
    fill(NGATE * KB)
    return order


ATTENTION = attention_order()


def build(nc, a, out):
    with ExitStack() as ctx:
        def sb(name, shape, dt=F32):
            return ctx.enter_context(nc.sbuf_tensor(name, shape, dt))

        def sem(name):
            return ctx.enter_context(nc.semaphore(name))

        ring = [sb(f"ring{i}", [P, SLOT]) for i in range(RING)]
        ps = [ctx.enter_context(nc.psum_tensor(f"ps{i}", [P, 2 * BANK], F32)) for i in range(4)]

        def bank(i):
            return ps[i // 2][:, (i % 2) * BANK:(i % 2 + 1) * BANK]

        xres = sb("xres", [P, TT, D])
        reg_n = sb("reg_n", [P, TT * D])
        reg_t = sb("reg_t", [P, KB * SEQ])
        reg_a = sb("reg_a", [P, TT * QKW])
        reg_b = sb("reg_b", [P, TT * QKW])
        vals = sb("vals", [P, TT, VW])
        gates = sb("gates", [P, TT, 2 * D])
        reg_r = sb("reg_r", [P, AH * SEQ])

        h = reg_n[:, :].rearrange("p (t d) -> p t d", t=TT)
        gate_bias = reg_n[:, :]
        merged = h
        xflat = xres[:, :, :].rearrange("p t d -> p (t d)")
        o_a = xflat[:, 0:TT * SLOTHEADS * HD].rearrange("p (t d) -> p t d", t=TT)
        o_b = xflat[:, TT * SLOTHEADS * HD:TT * (SLOTHEADS * HD + FW)].rearrange("p (t d) -> p t d", t=TT)
        hn = h
        hT = reg_t[:, :].rearrange("p (k s) -> p k s", k=KB)
        oT = reg_t[:, 0:6 * SEQ].rearrange("p (k s) -> p k s", k=6)
        qk = reg_a[:, :].rearrange("p (t d) -> p t d", t=TT)
        sq = reg_b[:, 2048:2048 + TT * BANK].rearrange("p (t d) -> p t d", t=TT)
        qkT = reg_b[:, :].rearrange("p (k s) -> p k s", k=QKW // P)
        mT = reg_b[:, 0:KB * SEQ].rearrange("p (k s) -> p k s", k=KB)
        bgu = reg_b[:, 2048:4096]
        bdown = reg_b[:, 4096:5120]
        toep = reg_r[:, :].rearrange("p (h c) -> p h c", h=AH)
        prod = reg_r[:, 0:2048].rearrange("p (i b c) -> p i b c", i=2, b=2)

        onehot = reg_b[0:NB, 0:TOEP]
        rmask = reg_b[0:AH, TOEP:2 * TOEP]
        rrow = reg_b[0:AH, 2 * TOEP:3 * TOEP]
        rel = reg_b[0:NB, 3 * TOEP:3 * TOEP + AH]
        vflat = vals[:, :, :].rearrange("p t d -> p (t d)")
        hw = TT * TOPK * NE
        hit = vflat[:, 0:hw].rearrange("p (t k e) -> p t k e", t=TT, k=TOPK)
        ghit = vflat[:, hw:2 * hw].rearrange("p (t k e) -> p t k e", t=TT, k=TOPK)
        GT = vflat[0:NE, 2 * hw:2 * hw + SEQ]
        logits, mask, G, posm = (vflat[:, 3 * hw + i * TT * NE:3 * hw + (i + 1) * TT * NE]
                                 .rearrange("p (t e) -> p t e", t=TT) for i in range(4))

        at = [0]

        def take(n):
            at[0] += n
            assert at[0] <= TT * QKW
            return reg_a[:, at[0] - n:at[0]]

        probs = [take(2 * GROUPS * SEQ).rearrange("p (i c) -> p i c", i=2) for _ in range(2)]
        probsT = [take(BANK) for _ in range(4)]
        at[0] = 0
        xT = take(KB * SLOTS).rearrange("p (k s) -> p k s", k=KB)
        glu_g, glu_u, glu_s, mid = [take(2 * P) for _ in range(4)]
        midT = take(4 * P).rearrange("p (j b s) -> p j b s", j=2, b=2)
        yb = take(BANK)
        pick = take(TT * SLOTS).rearrange("p (t s) -> p t s", t=TT)
        gpick = take(TT * P).rearrange("p (t s) -> p t s", t=TT)
        gpickT = take(TT * P)
        sel_e = take(SLOTS)
        cols = take(5)
        take(3)
        table = take(5 * (MAXPASS * NE + 1)).rearrange("p (e c) -> p e c", c=5)

        zeros = h[:, 0, 0:SEQ]
        ident = sb("ident", [P, P])
        anti = sb("anti", [P, P])
        ones = sb("ones", [P, P])
        tri_le = sb("tri_le", [P, P])
        tri_lt = sb("tri_lt", [P, P])
        causal = sb("causal", [P, SEQ])
        iota_i = sb("iota_i", [P, P], I32)
        slot_no = sb("slot_no", [P, P])
        exp_i = sb("exp_i", [P, NE], I32)
        exp_no = sb("exp_no", [P, NE])
        thr_i = sb("thr_i", [P, MAXPASS - 1], I32)
        thr = sb("thr", [P, MAXPASS - 1])
        g1 = sb("g1", [P, KB])
        g2 = sb("g2", [P, KB])
        gain = sb("gain", [P, 4])
        fbias = sb("fbias", [P, FH])
        rbias = sb("rbias", [P, NE])
        wr = sb("wr", [P, KB, NE])
        stat = sb("stat", [P, 4, TT])
        qstat = sb("qstat", [P, 2, TT, QKW // HD])
        fz = sb("fz", [P, TT, FH])
        fw = sb("fw", [P, 3, TT, FH])
        logf = sb("logf", [P, TT, FH])
        cum = sb("cum", [P, TT, FH])
        negcT = sb("negcT", [FH, SEQ])
        amax = sb("amax", [P, NU])
        nmax = sb("nmax", [P, NU])
        den = sb("den", [P, NU])
        rden = sb("rden", [P, NU])
        top = sb("top", [P, TT, 8])
        topi = sb("topi", [P, TT, 8], U32)
        topf = sb("topf", [P, TT, TOPK])
        ntop = sb("ntop", [P, TT])
        egate = sb("egate", [P, TT, TOPK])
        esum = sb("esum", [P, TT])
        ersum = sb("ersum", [P, TT])
        cmax = sb("cmax", [P, 1])
        over = sb("over", [P, MAXPASS - 1])
        more = sb("more", [P, 1])
        counts = sb("counts", [P, 2], I32)

        scratch = nc.dram_tensor("rel_rows", [AH * TOEP], F32, kind="Internal")

        landed = [sem(f"landed{i}") for i in range(RING)]
        used = sem("used")
        x_in, g1_in, rel_op_in, small_in = sem("x_in"), sem("g1_in"), sem("rel_op_in"), sem("small_in")
        gbias_in, ebias_in, x2_in = sem("gbias_in"), sem("ebias_in"), sem("x2_in")
        consts = sem("consts")
        sq1, var1, std1, rstd1, h_ok, hT_ps, hT_ok = (sem(n) for n in (
            "sq1", "var1", "std1", "rstd1", "h_ok", "hT_ps", "hT_ok"))
        flip_ps, flip_ok = sem("flip_ps"), sem("flip_ok")
        gain_ok, rel_ps, rel_ok, rel_out, rel_in = (sem(n) for n in ("gain_ok", "rel_ps", "rel_ok", "rel_out", "rel_in"))
        proj, ev_act, ev_dve = sem("proj"), sem("ev_act"), sem("ev_dve")
        gate_ps, gate_raw, gate_z, gate_ok = sem("gate_ps"), sem("gate_raw"), sem("gate_z"), sem("gate_ok")
        qsq, qsum, qvar, qstd, qrstd, qn = (sem(n) for n in ("qsq", "qsum", "qvar", "qstd", "qrstd", "qn"))
        qT_ps, qT_ok = sem("qT_ps"), sem("qT_ok")
        fstep, fexp, fln, logf_ok, cum_ps, cum_ok = (sem(n) for n in (
            "fstep", "fexp", "fln", "logf_ok", "cum_ps", "cum_ok"))
        sc_ps, sc_add, mx, nmx, pr_ok = (sem(n) for n in ("sc_ps", "sc_add", "mx", "nmx", "pr_ok"))
        pT_ps, pT_ok, pv, rden_ok, o_ok = (sem(n) for n in ("pT_ps", "pT_ok", "pv", "rden_ok", "o_ok"))
        oT_ps, oT_act, oT_dve, br_ps, br_mul, merged_ok = (sem(n) for n in (
            "oT_ps", "oT_act", "oT_dve", "br_ps", "br_mul", "merged_ok"))
        mT_ps, mT_ok, wo_ps, x1_ok = (sem(n) for n in ("mT_ps", "mT_ok", "wo_ps", "x1_ok"))
        sq2, var2, std2, rstd2, hn_ok, h2_ps, h2_ok = (sem(n) for n in (
            "sq2", "var2", "std2", "rstd2", "hn_ok", "h2_ps", "h2_ok"))
        lg_ps, lg_ok, tops, topm, gexp2, rt, mask_ok = (sem(n) for n in (
            "lg_ps", "lg_ok", "tops", "topm", "gexp2", "rt", "mask_ok"))
        pos_ps, GT_ps, GT_ok, tab_ok, cnt_ok = (sem(n) for n in ("pos_ps", "GT_ps", "GT_ok", "tab_ok", "cnt_ok"))
        zero_ok = sem("zero_ok")
        col_ok, pick_ok, xg_ps, xg_ok, gp_ps, gp_ok = (sem(n) for n in (
            "col_ok", "pick_ok", "xg_ps", "xg_ok", "gp_ps", "gp_ok"))
        gu_ps, g_ok, sig_ok, u_ok, ug_ok, mid_ok, midT_ps, midT_ok = (sem(n) for n in (
            "gu_ps", "g_ok", "sig_ok", "u_ok", "ug_ok", "mid_ok", "midT_ps", "midT_ok"))
        dn_ps, yb_ok, scat = sem("dn_ps"), sem("yb_ok"), sem("scat")
        fin, stored = sem("fin"), sem("stored")

        n_pre = NIN + 4
        lands = [[16 * (i // RING + 1)] for i in range(n_pre)]
        extra = {NIN % RING: NIN}

        def landing(n):
            s = n % RING
            return 16 * (n // RING + 1) + (16 if s in extra and n >= extra[s] else 0)

        pre_land = [max([landing(n) for n in range(n_pre) if n % RING == s]) for s in range(RING)]
        PER = 6

        def eslot(c):
            return (n_pre + c) % RING

        w_in = a["w_in"][0]

        def expert_load(eng, e, c):
            slot = ring[eslot(c)]
            if c < 4:
                j, kh = c // 2, c % 2
                src = a["w_gate_up"][0][bass.ds(e, 1)].rearrange(
                    "o (p k) (w j c) -> p (o k) w j c", k=KB, w=2, j=2)[:, kh * 4:kh * 4 + 4, :, j, :]
                dst = slot[:, :].rearrange("p (k w c) -> p k w c", k=4, w=2)
                for w in range(2):
                    eng.dma_start(dst[:, :, w, :], src[:, :, w, :]).then_inc(landed[eslot(c)], 16)
            else:
                kh = c - 4
                src = a["w_down"][0][bass.ds(e, 1)].rearrange("o (k p) c -> p (o k) c", p=P)[:, kh * 4:kh * 4 + 4, :]
                eng.dma_start(slot[:, :].rearrange("p (k c) -> p k c", k=4), src).then_inc(landed[eslot(c)], 16)

        def eland(c):
            return 32 if c < 4 else 16

        block = ctx.enter_context(nc.Block())

        @block.sync
        def _(sp):
            for t in range(TT):
                sp.dma_start(xres[:, t, :], a["x"][0, t * P:(t + 1) * P, :]).then_inc(x_in, 16)
            for n, (c0, w, _) in enumerate(IN_CHUNKS):
                if n >= RING:
                    sp.wait_ge(proj, 2 * (n - RING + 1))
                sp.dma_start(ring[n % RING][:, 0:KB * w].rearrange("p (k c) -> p k c", k=KB),
                             w_in.rearrange("(p k) c -> p k c", k=KB)[:, :, c0:c0 + w]).then_inc(landed[n % RING], 16)

            def in_chunk_read(n):
                if n < GATE0:
                    sp.wait_ge(proj, 2 * (n + 1))
                else:
                    sp.wait_ge(gate_ps, TT * (n - GATE0 + 1))

            wbr = [(NIN, 0, a["w_branch_a"][0], 0, 2), (NIN, 2, a["w_branch_b"][0], 0, 2),
                   (NIN + 1, 0, a["w_branch_b"][0], 2, 2), (NIN + 2, 0, a["w_out"][0], 0, 4),
                   (NIN + 3, 0, a["w_out"][0], 4, 4)]
            for n, k0, w, b0, nb in wbr:
                in_chunk_read(n - RING)
                sp.dma_start(ring[n % RING][:, k0 * D:(k0 + nb) * D].rearrange("p (k c) -> p k c", k=nb),
                             w.rearrange("(k p) c -> p k c", p=P)[:, b0:b0 + nb, :]).then_inc(landed[n % RING], 16)
            for c in range(PER):
                if c < 2:
                    in_chunk_read(NIN - 2 + c)
                elif c < 4:
                    sp.wait_ge(br_ps, 2 * TT)
                else:
                    sp.wait_ge(wo_ps, 2 * TT)
                if c == 2:
                    sp.wait_ge(oT_ps, 2)
                    for t in range(TT):
                        sp.dma_start(xres[:, t, :], a["x"][0, t * P:(t + 1) * P, :]).then_inc(x2_in, 16)
                expert_load(sp, 0, c)

            def refill(t, e):
                for c in range(PER):
                    if c in (0, 2, 4):
                        sp.wait_ge(used, t * 3 + (c // 2 - 2))
                    elif c < 4:
                        sp.wait_ge(gu_ps, t * 2 + (c // 2 - 1))
                    else:
                        sp.wait_ge(dn_ps, t)
                    expert_load(sp, e, c)

            with sp.Fori(1, NE) as e:
                refill(e, e)
            sp.wait_ge(cnt_ok, 3)
            passes = sp.value_load(counts[0:1, 1:2], min_val=1, max_val=MAXPASS)
            with sp.If(passes > 1):
                with sp.Fori(1, passes) as q:
                    with sp.Fori(0, NE) as e:
                        refill(q * NE + e, e)
            for t in range(TT):
                sp.wait_ge(fin, t + 1)
                sp.dma_start(out[0, t * P:(t + 1) * P, :], xres[:, t, :]).then_inc(stored, 16)
            sp.wait_ge(stored, 16 * TT)

        @block.gpsimd
        def _(pool):
            pool.memset(ones[:, :], 1.0).then_inc(consts, 1)
            pool.memset(zeros, 0.0).then_inc(consts, 1)
            pool.wait_ge(consts, 2)
            pool.affine_select(out=ident[:, :], in_=zeros[:, 0:P], compare_op=ALU.not_equal, fill=1.0, base=0,
                               pattern=[[-1, P]], channel_multiplier=1).then_inc(consts, 1)
            pool.affine_select(out=tri_le[:, :], in_=ones[:, :], compare_op=ALU.is_ge, fill=0.0, base=0,
                               pattern=[[1, P]], channel_multiplier=-1).then_inc(consts, 1)
            pool.affine_select(out=tri_lt[:, :], in_=ones[:, :], compare_op=ALU.is_gt, fill=0.0, base=0,
                               pattern=[[1, P]], channel_multiplier=-1).then_inc(consts, 1)
            pool.affine_select(out=causal[:, :], in_=zeros, compare_op=ALU.is_ge, fill=NEG, base=P,
                               pattern=[[-1, SEQ]], channel_multiplier=1).then_inc(consts, 1)
            pool.iota(iota_i[:, :], pattern=[[0, 2], [1, SLOTS]], base=0, channel_multiplier=0).then_inc(consts, 1)
            pool.iota(exp_i[:, :], pattern=[[1, NE]], base=0, channel_multiplier=0).then_inc(consts, 1)
            pool.iota(thr_i[:, :], pattern=[[SLOTS, MAXPASS - 1]], base=SLOTS, channel_multiplier=0).then_inc(consts, 1)
            pool.wait_ge(consts, 9)
            pool.tensor_copy(slot_no[:, :], iota_i[:, :]).then_inc(consts, 1)
            pool.tensor_copy(exp_no[:, :], exp_i[:, :]).then_inc(consts, 1)
            pool.tensor_copy(thr[:, :], thr_i[:, :]).then_inc(consts, 1)
            pool.affine_select(out=anti[:, :], in_=zeros[:, 0:P], compare_op=ALU.not_equal, fill=1.0, base=1 - P,
                               pattern=[[1, P]], channel_multiplier=1).then_inc(consts, 1)
            for c in range(NQK):
                s0, w, _, d0 = [x for x in IN_CHUNKS[c][2] if x[2] == "qk"][0]
                for t in range(TT):
                    pool.wait_ge((ev_act, ev_dve)[t], c + 1)
                    if c:
                        pool.wait_ge(qsum, TT * c)
                    q = qk[:, t, d0:d0 + w]
                    pool.tensor_tensor(sq[:, t, 0:w], q, q, ALU.mult).then_inc(qsq, 1)
            pool.wait_ge(gbias_in, 16)
            for i in range(NGATE):
                pool.wait_ge(gate_raw, i + 1)
                o = (i // TT) * BANK
                g = gates[:, i % TT, o:o + BANK]
                pool.tensor_tensor(g, g, gate_bias[:, o:o + BANK], ALU.add).then_inc(gate_z, 1)
            pool.wait_ge(tab_ok, 1)
            pool.wait_ge(cnt_ok, 3)
            steps = pool.value_load(counts[0:1, 0:1], min_val=NE, max_val=MAXPASS * NE)

            def select(t, first):
                pool.tensor_copy(cols, table[:, bass.ds(t, 1), :].rearrange("p o c -> p (o c)")).then_inc(col_ok, 1)
                pool.wait_ge(col_ok, t + 1)
                if not first:
                    pool.wait_ge(xg_ps, t)
                    pool.wait_ge(gp_ps, t)
                    pool.wait_ge(gu_ps, 2 * t)
                pool.tensor_tensor(sel_e, ones[:, 0:SLOTS], cols[:, 4:5].to_broadcast([P, SLOTS]), ALU.mult)
                for tt in range(TT):
                    pool.tensor_scalar(pick[:, tt, :], slot_no[:, 0:SLOTS], cols[:, tt:tt + 1], None, ALU.is_equal)
                for tt in range(TT):
                    last = pool.tensor_scalar(gpick[:, tt, :], slot_no[:, :], cols[:, tt:tt + 1],
                                              cols[:, 2 + tt:3 + tt], ALU.is_equal, ALU.mult)
                last.then_inc(pick_ok, 1)

            select(0, True)
            with pool.Fori(0, steps) as t:
                pool.wait_ge(pick_ok, t + 1)
                select(t + 1, False)

        @block.scalar
        def _(act):
            act.dma_start(g1[:, :], a["ln1_g"][0].rearrange("(p k) -> p k", k=KB)).then_inc(g1_in, 16)
            for dst, src in ((rel, a["rel_bias"]), (onehot, a["bucket_onehot"]), (rmask, a["reach_mask"])):
                act.dma_start(dst, src).then_inc(rel_op_in, 16)
            small = [
                (fbias[:, :], a["b_forget"][0:1, :].to_broadcast([P, FH])),
                (g2[:, :], a["ln2_g"][0].rearrange("(p k) -> p k", k=KB)),
                (rbias[:, :], a["b_router"][0:1, :].to_broadcast([P, NE])),
                (wr[:, :, :], a["w_router"][0].rearrange("(p k) e -> p k e", k=KB)),
            ]
            for i, n in enumerate(("q_norm_a", "k_norm_a", "q_norm_b", "k_norm_b")):
                for half in range(2):
                    small.append((gain[half * HD:(half + 1) * HD, i:i + 1], a[n].rearrange("o d -> d o")))
            assert len(small) == NSMALL
            for t in range(TT):
                act.wait_ge(x_in, 16 * TT)
                if t:
                    act.wait_ge(sq1, t)
                act.activation(hT[:, 0:4, :].rearrange("p k s -> p (k s)"), xres[:, t, :], ACT.Square,
                               accum_out=stat[:, 0, t:t + 1]).then_inc(sq1, 1)
            act.wait_ge(var1, 1)
            act.activation(stat[:, 2, :], stat[:, 1, :], ACT.Sqrt).then_inc(std1, 1)
            for dst, src in small:
                act.dma_start(dst, src).then_inc(small_in, 16)
            act.wait_ge(rel_ok, 1)
            act.dma_start(scratch.ap().rearrange("(h c) -> h c", h=AH), rrow).then_inc(rel_out, 16)
            act.wait_ge(rel_out, 16)
            act.dma_start(toep, bass.AP(scratch, 0, [[1, P], [TOEP, AH], [1, SEQ]])).then_inc(rel_in, 16)
            act.wait_ge(hT_ps, 4)
            act.dma_start(gate_bias, a["b_gate"][0:1, :].to_broadcast([P, 2 * D])).then_inc(gbias_in, 16)
            for c in range(GATE0):
                act.wait_ge(proj, 2 * c + 1)
                for s0, w, kind, d0 in IN_CHUNKS[c][2]:
                    dst = {"qk": qk, "v": vals, "f": fz}[kind]
                    last = act.activation(dst[:, 0, d0:d0 + w], bank((2 * c) % 4)[:, s0:s0 + w], ACT.Copy)
                last.then_inc(ev_act, 1)
                if c == FLIP_AT:
                    for i in range(AH // 2):
                        act.wait_ge(flip_ps, i + 1)
                        act.activation(reg_r[:, i * BANK:(i + 1) * BANK], bank(4 + i % 4), ACT.Copy).then_inc(flip_ok, 1)
            act.wait_ge(qvar, 1)
            act.activation(qstat[:, 1, :, :], qstat[:, 0, :, :], ACT.Sqrt).then_inc(qstd, 1)
            act.wait_ge(fstep, 2)
            act.activation(fw[:, 1, :, :], fw[:, 0, :, :], ACT.Exp).then_inc(fexp, 1)
            act.wait_ge(fstep, 3)
            act.activation(fw[:, 2, :, :], fw[:, 1, :, :], ACT.Ln).then_inc(fln, 1)
            for what, n in ATTENTION:
                if what == "soft":
                    act.wait_ge(nmx, n + 1)
                    for i in range(2):
                        pr = probs[n % 2][:, i, 0:width(n)]
                        act.activation(pr, pr, ACT.Exp, bias=nmax[:, 2 * n + i:2 * n + i + 1],
                                       accum_out=den[:, 2 * n + i:2 * n + i + 1]).then_inc(pr_ok, 1)
                if what == "turn":
                    act.wait_ge(pT_ps, n + 1)
                    if n >= 4:
                        act.wait_ge(pv, n - 3)
                    w = len(PIECES[n][1]) * P
                    act.activation(probsT[n % 4][:, 0:w], bank(4)[:, 0:w], ACT.Copy).then_inc(pT_ok, 1)
                if what == "fill" and n % KB == KB - 1:
                    i = n // KB
                    act.wait_ge(gate_ps, i + 1)
                    act.activation(gates[:, i % TT, (i // TT) * BANK:(i // TT + 1) * BANK], bank(5),
                                   ACT.Copy).then_inc(gate_raw, 1)
            for t in range(TT):
                for i in range(t, NGATE, TT):
                    act.wait_ge(gate_z, i + 1)
                    g = gates[:, t, (i // TT) * BANK:(i // TT + 1) * BANK]
                    act.activation(g, g, ACT.Sigmoid).then_inc(gate_ok, 1)
            act.wait_ge(zero_ok, 1)
            act.dma_start(bgu[0:NE, :], a["b_gate_up"][0]).then_inc(ebias_in, 16)
            act.dma_start(bdown[0:NE, :], a["b_down"][0]).then_inc(ebias_in, 16)
            act.wait_ge(oT_ps, 1)
            act.activation(oT[:, :, 0:P], ps[0][:, 0:6 * P].rearrange("p (k s) -> p k s", k=6), ACT.Copy).then_inc(oT_act, 1)
            for t in range(TT):
                act.wait_ge(mT_ps, t + 1)
                act.activation(mT[:, :, t * P:(t + 1) * P], ps[t][:, :].rearrange("p (k s) -> p k s", k=KB),
                               ACT.Copy).then_inc(mT_ok, 1)
            for t in range(TT):
                act.wait_ge(x1_ok, 2 * (t + 1))
                act.activation(merged[:, t, :], xres[:, t, :], ACT.Square, accum_out=stat[:, 0, t:t + 1]).then_inc(sq2, 1)
            act.wait_ge(var2, 1)
            act.activation(stat[:, 2, :], stat[:, 1, :], ACT.Sqrt).then_inc(std2, 1)
            act.wait_ge(topm, 1)
            for t in range(TT):
                act.activation(egate[:, t, :], top[:, t, 0:TOPK], ACT.Exp, bias=ntop[:, t:t + 1],
                               accum_out=esum[:, t:t + 1]).then_inc(gexp2, 1)
            act.wait_ge(GT_ps, 1)
            act.activation(GT, bank(5)[0:NE, 0:SEQ], ACT.Copy).then_inc(GT_ok, 1)

            act.wait_ge(cnt_ok, 3)
            steps = act.value_load(counts[0:1, 0:1], min_val=NE, max_val=MAXPASS * NE)
            act.wait_ge(gp_ps, 1)
            act.activation(gpickT, bank(7)[:, 0:TT * P], ACT.Copy).then_inc(gp_ok, 1)
            with act.Fori(0, steps) as t:
                for j in range(2):
                    act.wait_ge(g_ok, 2 * t + j + 1)
                    act.activation(glu_s, glu_g, ACT.Sigmoid, scale=ALPHA).then_inc(sig_ok, 1)
                for j in range(2):
                    act.wait_ge(midT_ps, 2 * t + j + 1)
                    act.activation(midT[:, j, :, :].rearrange("p b s -> p (b s)"), bank(7)[:, 0:2 * P],
                                   ACT.Copy).then_inc(midT_ok, 1)
                act.wait_ge(dn_ps, t + 1)
                act.activation(yb, bank(6), ACT.Copy).then_inc(yb_ok, 1)
                act.wait_ge(gp_ps, t + 2)
                act.wait_ge(scat, t + 1)
                act.activation(gpickT, bank(7)[:, 0:TT * P], ACT.Copy).then_inc(gp_ok, 1)

        @block.vector
        def _(dve):
            dve.memset(bdown[:, :], 0.0)
            dve.wait_ge(sq1, TT)
            dve.tensor_scalar(stat[:, 1, :], stat[:, 0, :], 1.0 / D, EPS, ALU.mult, ALU.add).then_inc(var1, 1)
            dve.wait_ge(std1, 1)
            dve.reciprocal(stat[:, 3, :], stat[:, 2, :]).then_inc(rstd1, 1)
            dve.wait_ge(rstd1, 1)
            for t in range(TT):
                dve.wait_ge(consts, 13)
                dve.tensor_scalar(h[:, t, :], xres[:, t, :], stat[:, 3, t:t + 1], None, ALU.mult).then_inc(h_ok, 1)
            dve.wait_ge(g1_in, 16)
            for i in range(4):
                t, half = i // 2, i % 2
                dve.wait_ge(hT_ps, i + 1)
                dve.tensor_tensor(hT[:, 4 * half:4 * half + 4, t * P:(t + 1) * P],
                                  bank(i).rearrange("p (k s) -> p k s", k=4),
                                  g1[:, 4 * half:4 * half + 4].unsqueeze(2).to_broadcast([P, 4, P]),
                                  ALU.mult).then_inc(hT_ok, 1)
            dve.wait_ge(rel_ps, 1)
            dve.tensor_tensor(rrow, bank(4)[0:AH, 0:TOEP], rmask, ALU.add).then_inc(rel_ok, 1)
            dve.wait_ge(small_in, 16 * NSMALL)
            for i in (0, 2):
                dve.tensor_scalar(gain[:, i:i + 1], gain[:, i:i + 1], HD ** -0.5, None, ALU.mult).then_inc(gain_ok, 1)
            for c in range(GATE0):
                dve.wait_ge(proj, 2 * c + 2)
                for s0, w, kind, d0 in IN_CHUNKS[c][2]:
                    dst = {"qk": qk, "v": vals, "f": fz}[kind]
                    last = dve.tensor_copy(dst[:, 1, d0:d0 + w], bank((2 * c + 1) % 4)[:, s0:s0 + w])
                last.then_inc(ev_dve, 1)
                if 1 <= c <= NQK:
                    s0, w, _, d0 = [x for x in IN_CHUNKS[c - 1][2] if x[2] == "qk"][0]
                    for t in range(TT):
                        dve.wait_ge(qsq, TT * (c - 1) + t + 1)
                        dve.tensor_reduce(qstat[:, 0, t, d0 // HD:(d0 + w) // HD],
                                          sq[:, t, 0:w].rearrange("p (h d) -> p h d", d=HD), AX_X,
                                          ALU.add).then_inc(qsum, 1)
                if c == NQK:
                    dve.wait_ge(qsum, TT * NQK)
                    dve.tensor_scalar(qstat[:, 0, :, :], qstat[:, 0, :, :], 1.0 / HD, EPS, ALU.mult,
                                      ALU.add).then_inc(qvar, 1)
            dve.wait_ge(qstd, 1)
            dve.reciprocal(qstat[:, 0, :, :], qstat[:, 1, :, :]).then_inc(qrstd, 1)
            dve.wait_ge(qrstd, 1)
            for t in range(TT):
                q = qk[:, t, :].rearrange("p (h d) -> p h d", d=HD)
                dve.tensor_tensor(q, q, qstat[:, 0, t, :].unsqueeze(2).to_broadcast([P, QKW // HD, HD]),
                                  ALU.mult).then_inc(qn, 1)
            dve.wait_ge(ev_act, GATE0)
            dve.wait_ge(ev_dve, GATE0)
            dve.tensor_tensor(fz[:, :, :], fz[:, :, :], fbias[:, :].unsqueeze(1).to_broadcast([P, TT, FH]),
                              ALU.add).then_inc(fstep, 1)
            dve.wait_ge(fstep, 1)
            dve.scalar_tensor_tensor(out=fw[:, 0, :, :], in0=fz[:, :, :], scalar=-1.0, in1=fz[:, :, :], op0=ALU.mult,
                                     op1=ALU.min).then_inc(fstep, 1)
            dve.wait_ge(fexp, 1)
            dve.tensor_scalar(fw[:, 1, :, :], fw[:, 1, :, :], 1.0, None, ALU.add).then_inc(fstep, 1)
            dve.wait_ge(fln, 1)
            dve.scalar_tensor_tensor(out=logf[:, :, :], in0=fz[:, :, :], scalar=0.0, in1=fw[:, 2, :, :], op0=ALU.min,
                                     op1=ALU.subtract).then_inc(logf_ok, 1)

            dve.wait_ge(gain_ok, 2)
            for i in range(len(QK_BATCHES) * TT):
                t, (b0, nb, gi) = i // len(QK_BATCHES), QK_BATCHES[i % len(QK_BATCHES)]
                dve.wait_ge(qT_ps, i + 1)
                dve.tensor_scalar(qkT[:, b0:b0 + nb, t * P:(t + 1) * P],
                                  bank(i % 4)[:, 0:nb * P].rearrange("p (k s) -> p k s", k=nb),
                                  gain[:, gi:gi + 1], None, ALU.mult).then_inc(qT_ok, 1)
            dve.wait_ge(cum_ps, 1)
            dve.tensor_copy(cum[:, :, :], bank(6)[:, 0:TT * FH].rearrange("p (t h) -> p t h", t=TT)).then_inc(cum_ok, 1)
            dve.tensor_scalar(negcT[:, :], bank(7)[0:FH, 0:SEQ], -1.0, None, ALU.mult).then_inc(cum_ok, 1)
            dve.wait_ge(consts, 13)

            def attn_out(n, u0, u1, src, dst):
                dve.wait_ge(pr_ok, u1)
                dve.reciprocal(rden[:, u0:u1], den[:, u0:u1]).then_inc(rden_ok, 1)
                dve.wait_ge(rden_ok, n)
                dve.wait_ge(pv, 1 + max(i for i, (p, _) in enumerate(PIECES) if 2 * p < u1))
                dve.tensor_tensor(dst.rearrange("p (u d) -> p u d", d=HD), src.rearrange("p (u d) -> p u d", d=HD),
                                  rden[:, u0:u1].unsqueeze(2).to_broadcast([P, u1 - u0, HD]), ALU.mult).then_inc(o_ok, 1)

            for what, p in ATTENTION:
                if what != "scores":
                    continue
                kind, t, s0 = PAIRS[p]
                nk = keys(p)
                dve.wait_ge(sc_ps, p + 1)
                if p >= 2:
                    dve.wait_ge(pT_ps, 1 + max(i for i, (v, _) in enumerate(PIECES) if v == p - 2))
                if p == 0:
                    dve.wait_ge(flip_ok, AH // 2)
                if p == NPA:
                    dve.wait_ge(cum_ok, 2)
                for i in range(2):
                    if kind == "a":
                        dve.tensor_tensor(probs[p % 2][:, i, 0:3 * nk].rearrange("p (g c) -> p g c", g=3),
                                          ps[i][:, 0:3 * SEQ].rearrange("p (g c) -> p g c", g=3)[:, :, 0:nk],
                                          toep[:, :, :].rearrange("p (g s) c -> p g s c", g=3)[:, :, s0 + i, SEQ - nk:SEQ],
                                          ALU.add).then_inc(sc_add, 1)
                    else:
                        dve.scalar_tensor_tensor(out=probs[p % 2][:, i, 0:nk], in0=bank(2 * i + p % 2)[:, 0:nk],
                                                 scalar=cum[:, t, s0 + i:s0 + i + 1], in1=causal[:, SEQ - nk:SEQ],
                                                 op0=ALU.add, op1=ALU.add).then_inc(sc_add, 1)
                dve.wait_ge(sc_add, 2 * p + 2)
                dve.tensor_reduce(amax[:, 2 * p:2 * p + 2], probs[p % 2][:, :, 0:width(p)], AX_X, ALU.max).then_inc(mx, 1)
                dve.wait_ge(mx, p + 1)
                dve.tensor_scalar(nmax[:, 2 * p:2 * p + 2], amax[:, 2 * p:2 * p + 2], -1.0, None, ALU.mult).then_inc(nmx, 1)
                if p == NPA + 1:
                    attn_out(1, 0, NUA, bank(6), o_a.rearrange("p t d -> p (t d)"))
                if p == NPA + FH // 2 + 1:
                    attn_out(2, NUA, NUA + FH, bank(7), o_b[:, 0, :])
            attn_out(3, NUA + FH, NU, bank(6), o_b[:, 1, :])
            dve.memset(bgu[:, :], 0.0).then_inc(zero_ok, 1)
            dve.wait_ge(oT_ps, 2)
            dve.tensor_copy(oT[:, :, P:SEQ], ps[1][:, 0:6 * P].rearrange("p (k s) -> p k s", k=6)).then_inc(oT_dve, 1)
            for i in range(2 * TT):
                t, n = i // 2, i % 2
                dve.wait_ge(br_ps, i + 1)
                dve.wait_ge(gate_ok, (t + 1) * NGATE // TT)
                for b in range(2):
                    dve.tensor_tensor(prod[:, i % 2, b, :], bank(4 + 2 * (i % 2) + b),
                                      gates[:, t, b * D + n * BANK:b * D + (n + 1) * BANK], ALU.mult).then_inc(br_mul, 1)
                dve.wait_ge(br_mul, 2 * i + 2)
                dve.tensor_tensor(merged[:, t, n * BANK:(n + 1) * BANK], prod[:, i % 2, 0, :], prod[:, i % 2, 1, :],
                                  ALU.add).then_inc(merged_ok, 1)
            dve.wait_ge(x2_in, 16 * TT)
            for i in range(2 * TT):
                t, n = i // 2, i % 2
                dve.wait_ge(wo_ps, i + 1)
                xs = xres[:, t, n * BANK:(n + 1) * BANK]
                dve.tensor_tensor(xs, bank(4 + i), xs, ALU.add).then_inc(x1_ok, 1)
            dve.wait_ge(sq2, TT)
            dve.tensor_scalar(stat[:, 1, :], stat[:, 0, :], 1.0 / D, EPS, ALU.mult, ALU.add).then_inc(var2, 1)
            dve.wait_ge(std2, 1)
            dve.reciprocal(stat[:, 3, :], stat[:, 2, :]).then_inc(rstd2, 1)
            dve.wait_ge(rstd2, 1)
            for t in range(TT):
                dve.tensor_scalar(hn[:, t, :], xres[:, t, :], stat[:, 3, t:t + 1], None, ALU.mult).then_inc(hn_ok, 1)
            for i in range(4):
                t, half = i // 2, i % 2
                dve.wait_ge(h2_ps, i + 1)
                dve.tensor_tensor(hT[:, 4 * half:4 * half + 4, t * P:(t + 1) * P],
                                  bank(i).rearrange("p (k s) -> p k s", k=4),
                                  g2[:, 4 * half:4 * half + 4].unsqueeze(2).to_broadcast([P, 4, P]),
                                  ALU.mult).then_inc(h2_ok, 1)
            dve.wait_ge(lg_ps, 1)
            dve.tensor_tensor(logits[:, :, :], bank(4)[:, 0:TT * NE].rearrange("p (t e) -> p t e", t=TT),
                              rbias[:, :].unsqueeze(1).to_broadcast([P, TT, NE]), ALU.add).then_inc(lg_ok, 1)
            dve.wait_ge(lg_ok, 1)
            for t in range(TT):
                dve.max(top[:, t, :], logits[:, t, :]).then_inc(tops, 1)
            dve.wait_ge(tops, TT)
            for t in range(TT):
                dve.max_index(topi[:, t, :], top[:, t, :], logits[:, t, :]).then_inc(tops, 1)
            dve.tensor_scalar(ntop[:, :], top[:, :, 0], -1.0, None, ALU.mult).then_inc(topm, 1)
            dve.wait_ge(tops, 2 * TT)
            dve.tensor_copy(topf[:, :, :], topi[:, :, 0:TOPK]).then_inc(rt, 1)
            dve.wait_ge(rt, 1)
            hs = [P, TT, TOPK, NE]
            dve.tensor_tensor(hit, exp_no[:, :].unsqueeze(1).unsqueeze(1).to_broadcast(hs),
                              topf[:, :, :].unsqueeze(3).to_broadcast(hs), ALU.is_equal).then_inc(rt, 1)
            dve.wait_ge(rt, 2)
            dve.tensor_reduce(mask[:, :, :], hit.rearrange("p t k e -> p t e k"), AX_X,
                              ALU.add).then_inc(mask_ok, 1)
            dve.memset(table[:, :, :], BIG).then_inc(rt, 1)
            dve.wait_ge(gexp2, TT)
            dve.reciprocal(ersum[:, :], esum[:, :]).then_inc(rt, 1)
            dve.wait_ge(rt, 4)
            dve.tensor_tensor(egate[:, :, :], egate[:, :, :], ersum[:, :].unsqueeze(2).to_broadcast([P, TT, TOPK]),
                              ALU.mult).then_inc(rt, 1)
            dve.wait_ge(rt, 5)
            dve.tensor_tensor(ghit, hit, egate[:, :, :].unsqueeze(3).to_broadcast(hs),
                              ALU.mult).then_inc(rt, 1)
            dve.wait_ge(rt, 6)
            dve.tensor_reduce(G[:, :, :], ghit.rearrange("p t k e -> p t e k"), AX_X,
                              ALU.add).then_inc(rt, 1)
            dve.wait_ge(pos_ps, 1)
            dve.scalar_tensor_tensor(out=posm[:, :, :], in0=mask[:, :, :], scalar=-BIG,
                                     in1=bank(4)[:, 0:TT * NE].rearrange("p (t e) -> p t e", t=TT), op0=ALU.mult,
                                     op1=ALU.add).then_inc(rt, 1)
            dve.tensor_reduce(cmax[:, :], bank(4)[:, TT * NE:(TT + 1) * NE], AX_X, ALU.max).then_inc(cnt_ok, 1)
            dve.wait_ge(rt, 8)
            for q in range(MAXPASS):
                for t in range(TT):
                    dve.tensor_scalar(table[:, q * NE:(q + 1) * NE, t], posm[:, t, :], BIG - SLOTS * q, None,
                                      ALU.add)
                    dve.tensor_copy(table[:, q * NE:(q + 1) * NE, 2 + t], G[:, t, :])
                last = dve.tensor_copy(table[:, q * NE:(q + 1) * NE, 4], ident[:, 0:NE])
            last.then_inc(tab_ok, 1)
            dve.wait_ge(cnt_ok, 1)
            dve.tensor_scalar(over[:, :], thr[:, :], cmax[:, 0:1], None, ALU.is_lt).then_inc(rt, 1)
            dve.wait_ge(rt, 9)
            dve.tensor_reduce(more[:, :], over[:, :], AX_X, ALU.add).then_inc(rt, 1)
            dve.wait_ge(rt, 10)
            dve.tensor_scalar(counts[:, 0:1], more[:, :], float(NE), float(NE), ALU.mult, ALU.add).then_inc(cnt_ok, 1)
            dve.tensor_scalar(counts[:, 1:2], more[:, :], 1.0, None, ALU.add).then_inc(cnt_ok, 1)

            def gathered(t):
                dve.wait_ge(xg_ps, t + 1)
                dve.tensor_tensor(xT, bank(7).rearrange("p (k s) -> p k s", k=KB),
                                  g2[:, :].unsqueeze(2).to_broadcast([P, KB, SLOTS]), ALU.mult).then_inc(xg_ok, 1)

            dve.wait_ge(cnt_ok, 3)
            steps = dve.value_load(counts[0:1, 0:1], min_val=NE, max_val=MAXPASS * NE)
            gathered(0)
            with dve.Fori(0, steps) as t:
                for j in range(2):
                    dve.wait_ge(gu_ps, 2 * t + j + 1)
                    if j:
                        dve.wait_ge(mid_ok, 2 * t + 1)
                    dve.tensor_scalar(glu_g, bank(4 + j)[:, 0:2 * P], LIMIT, None, ALU.min).then_inc(g_ok, 1)
                    dve.tensor_scalar(glu_u, bank(4 + j)[:, 2 * P:4 * P], LIMIT, -LIMIT, ALU.min, ALU.max).then_inc(u_ok, 1)
                    dve.wait_ge(u_ok, 2 * t + j + 1)
                    dve.wait_ge(g_ok, 2 * t + j + 1)
                    dve.scalar_tensor_tensor(out=glu_u, in0=glu_u, scalar=1.0, in1=glu_g, op0=ALU.add,
                                             op1=ALU.mult).then_inc(ug_ok, 1)
                    dve.wait_ge(ug_ok, 2 * t + j + 1)
                    dve.wait_ge(sig_ok, 2 * t + j + 1)
                    if j:
                        dve.wait_ge(midT_ps, 2 * t + 1)
                    dve.tensor_tensor(mid, glu_u, glu_s, ALU.mult).then_inc(mid_ok, 1)
                gathered(t + 1)
            dve.wait_ge(scat, steps)
            for t in range(TT):
                dve.tensor_tensor(xres[:, t, :], ps[t][:, :], xres[:, t, :], ALU.add).then_inc(fin, 1)

        @block.tensor
        def _(pe):
            dma_done = lambda n: pe.wait_ge(landed[n % RING], landing(n))
            pe.wait_ge(consts, 3)
            for i in range(4):
                t, half = i // 2, i % 2
                pe.wait_ge(h_ok, t + 1)
                for k in range(4):
                    last = pe.transpose(bank(i)[:, k * P:(k + 1) * P],
                                        h[:, t, :].rearrange("p (q k) -> p k q", k=KB)[:, 4 * half + k, :], ident[:, :])
                last.then_inc(hT_ps, 1)
            pe.wait_ge(rel_op_in, 48)
            pe.matmul(bank(4)[0:AH, 0:TOEP], rel, onehot, start=True, stop=True).then_inc(rel_ps, 1)

            def project(c):
                w = IN_CHUNKS[c][1]
                wt = ring[c % RING][:, 0:KB * w].rearrange("p (k c) -> p k c", k=KB)
                dma_done(c)
                for t in range(TT):
                    if c >= 2:
                        pe.wait_ge((ev_act, ev_dve)[t], c - 1)
                    for k in range(KB):
                        last = pe.matmul(bank((2 * c + t) % 4)[:, 0:w], hT[:, k, t * P:(t + 1) * P], wt[:, k, :],
                                         start=(k == 0), stop=(k == KB - 1))
                    last.then_inc(proj, 1)

            def fill(n):
                i, k = n // KB, n % KB
                c, t = GATE0 + i // TT, i % TT
                if k == 0:
                    dma_done(c)
                    if i:
                        pe.wait_ge(gate_raw, i)
                wt = ring[c % RING][:, 0:KB * BANK].rearrange("p (k c) -> p k c", k=KB)
                mm = pe.matmul(bank(5), hT[:, k, t * P:(t + 1) * P], wt[:, k, :], start=(k == 0), stop=(k == KB - 1))
                if k == KB - 1:
                    mm.then_inc(gate_ps, 1)

            pe.wait_ge(hT_ok, 4)
            for c in range(GATE0):
                project(c)
                if c == FLIP_AT:
                    pe.wait_ge(rel_in, 16)
                    pe.wait_ge(consts, 13)
                    for i in range(AH // 2):
                        if i >= 4:
                            pe.wait_ge(flip_ok, i - 3)
                        pe.matmul(bank(4 + i % 4), anti[:, :], reg_r[:, i * BANK:(i + 1) * BANK], start=True,
                                  stop=True).then_inc(flip_ps, 1)
            pe.wait_ge(flip_ok, AH // 2)
            for i in range(len(QK_BATCHES) * TT):
                t, (b0, nb, _) = i // len(QK_BATCHES), QK_BATCHES[i % len(QK_BATCHES)]
                if i == 0:
                    for n in range(KB):
                        fill(n)
                pe.wait_ge(qn, t + 1)
                if i >= 4:
                    pe.wait_ge(qT_ok, i - 3)
                for k in range(nb):
                    last = pe.transpose(bank(i % 4)[:, k * P:(k + 1) * P], qk[:, t, (b0 + k) * P:(b0 + k + 1) * P],
                                        ident[:, :])
                last.then_inc(qT_ps, 1)

            def cumulate():
                pe.wait_ge(logf_ok, 1)
                pe.wait_ge(consts, 13)
                pe.matmul(bank(6)[:, 0:FH], tri_le[:, :], logf[:, 0, :], start=True, stop=True)
                pe.matmul(bank(6)[:, FH:2 * FH], ones[:, :], logf[:, 0, :], start=True, stop=False)
                pe.matmul(bank(6)[:, FH:2 * FH], tri_le[:, :], logf[:, 1, :], start=False, stop=True)
                pe.matmul(bank(7)[0:FH, 0:P], logf[:, 0, :], tri_le[:, :], start=True, stop=True)
                pe.matmul(bank(7)[0:FH, P:SEQ], logf[:, 0, :], ones[:, :], start=True, stop=False)
                pe.matmul(bank(7)[0:FH, P:SEQ], logf[:, 1, :], tri_le[:, :], start=False, stop=True).then_inc(cum_ps, 1)

            def scores(p):
                kind, t, s0 = PAIRS[p]
                nk = keys(p)
                if p:
                    pe.wait_ge(sc_add, 2 * (p if p <= NPA else p - 1))
                out = [ps[i][:, :] if kind == "a" else bank(2 * i + p % 2) for i in range(2)]
                if kind == "b":
                    for i in range(2):
                        pe.matmul(out[i][:, 0:nk], ident[0:FH, s0 + i:s0 + i + 1].to_broadcast([FH, P]), negcT[:, 0:nk],
                                  start=True, stop=False)
                for g in range(GROUPS if kind == "a" else 1):
                    for i in range(2):
                        hd = g * SLOTHEADS + s0 + i if kind == "a" else s0 + i
                        qb, kb = (hd // 2, AH // 2 + hd // 2) if kind == "a" else (AH + hd // 2, AH + FH // 2 + hd // 2)
                        last = pe.matmul(out[i][:, g * SEQ:g * SEQ + nk], qkT[i * HD:(i + 1) * HD, qb, t * P:(t + 1) * P],
                                         qkT[i * HD:(i + 1) * HD, kb, 0:nk], start=(kind == "a"), stop=True)
                last.then_inc(sc_ps, 1)

            def turn(n):
                p, bs = PIECES[n]
                pe.wait_ge(pr_ok, 2 * p + 2)
                if n:
                    pe.wait_ge(pT_ok, n)
                for m, (i, g, k) in enumerate(bs):
                    o = g * keys(p) + k * P
                    last = pe.transpose(bank(4)[:, m * P:(m + 1) * P], probs[p % 2][:, i, o:o + P], ident[:, :])
                last.then_inc(pT_ps, 1)

            def values(n):
                p, bs = PIECES[n]
                kind, t, s0 = PAIRS[p]
                pe.wait_ge(pT_ok, n + 1)
                if p == NPA + FH // 2:
                    pe.wait_ge(o_ok, 1)
                ob = bank(6) if kind == "a" or t == 1 else bank(7)
                for m, (i, g, k) in enumerate(bs):
                    o = (t * SLOTHEADS + s0 + i if kind == "a" else s0 + i) * HD
                    v0 = (g * SLOTHEADS + s0 + i) * HD if kind == "a" else AW + (s0 + i) * HD
                    last = pe.matmul(ob[:, o:o + HD], probsT[n % 4][:, m * P:(m + 1) * P], vals[:, k, v0:v0 + HD],
                                     start=((i, g, k) == (i, 0, 0)),
                                     stop=(k == t and g == (GROUPS - 1 if kind == "a" else 0)))
                last.then_inc(pv, 1)

            pe.wait_ge(qT_ok, len(QK_BATCHES) * TT)
            cumulate()
            pe.wait_ge(cum_ok, 2)
            for what, n in ATTENTION:
                if what == "fill" and n >= KB:
                    fill(n)
                if what == "scores":
                    scores(n)
                if what == "turn":
                    turn(n)
                if what == "values":
                    values(n)
            pe.wait_ge(o_ok, 3)
            for t in range(TT):
                for b in range(6):
                    src = o_a[:, t, b * P:(b + 1) * P] if b < 2 else o_b[:, t, (b - 2) * P:(b - 1) * P]
                    last = pe.transpose(ps[t][:, b * P:(b + 1) * P], src, ident[:, :])
                last.then_inc(oT_ps, 1)
            dma_done(NIN)
            dma_done(NIN + 1)
            pe.wait_ge(oT_act, 1)
            pe.wait_ge(oT_dve, 1)
            for i in range(2 * TT):
                t, n = i // 2, i % 2
                if i >= 2:
                    pe.wait_ge(br_mul, 2 * (i - 1))
                for b, ks in ((0, range(0, 2)), (1, range(2, 6))):
                    for k in ks:
                        w = ring[(NIN + k // 4) % RING]
                        last = pe.matmul(bank(4 + 2 * (i % 2) + b), oT[:, k, t * P:(t + 1) * P],
                                         w[:, (k % 4) * D + n * BANK:(k % 4) * D + (n + 1) * BANK],
                                         start=(k == ks[0]), stop=(k == ks[-1]))
                last.then_inc(br_ps, 1)
            for t in range(TT):
                pe.wait_ge(merged_ok, 2 * (t + 1))
                for k in range(KB):
                    last = pe.transpose(ps[t][:, k * P:(k + 1) * P], merged[:, t, k * P:(k + 1) * P], ident[:, :])
                last.then_inc(mT_ps, 1)
            dma_done(NIN + 2)
            dma_done(NIN + 3)
            for i in range(2 * TT):
                t, n = i // 2, i % 2
                pe.wait_ge(mT_ok, t + 1)
                for k in range(KB):
                    w = ring[(NIN + 2 + k // 4) % RING]
                    last = pe.matmul(bank(4 + i), mT[:, k, t * P:(t + 1) * P],
                                     w[:, (k % 4) * D + n * BANK:(k % 4) * D + (n + 1) * BANK],
                                     start=(k == 0), stop=(k == KB - 1))
                last.then_inc(wo_ps, 1)
            for i in range(4):
                t, half = i // 2, i % 2
                pe.wait_ge(hn_ok, t + 1)
                for k in range(4):
                    last = pe.transpose(bank(i)[:, k * P:(k + 1) * P],
                                        hn[:, t, :].rearrange("p (q k) -> p k q", k=KB)[:, 4 * half + k, :], ident[:, :])
                last.then_inc(h2_ps, 1)
            pe.wait_ge(h2_ok, 4)
            for t in range(TT):
                for k in range(KB):
                    last = pe.matmul(bank(4)[:, t * NE:(t + 1) * NE], hT[:, k, t * P:(t + 1) * P], wr[:, k, :],
                                     start=(k == 0), stop=(k == KB - 1))
            last.then_inc(lg_ps, 1)
            pe.wait_ge(mask_ok, 1)
            pe.matmul(bank(4)[:, 0:NE], tri_lt[:, :], mask[:, 0, :], start=True, stop=True)
            pe.matmul(bank(4)[:, NE:2 * NE], ones[:, :], mask[:, 0, :], start=True, stop=False)
            pe.matmul(bank(4)[:, NE:2 * NE], tri_lt[:, :], mask[:, 1, :], start=False, stop=True)
            pe.matmul(bank(4)[:, 2 * NE:3 * NE], ones[:, :], mask[:, 0, :], start=True, stop=False)
            pe.matmul(bank(4)[:, 2 * NE:3 * NE], ones[:, :], mask[:, 1, :], start=False, stop=True).then_inc(pos_ps, 1)
            pe.wait_ge(rt, 7)
            for t in range(TT):
                last = pe.transpose(bank(5)[0:NE, t * P:(t + 1) * P], G[:, t, :], ident[:, :])
            last.then_inc(GT_ps, 1)
            pe.wait_ge(GT_ok, 1)
            pe.wait_ge(ebias_in, 32)
            for t in range(TT):
                for n in range(2):
                    pe.matmul(bank(2 * t + n), GT[:, t * P:(t + 1) * P], bdown[0:NE, n * BANK:(n + 1) * BANK],
                              start=True, stop=False, skip_group_check=True)

            def gather(t):
                pe.wait_ge(pick_ok, t + 1)
                for k in range(KB):
                    for tt in range(TT):
                        last = pe.matmul(bank(7)[:, k * SLOTS:(k + 1) * SLOTS],
                                         hn[:, tt, :].rearrange("p (q k) -> p k q", k=KB)[:, k, :], pick[:, tt, :],
                                         start=(tt == 0), stop=(tt == TT - 1))
                last.then_inc(xg_ps, 1)

            def turn_gates(t):
                pe.wait_ge(xg_ok, t + 1)
                for tt in range(TT):
                    last = pe.transpose(bank(7)[:, tt * P:(tt + 1) * P], gpick[:, tt, :], ident[:, :])
                last.then_inc(gp_ps, 1)

            def turn_mid(t, j):
                pe.wait_ge(mid_ok, 2 * t + j + 1)
                if j:
                    pe.wait_ge(midT_ok, 2 * t + 1)
                for b in range(2):
                    last = pe.transpose(bank(7)[:, b * P:(b + 1) * P], mid[:, b * P:(b + 1) * P], ident[:, :])
                last.then_inc(midT_ps, 1)

            def chunk(t, c):
                pe.wait_ge(landed[eslot(c)], t * eland(c) + (pre_land[eslot(c)] + eland(c)))

            def down(t, half):
                chunk(t, 4 + half)
                pe.wait_ge(midT_ok, 2 * t + half + 1)
                w = ring[eslot(4 + half)]
                for k in range(4):
                    for n in range(2):
                        last = pe.matmul(bank(6)[n * SLOTS:(n + 1) * SLOTS, :],
                                         midT[:, half, k % 2, (k // 2) * SLOTS:(k // 2 + 1) * SLOTS],
                                         w[:, k * D + n * BANK:k * D + (n + 1) * BANK],
                                         start=(half == 0 and k == 0), stop=(half == 1 and k == 3))
                last.then_inc((used, dn_ps)[half], 1)

            pe.wait_ge(cnt_ok, 3)
            steps = pe.value_load(counts[0:1, 0:1], min_val=NE, max_val=MAXPASS * NE)
            gather(0)
            turn_gates(0)
            with pe.Fori(0, steps) as t:
                pe.wait_ge(xg_ok, t + 1)
                for j in range(2):
                    gu = bank(4 + j)
                    for n in range(2):
                        pe.matmul(gu[n * SLOTS:(n + 1) * SLOTS, :], sel_e,
                                  bgu.rearrange("p (w j n c) -> p w j n c", w=2, j=2, n=2)[:, :, j, n, :],
                                  start=True, stop=False)
                    for kh in range(2):
                        chunk(t, 2 * j + kh)
                        w = ring[eslot(2 * j + kh)][:, :].rearrange("p (k w n c) -> p k w n c", k=4, w=2, n=2)
                        for k in range(4):
                            for n in range(2):
                                last = pe.matmul(gu[n * SLOTS:(n + 1) * SLOTS, :], xT[:, 4 * kh + k, :],
                                                 w[:, k, :, n, :], start=False, stop=(kh == 1 and k == 3))
                        if kh == 0:
                            last.then_inc(used, 1)
                    last.then_inc(gu_ps, 1)
                pe.wait_ge(gp_ok, t + 1)
                turn_mid(t, 0)
                down(t, 0)
                turn_mid(t, 1)
                down(t, 1)
                pe.wait_ge(midT_ok, 2 * t + 2)
                gather(t + 1)
                pe.wait_ge(yb_ok, t + 1)
                for tt in range(TT):
                    for n in range(2):
                        last = pe.matmul(bank(2 * tt + n), gpickT[n * SLOTS:(n + 1) * SLOTS, tt * P:(tt + 1) * P],
                                         yb[n * SLOTS:(n + 1) * SLOTS, :], start=False, stop=False,
                                         skip_group_check=True)
                last.then_inc(scat, 1)
                turn_gates(t + 1)


def _tables():
    max_exact, max_distance = NB // 2, 2048
    dist = 2 * P - 1 - np.arange(TOEP)
    n = np.maximum(dist, 0)
    large = max_exact + (np.log(np.maximum(n, 1).astype(np.float64) / max_exact) / np.log(max_distance / max_exact)
                         * (NB - max_exact)).astype(np.int64)
    bucket = np.where(n < max_exact, n, np.minimum(large, NB - 1))
    onehot = ((np.arange(NB)[:, None] == bucket[None, :]) & (dist >= 0)[None, :]).astype(np.float32)
    reach = np.zeros((AH, TOEP), np.float32)
    for g, (window, dilation) in enumerate(((128, 1), (512, 4), (2048, 16))):
        ok = (dist >= 0) & (dist % dilation == 0) & (dist <= window)
        reach[g * SLOTHEADS:(g + 1) * SLOTHEADS] = np.where(ok, 0.0, NEG)
    return onehot, reach


_INS = ["x", "ln1_g", "w_in", "b_forget", "b_gate", "q_norm_a", "k_norm_a", "q_norm_b", "k_norm_b", "rel_bias",
        "w_branch_a", "w_branch_b", "w_out", "ln2_g", "w_router", "b_router", "w_gate_up", "b_gate_up", "w_down",
        "b_down"]


def kernel(**inputs):
    import numpy as _np
    import concourse.bacc as _bacc
    from concourse import mybir as _mybir
    from concourse.bass_utils import run_bass_kernel_spmd as _run

    nc = _bacc.Bacc("TRN2", target_bir_lowering=False, num_devices=1)
    arrays, args = {}, {}
    given = {n: _np.ascontiguousarray(inputs[n]) for n in _INS}
    given["bucket_onehot"], given["reach_mask"] = _tables()
    for name, v in given.items():
        arrays[f"in_{name}"] = v
        args[name] = nc.dram_tensor(f"in_{name}", v.shape, _mybir.dt.from_np(v.dtype), kind="ExternalInput").ap()
    out = nc.dram_tensor("out_0", (1, SEQ, D), F32, kind="ExternalOutput").ap()
    build(nc, args, out)
    r = _run(nc, [arrays], core_ids=[0])
    return r.results[0]["out_0"]
```

```python
from contextlib import ExitStack

import numpy as np

import concourse.bass as bass
from concourse import mybir

F32 = mybir.dt.float32
F32R = mybir.dt.float32r
I32 = mybir.dt.int32
U32 = mybir.dt.uint32
ALU = mybir.AluOpType
ACT = mybir.ActivationFunctionType
AX_X = mybir.AxisListType.X

P = 128
D = 1024
SEQ = 256
TT = SEQ // P
KB = D // P
HD = 64
GROUPS, SLOTHEADS = 3, 4
AH = GROUPS * SLOTHEADS
AW = AH * HD
FH = 8
FW = FH * HD
EPS = 1e-6
NEG = -1e30
NB = 32
NE = 32
TOPK = 4
LIMIT, ALPHA = 7.0, 1.702
SLOTS = 64
MAXPASS = SEQ // SLOTS
BIG = 10000.0

RING = 6
EXTRA = 3
LEAD = 20
PAIR = 3
SLOT = 4096
BANK = 512

QKW = 2 * AW + 2 * FW
VW = AW + FW
IN_CHUNKS = [
    (0, 512, [(0, 512, "qk", 0)]),
    (512, 512, [(0, 512, "qk", 512)]),
    (1024, 512, [(0, 512, "qk", 1024)]),
    (2048, 512, [(0, 256, "v", 512), (256, 256, "qk", 1536)]),
    (2560, 512, [(0, 512, "qk", 1792)]),
    (3072, 512, [(0, 256, "qk", 2304), (256, 256, "v", 768)]),
    (3584, 264, [(0, 256, "v", 1024), (256, 8, "f", 0)]),
    (1536, 512, [(0, 512, "v", 0)]),
    (3848, 512, [(0, 512, "g", 0)]),
    (4360, 512, [(0, 512, "g", 512)]),
    (4872, 512, [(0, 512, "g", 1024)]),
    (5384, 512, [(0, 512, "g", 1536)]),
]
NQK = 6
NIN = len(IN_CHUNKS)
NSMALL = 14
GATE0 = 8
QK_BATCHES = [(0, 4, 0), (4, 2, 0), (6, 4, 1), (10, 2, 1), (12, 4, 2), (16, 4, 3)]
FLIP_AT = 2
TOEP = 2 * P + P

PAIRS = ([("a", t, s) for t in range(TT) for s in (0, 2)]
         + [("b", t, s) for t in range(TT) for s in (0, 2, 4, 6)])
NPAIR = len(PAIRS)
NPA = 2 * TT
NU = 2 * NPAIR
NUA = 2 * NPA


def keys(p):
    return (PAIRS[p][1] + 1) * P


def width(p):
    return keys(p) * (GROUPS if PAIRS[p][0] == "a" else 1)


def blocks(p):
    kind, t, _ = PAIRS[p]
    return [(i, g, k) for i in range(2) for g in range(GROUPS if kind == "a" else 1) for k in range(t + 1)]


PIECES = [(p, blocks(p)[n:n + 4]) for p in range(NPAIR) for n in range(0, len(blocks(p)), 4)]
NGB = 2 * D // P
PER_GB = 3 * KB
FILLS = NGB * PER_GB
LATE = 24
SPLIT_POOL = 9


def attention_order():
    order, filled = [], 0

    def fill(count):
        nonlocal filled
        for n in range(min(count, FILLS - LATE - filled)):
            if n and filled % (2 * PER_GB) == 0:
                break
            order.append(("fill", filled))
            filled += 1

    while filled < 4 * PER_GB:
        fill(PER_GB)
    order.append(("scores", 0))
    fill(30)
    order.append(("soft", 0))
    for p in range(NPAIR):
        pieces = [i for i, (v, _) in enumerate(PIECES) if v == p]
        if p + 1 < NPAIR:
            order.append(("scores", p + 1))
            fill(14)
        for i in pieces:
            order.append(("turn", i))
            if i:
                order.append(("values", i - 1))
            fill(5)
            if i == pieces[max(len(pieces) - 2, 0)] and p + 1 < NPAIR:
                order.append(("soft", p + 1))
    order.append(("values", len(PIECES) - 1))
    while filled < FILLS - LATE:
        fill(FILLS)
    return order


ATTENTION = attention_order()


def build(nc, a, out):
    with ExitStack() as ctx:
        def sb(name, shape, dt=F32):
            return ctx.enter_context(nc.sbuf_tensor(name, shape, dt))

        def sem(name):
            return ctx.enter_context(nc.semaphore(name))

        def sb_split(name, n):
            t = sb(name, [P, n])
            return t, nc.alloc_sbuf_tensor_at(name + "_r", [P, n], F32R, offset=nc.sbuf_base - 4 * n)

        pairs_of = [sb_split(f"ring{i}", SLOT) for i in range(RING)]
        ring = [x[0] for x in pairs_of]
        ring_r = [x[1] for x in pairs_of]
        ps = [ctx.enter_context(nc.psum_tensor(f"ps{i}", [P, 2 * BANK], F32)) for i in range(4)]

        def bank(i):
            return ps[i // 2][:, (i % 2) * BANK:(i % 2 + 1) * BANK]

        xres_f, hT_lo_f = sb_split("xres", TT * D)
        xres = xres_f[:, :].rearrange("p (t d) -> p t d", t=TT)
        reg_n, reg_n_r = sb_split("reg_n", TT * D)
        reg_t, hT_hi_f = sb_split("reg_t", KB * SEQ)
        reg_a = sb("reg_a", [P, TT * QKW])
        reg_b = sb("reg_b", [P, TT * QKW])
        vals = sb("vals", [P, TT, VW])
        gates = sb("gates", [P, NGB, SEQ])
        reg_r = sb("reg_r", [P, AH * SEQ])

        slots = [r[:, :] for r in ring]
        slots += [reg_b[:, 0:SLOT], gates[:, :, :].rearrange("p j s -> p (j s)"), reg_a[:, 0:SLOT]]

        h = reg_n[:, :].rearrange("p (t d) -> p t d", t=TT)
        oflat = reg_n[:, :]
        o_a = oflat[:, 0:TT * SLOTHEADS * HD].rearrange("p (t d) -> p t d", t=TT)
        o_b = oflat[:, TT * SLOTHEADS * HD:TT * (SLOTHEADS * HD + FW)].rearrange("p (t d) -> p t d", t=TT)
        hn = h
        hT = xres_f[:, :].rearrange("p (k s) -> p k s", k=KB)
        hT_hi = hT_hi_f[:, :].rearrange("p (k s) -> p k s", k=KB)
        hT_lo = hT_lo_f[:, :].rearrange("p (k s) -> p k s", k=KB)
        qk = reg_a[:, :].rearrange("p (t d) -> p t d", t=TT)
        sq = reg_b[:, 2048:2048 + TT * BANK].rearrange("p (t d) -> p t d", t=TT)
        qkT = reg_b[:, :].rearrange("p (k s) -> p k s", k=QKW // P)
        mT = reg_n[:, :].rearrange("p (k s) -> p k s", k=KB)
        junk = reg_t[:, :].rearrange("p (t d) -> p t d", t=TT)
        bgu = reg_r[:, 0:2 * D]
        bdown = reg_r[:, 2 * D:3 * D]
        toep = reg_r[:, :].rearrange("p (h c) -> p h c", h=AH)
        prod = reg_a[:, 0:4 * SEQ].rearrange("p (i b s) -> p i b s", i=2, b=2)

        onehot = reg_b[0:NB, 0:TOEP]
        rmask = reg_b[0:AH, TOEP:2 * TOEP]
        rrow = reg_b[0:AH, 2 * TOEP:3 * TOEP]
        rel = reg_b[0:NB, 3 * TOEP:3 * TOEP + AH]
        vflat = vals[:, :, :].rearrange("p t d -> p (t d)")
        hw = TT * TOPK * NE
        oT = vflat[:, 0:6 * SEQ].rearrange("p (k s) -> p k s", k=6)
        x1T = vflat[:, 512:512 + KB * SEQ].rearrange("p (k s) -> p k s", k=KB)
        hit = vflat[:, 0:hw].rearrange("p (t k e) -> p t k e", t=TT, k=TOPK)
        ghit = vflat[:, hw:2 * hw].rearrange("p (t k e) -> p t k e", t=TT, k=TOPK)
        GT = vflat[0:NE, 2 * hw:2 * hw + SEQ]
        logits, mask, G, posm = (vflat[:, 3 * hw + i * TT * NE:3 * hw + (i + 1) * TT * NE]
                                 .rearrange("p (t e) -> p t e", t=TT) for i in range(4))

        at = [0]

        def take(n):
            at[0] += n
            assert at[0] <= TT * QKW
            return reg_a[:, at[0] - n:at[0]]

        probs = [take(2 * GROUPS * SEQ).rearrange("p (i c) -> p i c", i=2) for _ in range(2)]
        probsT = [take(BANK) for _ in range(4)]
        xT = reg_t[:, 0:KB * SLOTS].rearrange("p (k s) -> p k s", k=KB)
        glu_g, glu_u, glu_s, mid = (reg_t[:, i * 2 * P:(i + 1) * 2 * P] for i in range(2, 6))
        midT = reg_t[:, 12 * P:16 * P].rearrange("p (j b s) -> p j b s", j=2, b=2)
        yb = vflat[:, 1024:1536]
        gpick = vflat[:, 1536:1792].rearrange("p (t s) -> p t s", t=TT)
        gpickT = vflat[:, 1792:2048]
        pick = reg_b[:, SLOT:SLOT + TT * SLOTS].rearrange("p (t s) -> p t s", t=TT)
        sel_e = reg_b[:, SLOT + 128:SLOT + 256].rearrange("p (u s) -> p u s", u=2)
        cols = reg_b[:, SLOT + 256:SLOT + 261]
        table = reg_b[:, SLOT + 264:SLOT + 264 + 5 * (MAXPASS * NE + 1)].rearrange("p (e c) -> p e c", c=5)

        zeros = h[:, 0, 0:SEQ]
        ident = sb("ident", [P, P])
        anti = sb("anti", [P, P])
        ones = sb("ones", [P, P])
        tri_le = sb("tri_le", [P, P])
        tri_lt = sb("tri_lt", [P, P])
        causal = sb("causal", [P, SEQ])
        iota_i = sb("iota_i", [P, P], I32)
        slot_no = sb("slot_no", [P, P])
        exp_i = sb("exp_i", [P, NE], I32)
        exp_no = sb("exp_no", [P, NE])
        thr_i = sb("thr_i", [P, MAXPASS - 1], I32)
        thr = sb("thr", [P, MAXPASS - 1])
        g1 = sb("g1", [P, KB])
        g2 = sb("g2", [P, KB])
        brow = sb("brow", [NGB + KB, P])
        bcol = sb("bcol", [P, NGB + KB])
        gain = sb("gain", [P, 4])
        fbias = sb("fbias", [P, FH])
        rbias = sb("rbias", [P, NE])
        wr = sb("wr", [P, KB, NE])
        stat = sb("stat", [P, 4, TT])
        ssq = sb("ssq", [P, TT, 2])
        qstat = sb("qstat", [P, 2, TT, QKW // HD])
        fz = sb("fz", [P, TT, FH])
        fw = sb("fw", [P, 3, TT, FH])
        logf = sb("logf", [P, TT, FH])
        cum = sb("cum", [P, TT, FH])
        negcT = sb("negcT", [FH, SEQ])
        ck = [reg_n_r[0:FH, 1536 + i * SEQ:1536 + (i + 1) * SEQ] for i in range(2)]
        _, ck_sel = sb_split("ck_sel", FH)
        amax = sb("amax", [P, NU])
        nmax = sb("nmax", [P, NU])
        den = sb("den", [P, NU])
        rden = sb("rden", [P, NU])
        top = sb("top", [P, TT, 8])
        topi = sb("topi", [P, TT, 8], U32)
        topf = sb("topf", [P, TT, TOPK])
        ntop = sb("ntop", [P, TT])
        egate = sb("egate", [P, TT, TOPK])
        esum = sb("esum", [P, TT])
        ersum = sb("ersum", [P, TT])
        cmax = sb("cmax", [P, 1])
        over = sb("over", [P, MAXPASS - 1])
        more = sb("more", [P, 1])
        counts = sb("counts", [P, 4], I32)

        scratch = nc.dram_tensor("rel_rows", [AH * TOEP], F32, kind="Internal")

        landed = [sem(f"landed{i}") for i in range(RING + EXTRA)]
        landed_half = sem("landed_half")
        used = sem("used")
        x_in = [sem(f"x_in{t}") for t in range(TT)]
        w0_tail = sem("w0_tail")
        g1_in, rel_op_in, small_in = sem("g1_in"), sem("rel_op_in"), sem("small_in")
        ebias_in, x2_in = sem("ebias_in"), sem("x2_in")
        consts = sem("consts")
        sq1, var1, std1, rstd1, h_ok, hT_ps, hT_raw = (sem(n) for n in (
            "sq1", "var1", "std1", "rstd1", "h_ok", "hT_ps", "hT_raw"))
        hT_hi_ok, hT_lo_ok = sem("hT_hi_ok"), sem("hT_lo_ok")
        w_hi, w_lo, pool_hi, pool_lo = sem("w_hi"), sem("w_lo"), sem("pool_hi"), sem("pool_lo")
        flip_ps, flip_ok = sem("flip_ps"), sem("flip_ok")
        gain_ok, rel_ps, rel_ok, rel_out, rel_in = (sem(n) for n in ("gain_ok", "rel_ps", "rel_ok", "rel_out", "rel_in"))
        proj, ev_act, ev_dve = sem("proj"), sem("ev_act"), sem("ev_dve")
        gate_ps, gate_raw, gate_ok = sem("gate_ps"), sem("gate_raw"), sem("gate_ok")
        bcol_ps, bcol_ok = sem("bcol_ps"), sem("bcol_ok")
        qsq, qsum, qvar, qstd, qrstd, qn = (sem(n) for n in ("qsq", "qsum", "qvar", "qstd", "qrstd", "qn"))
        qT_ps, qT_ok = sem("qT_ps"), sem("qT_ok")
        fstep, fexp, fln, logf_ok, cum_ps, cum_ok = (sem(n) for n in (
            "fstep", "fexp", "fln", "logf_ok", "cum_ps", "cum_ok"))
        ck_ok = sem("ck_ok")
        sc_ps, sc_add, mx, nmx, pr_ok = (sem(n) for n in ("sc_ps", "sc_add", "mx", "nmx", "pr_ok"))
        pT_ps, pT_ok, pv, rden_ok, o_ok = (sem(n) for n in ("pT_ps", "pT_ok", "pv", "rden_ok", "o_ok"))
        oT_ps, oT_act, oT_dve, br_ps, br_mul = (sem(n) for n in ("oT_ps", "oT_act", "oT_dve", "br_ps", "br_mul"))
        mT_ok, wo_ps, x1_ok = sem("mT_ok"), sem("wo_ps"), sem("x1_ok")
        sq2, norm2, std2, hn_ok, x1T_ps, x1T_act, x1T_dve = (sem(n) for n in (
            "sq2", "norm2", "std2", "hn_ok", "x1T_ps", "x1T_act", "x1T_dve"))
        lg_ps, lg_ok, tops, topm, gexp2, rt, mask_ok = (sem(n) for n in (
            "lg_ps", "lg_ok", "tops", "topm", "gexp2", "rt", "mask_ok"))
        tot_ps = sem("tot_ps")
        pos_ps, GT_ps, GT_ok, tab_ok, cnt_ok = (sem(n) for n in ("pos_ps", "GT_ps", "GT_ok", "tab_ok", "cnt_ok"))
        zero_ok, wr_ok = sem("zero_ok"), sem("wr_ok")
        col_ok, pick_ok, gpick_ok, xg_ps, xg_ok, gp_ps, gp_ok = (sem(n) for n in (
            "col_ok", "pick_ok", "gpick_ok", "xg_ps", "xg_ok", "gp_ps", "gp_ok"))
        gu_ps, g_ok, sig_ok, u_ok, ug_ok, mid_ok, midT_ps, midT_ok = (sem(n) for n in (
            "gu_ps", "g_ok", "sig_ok", "u_ok", "ug_ok", "mid_ok", "midT_ps", "midT_ok"))
        dn_ps, yb_ok = sem("dn_ps"), sem("yb_ok")
        scat = [sem(f"scat{i}") for i in range(2 * TT)]
        fin, stored = sem("fin"), sem("stored")

        n_pre = NIN + 4

        def home(n):
            if n < NIN:
                return 2 * (n % PAIR), 16 * (n // PAIR + 1)
            s = n - NIN
            return s, (0 if s % 2 else 16 * (NIN // PAIR)) + (32 if s == 0 else 16)

        def rounded(n):
            return 2 * (n % PAIR) + 1

        pre_land = [max([home(n)[1] for n in range(n_pre) if home(n)[0] == s], default=0) for s in range(RING)]
        pre_land += [0] * EXTRA

        def in_chunk_read(eng, n):
            if n < GATE0:
                eng.wait_ge(proj, 2 * (n + 1))
            else:
                eng.wait_ge(gate_ps, 2 * (n - GATE0 + 1))

        def chunk_of(slot, n):
            w = IN_CHUNKS[n][1]
            return slot[:, 0:KB * w].rearrange("p (k c) -> p k c", k=KB)

        PER = 6

        def eslot(c, odd):
            return RING + c if odd and c < EXTRA else (n_pre + c) % RING

        w_in = a["w_in"][0]

        def expert_load(eng, e, c, odd):
            slot, done = slots[eslot(c, odd)], landed[eslot(c, odd)]
            if c < 4:
                j, kh = c // 2, c % 2
                src = a["w_gate_up"][0][bass.ds(e, 1)].rearrange(
                    "o (p k) (w j c) -> p (o k) w j c", k=KB, w=2, j=2)[:, kh * 4:kh * 4 + 4, :, j, :]
                dst = slot.rearrange("p (k w c) -> p k w c", k=4, w=2)
                for w in range(2):
                    eng.dma_start(dst[:, :, w, :], src[:, :, w, :]).then_inc(done, 16)
            else:
                kh = c - 4
                src = a["w_down"][0][bass.ds(e, 1)].rearrange("o (k p) c -> p (o k) c", p=P)[:, kh * 4:kh * 4 + 4, :]
                dst = slot.rearrange("p (k c) -> p k c", k=4)
                if c == 4:
                    eng.dma_start(dst, src).then_inc(done, 16)
                else:
                    eng.dma_start(dst[:, 0:2, :], src[:, 0:2, :]).then_inc(landed_half, 16)
                    eng.dma_start(dst[:, 2:4, :], src[:, 2:4, :]).then_inc(done, 16)

        def eland(c):
            return 32 if c < 4 else 16

        block = ctx.enter_context(nc.Block())

        @block.sync
        def _(sp):
            small = [
                (brow[0:NGB, :], a["b_gate"][0].rearrange("(j p) -> j p", p=P)),
                (brow[NGB:NGB + KB, :], a["ln2_g"][0].rearrange("(j p) -> j p", p=P)),
                (fbias[:, :], a["b_forget"][0:1, :].to_broadcast([P, FH])),
                (g2[:, :], a["ln2_g"][0].rearrange("(p k) -> p k", k=KB)),
                (rbias[:, :], a["b_router"][0:1, :].to_broadcast([P, NE])),
                (wr[:, :, :], a["w_router"][0].rearrange("(k p) e -> p k e", k=KB)),
            ]
            for i, n in enumerate(("q_norm_a", "k_norm_a", "q_norm_b", "k_norm_b")):
                for half in range(2):
                    small.append((gain[half * HD:(half + 1) * HD, i:i + 1], a[n].rearrange("o d -> d o")))
            assert len(small) == NSMALL
            for t in range(TT):
                sp.dma_start(xres[:, t, :], a["x"][0, t * P:(t + 1) * P, :]).then_inc(x_in[t], 16)
            for n, (c0, w, _) in enumerate(IN_CHUNKS):
                if n >= PAIR:
                    in_chunk_read(sp, n - PAIR)
                sp.dma_start(chunk_of(ring[home(n)[0]], n),
                             w_in.rearrange("(p k) c -> p k c", k=KB)[:, :, c0:c0 + w]).then_inc(landed[home(n)[0]], 16)
                if n == PAIR - 1:
                    for dst, src in ((rel, a["rel_bias"]), (onehot, a["bucket_onehot"]), (rmask, a["reach_mask"])):
                        sp.dma_start(dst, src).then_inc(rel_op_in, 16)
                    for dst, src in small:
                        sp.dma_start(dst, src).then_inc(small_in, 16)
                if n == PAIR:
                    sp.wait_ge(rel_ok, 1)
                    sp.dma_start(scratch.ap().rearrange("(h c) -> h c", h=AH), rrow).then_inc(rel_out, 16)
                    sp.wait_ge(rel_out, 16)
                    sp.dma_start(toep, bass.AP(scratch, 0, [[1, P], [TOEP, AH], [1, SEQ]])).then_inc(rel_in, 16)
            wbr = [(NIN, 0, a["w_branch_a"][0], 0, 2), (NIN, 2, a["w_branch_b"][0], 0, 2),
                   (NIN + 1, 0, a["w_branch_b"][0], 2, 2), (NIN + 2, 0, a["w_out"][0], 0, 4),
                   (NIN + 3, 0, a["w_out"][0], 4, 4)]
            for n, k0, w, b0, nb in wbr:
                in_chunk_read(sp, NIN - PAIR + (n - NIN) // 2)
                sp.dma_start(ring[home(n)[0]][:, k0 * D:(k0 + nb) * D].rearrange("p (k c) -> p k c", k=nb),
                             w.rearrange("(k p) c -> p k c", p=P)[:, b0:b0 + nb, :]).then_inc(landed[home(n)[0]], 16)
            in_chunk_read(sp, NIN - 1)
            for c in range(2):
                expert_load(sp, 0, c, False)
            sp.wait_ge(oT_ps, 2)
            expert_load(sp, 1, 0, True)
            sp.wait_ge(gate_ps, NGB // 2)
            for t in range(TT):
                sp.dma_start(xres[:, t, :], a["x"][0, t * P:(t + 1) * P, :]).then_inc(x2_in, 16)
            sp.wait_ge(br_ps, KB)
            expert_load(sp, 0, 2, False)
            expert_load(sp, 0, 3, False)
            sp.wait_ge(mT_ok, KB)
            expert_load(sp, 1, 1, True)
            expert_load(sp, 1, 2, True)
            sp.wait_ge(wo_ps, 2 * TT)
            expert_load(sp, 0, 4, False)
            expert_load(sp, 0, 5, False)

            def load_first(t, e, odd):
                sp.wait_ge(used, t * 3 - 5)
                expert_load(sp, e, 0, odd)
                sp.wait_ge(gu_ps, t * 2 - 3)
                expert_load(sp, e, 1, odd)
                sp.wait_ge(used, t * 3 - 4)
                expert_load(sp, e, 2, odd)

            def load_last(t, e):
                sp.wait_ge(gu_ps, t * 2)
                expert_load(sp, e, 3, False)
                sp.wait_ge(used, t * 3)
                expert_load(sp, e, 4, False)
                sp.wait_ge(dn_ps, t)
                expert_load(sp, e, 5, False)

            with sp.Fori(0, LEAD // 2) as i:
                for u in range(2):
                    load_first(i * 2 + (u + 2), i * 2 + (u + 2), u == 1)
                    load_last(i * 2 + (u + 1), i * 2 + (u + 1))
            with sp.Fori(LEAD // 2, NE // 2 - 1) as i:
                for u in range(2):
                    load_last(i * 2 + (u + 1), i * 2 + (u + 1))
                    load_first(i * 2 + (u + 2), i * 2 + (u + 2), u == 1)
            load_last(NE - 1, NE - 1)
            sp.wait_ge(cnt_ok, 5)
            passes = sp.value_load(counts[0:1, 1:2], min_val=1, max_val=MAXPASS)
            with sp.If(passes > 1):
                with sp.Fori(1, passes) as q:
                    load_first(q * NE, 0, False)
                    load_first(q * NE + 1, 1, True)
                    load_last(q * NE, 0)
                    with sp.Fori(0, (NE - 2) // 2) as i:
                        for u in range(2):
                            load_first(q * NE + i * 2 + (u + 2), i * 2 + (u + 2), u == 1)
                            load_last(q * NE + i * 2 + (u + 1), i * 2 + (u + 1))
                    load_last(q * NE + (NE - 1), NE - 1)
            for t in range(TT):
                sp.wait_ge(fin, 2 * t + 1)
                sp.dma_start(out[0, t * P:(t + 1) * P, 0:BANK], xres[:, t, 0:BANK]).then_inc(stored, 16)
            sp.wait_ge(stored, 16 * 2 * TT)

        @block.gpsimd
        def _(pool):
            pool.memset(ones[:, :], 1.0).then_inc(consts, 1)
            pool.memset(zeros, 0.0).then_inc(consts, 1)
            pool.wait_ge(consts, 2)
            pool.affine_select(out=ident[:, :], in_=zeros[:, 0:P], compare_op=ALU.not_equal, fill=1.0, base=0,
                               pattern=[[-1, P]], channel_multiplier=1).then_inc(consts, 1)
            pool.affine_select(out=tri_le[:, :], in_=ones[:, :], compare_op=ALU.is_ge, fill=0.0, base=0,
                               pattern=[[1, P]], channel_multiplier=-1).then_inc(consts, 1)
            pool.affine_select(out=tri_lt[:, :], in_=ones[:, :], compare_op=ALU.is_gt, fill=0.0, base=0,
                               pattern=[[1, P]], channel_multiplier=-1).then_inc(consts, 1)
            pool.affine_select(out=causal[:, :], in_=zeros, compare_op=ALU.is_ge, fill=NEG, base=P,
                               pattern=[[-1, SEQ]], channel_multiplier=1).then_inc(consts, 1)
            pool.iota(iota_i[:, :], pattern=[[0, 2], [1, SLOTS]], base=0, channel_multiplier=0).then_inc(consts, 1)
            pool.iota(exp_i[:, :], pattern=[[1, NE]], base=0, channel_multiplier=0).then_inc(consts, 1)
            pool.iota(thr_i[:, :], pattern=[[SLOTS, MAXPASS - 1]], base=SLOTS, channel_multiplier=0).then_inc(consts, 1)
            pool.wait_ge(consts, 9)
            pool.tensor_copy(slot_no[:, :], iota_i[:, :]).then_inc(consts, 1)
            pool.tensor_copy(exp_no[:, :], exp_i[:, :]).then_inc(consts, 1)
            pool.tensor_copy(thr[:, :], thr_i[:, :]).then_inc(consts, 1)
            pool.affine_select(out=anti[:, :], in_=zeros[:, 0:P], compare_op=ALU.not_equal, fill=1.0, base=1 - P,
                               pattern=[[1, P]], channel_multiplier=1).then_inc(consts, 1)
            for c in range(NQK):
                s0, w, _, d0 = [x for x in IN_CHUNKS[c][2] if x[2] == "qk"][0]
                for t in range(TT):
                    pool.wait_ge((ev_act, ev_dve)[t], c + 1)
                    if c:
                        pool.wait_ge(qsum, TT * c)
                    q = qk[:, t, d0:d0 + w]
                    pool.tensor_tensor(sq[:, t, 0:w], q, q, ALU.mult).then_inc(qsq, 1)
            for c in range(SPLIT_POOL, NIN):
                s, count = home(c)
                in_chunk_read(pool, c - PAIR)
                pool.wait_ge(landed[s], count)
                pool.tensor_copy(chunk_of(ring_r[rounded(c)], c), chunk_of(ring[s], c)).then_inc(pool_hi, 1)
                pool.wait_ge(pool_hi, c - SPLIT_POOL + 1)
                pool.tensor_tensor(chunk_of(ring_r[s], c), chunk_of(ring[s], c), chunk_of(ring_r[rounded(c)], c),
                                   ALU.subtract).then_inc(pool_lo, 1)
            for j in range(KB):
                pool.wait_ge(br_mul, j + 1)
                pool.tensor_tensor(mT[:, j, :], prod[:, j % 2, 0, :], prod[:, j % 2, 1, :], ALU.add).then_inc(mT_ok, 1)
            pool.wait_ge(tab_ok, 1)
            def select(t, odd, first):
                pool.tensor_copy(cols, table[:, bass.ds(t, 1), :].rearrange("p o c -> p (o c)")).then_inc(col_ok, 1)
                pool.wait_ge(col_ok, t + 1)
                if not first:
                    pool.wait_ge(xg_ps, t)
                    pool.wait_ge(gp_ps, t)
                pool.tensor_tensor(sel_e[:, odd, :], ones[:, 0:SLOTS], cols[:, 4:5].to_broadcast([P, SLOTS]), ALU.mult)
                for tt in range(TT):
                    last = pool.tensor_scalar(pick[:, tt, :], slot_no[:, 0:SLOTS], cols[:, tt:tt + 1], None,
                                              ALU.is_equal)
                last.then_inc(pick_ok, 1)
                for tt in range(TT):
                    last = pool.tensor_scalar(gpick[:, tt, :], slot_no[:, :], cols[:, tt:tt + 1],
                                              cols[:, 2 + tt:3 + tt], ALU.is_equal, ALU.mult)
                last.then_inc(gpick_ok, 1)

            select(0, 0, True)
            pool.wait_ge(tab_ok, MAXPASS + 1)
            pool.wait_ge(cnt_ok, 5)
            pairs = pool.value_load(counts[0:1, 2:3], min_val=NE // 2, max_val=MAXPASS * NE // 2)

            with pool.Fori(0, pairs) as i:
                for u in range(2):
                    pool.wait_ge(gpick_ok, i * 2 + (u + 1))
                    select(i * 2 + (u + 1), 1 - u, False)

        @block.scalar
        def _(act):
            act.dma_start(g1[:, :], a["ln1_g"][0].rearrange("(p k) -> p k", k=KB)).then_inc(g1_in, 16)
            act.wait_ge(consts, 1)
            act.activation(nmax[:, 0:1], ones[:, 0:1], ACT.Sqrt)
            for t in range(TT):
                act.wait_ge(x_in[t], 16)
                if t:
                    act.wait_ge(sq1, t)
                act.activation(reg_t[:, 0:D], xres[:, t, :], ACT.Square,
                               accum_out=stat[:, 0, t:t + 1]).then_inc(sq1, 1)
            act.wait_ge(var1, 1)
            act.activation(stat[:, 2, :], stat[:, 1, :], ACT.Sqrt).then_inc(std1, 1)
            for i in range(4):
                t, half = i // 2, i % 2
                act.wait_ge(hT_raw, i + 1)
                q = (slice(None), slice(4 * half, 4 * half + 4), slice(t * P, (t + 1) * P))
                act.activation(hT_hi[q], hT[q], ACT.Copy).then_inc(hT_hi_ok, 1)

            def round_chunk(c):
                if c >= SPLIT_POOL:
                    return
                if c >= PAIR:
                    in_chunk_read(act, c - PAIR)
                s, count = home(c)
                act.wait_ge(landed[s], count)
                ks = slice(0, KB // 2 if c == 0 else KB)
                act.activation(chunk_of(ring_r[rounded(c)], c)[:, ks, :], chunk_of(ring[s], c)[:, ks, :],
                               ACT.Copy).then_inc(w_hi, 1)

            round_chunk(0)
            round_chunk(1)
            for c in range(GATE0):
                act.wait_ge(proj, 2 * c + 1)
                for s0, w, kind, d0 in IN_CHUNKS[c][2]:
                    dst = {"qk": qk, "v": vals, "f": fz}[kind]
                    last = act.activation(dst[:, 0, d0:d0 + w], bank((2 * c) % 4)[:, s0:s0 + w], ACT.Copy)
                last.then_inc(ev_act, 1)
                round_chunk(c + 2)
                if c == FLIP_AT:
                    for i in range(AH // 2):
                        act.wait_ge(flip_ps, i + 1)
                        act.activation(reg_r[:, i * BANK:(i + 1) * BANK], bank(4 + i % 4), ACT.Copy).then_inc(flip_ok, 1)
            act.wait_ge(qvar, 1)
            act.activation(qstat[:, 1, :, :], qstat[:, 0, :, :], ACT.Sqrt).then_inc(qstd, 1)

            def gates_out(i):
                act.wait_ge(gate_ps, i + 1)
                for j in (2 * i, 2 * i + 1):
                    last = act.activation(gates[:, j, :], bank(5)[:, (j % 2) * SEQ:(j % 2 + 1) * SEQ], ACT.Identity,
                                          bias=bcol[:, j:j + 1])
                last.then_inc(gate_raw, 1)

            act.wait_ge(bcol_ok, 1)
            gates_out(0)
            act.wait_ge(fstep, 2)
            act.activation(fw[:, 1, :, :], fw[:, 0, :, :], ACT.Exp).then_inc(fexp, 1)
            act.wait_ge(fstep, 3)
            act.activation(fw[:, 2, :, :], fw[:, 1, :, :], ACT.Ln).then_inc(fln, 1)
            for what, n in ATTENTION:
                if what == "soft":
                    act.wait_ge(nmx, n + 1)
                    for i in range(2):
                        pr = probs[n % 2][:, i, 0:width(n)]
                        act.activation(pr, pr, ACT.Exp, bias=nmax[:, 2 * n + i:2 * n + i + 1],
                                       accum_out=den[:, 2 * n + i:2 * n + i + 1]).then_inc(pr_ok, 1)
                if what == "turn":
                    act.wait_ge(pT_ps, n + 1)
                    if n >= 4:
                        act.wait_ge(pv, n - 3)
                    w = len(PIECES[n][1]) * P
                    act.activation(probsT[n % 4][:, 0:w], bank(4)[:, 0:w], ACT.Copy).then_inc(pT_ok, 1)
                if what == "fill" and n % (2 * PER_GB) == 2 * PER_GB - 1:
                    if n // (2 * PER_GB):
                        gates_out(n // (2 * PER_GB))
            act.wait_ge(oT_ps, 1)
            act.activation(oT[:, :, 0:P], ps[0][:, 0:6 * P].rearrange("p (k s) -> p k s", k=6),
                           ACT.Copy).then_inc(oT_act, 1)
            gates_out(NGB // 2 - 1)
            act.wait_ge(gate_raw, NGB // 2)
            for j in range(KB):
                g = gates[:, :, :].rearrange("p (b j) s -> p j b s", b=2)[:, j, :, :]
                act.activation(g, g, ACT.Sigmoid).then_inc(gate_ok, 1)
            act.wait_ge(zero_ok, 1)
            act.dma_start(bgu[0:NE, :], a["b_gate_up"][0]).then_inc(ebias_in, 16)
            act.dma_start(bdown[0:NE, :], a["b_down"][0]).then_inc(ebias_in, 16)
            for i in range(2 * TT):
                t, n = i // 2, i % 2
                act.wait_ge(x1_ok, i + 1)
                hs = slice(n * BANK, (n + 1) * BANK)
                act.activation(junk[:, t, hs], xres[:, t, hs], ACT.Square,
                               accum_out=ssq[:, t, n:n + 1]).then_inc(sq2, 1)
                if n == 0:
                    act.wait_ge(x1T_ps, i + 1)
                    act.activation(x1T[:, 0:4, t * P:(t + 1) * P], bank(4 + i).rearrange("p (k s) -> p k s", k=4),
                                   ACT.Copy).then_inc(x1T_act, 1)
            act.wait_ge(norm2, 2)
            act.activation(stat[:, 2, :], stat[:, 1, :], ACT.Sqrt).then_inc(std2, 1)
            act.wait_ge(topm, 1)
            for t in range(TT):
                act.activation(egate[:, t, :], top[:, t, 0:TOPK], ACT.Exp, bias=ntop[:, t:t + 1],
                               accum_out=esum[:, t:t + 1]).then_inc(gexp2, 1)
            for t in range(TT):
                act.activation(hn[:, t, :], xres[:, t, :], ACT.Copy, scale=stat[:, 3, t:t + 1]).then_inc(hn_ok, 1)

            act.wait_ge(cnt_ok, 5)
            last_step = act.value_load(counts[0:1, 0:1], min_val=NE - 1, max_val=MAXPASS * NE - 1)
            act.wait_ge(gp_ps, 1)
            act.activation(gpickT, bank(7)[:, 0:TT * P], ACT.Copy).then_inc(gp_ok, 1)
            act.wait_ge(GT_ps, 1)
            act.activation(GT, bank(6)[0:NE, 0:SEQ], ACT.Copy).then_inc(GT_ok, 1)
            def expert_step(t, last):
                for j in range(2):
                    act.wait_ge(g_ok, 2 * t + j + 1)
                    act.activation(glu_s, glu_g, ACT.Sigmoid, scale=ALPHA).then_inc(sig_ok, 1)
                for j in range(2):
                    act.wait_ge(midT_ps, 2 * t + j + 1)
                    act.activation(midT[:, j, :, :].rearrange("p b s -> p (b s)"), bank(7)[:, 2 * j * P:2 * (j + 1) * P],
                                   ACT.Copy).then_inc(midT_ok, 1)
                act.wait_ge(dn_ps, t + 1)
                act.activation(yb, bank(6), ACT.Copy).then_inc(yb_ok, 1)
                if not last:
                    act.wait_ge(gp_ps, t + 2)
                    act.wait_ge(scat[3], t + 1)
                    act.activation(gpickT, bank(7)[:, 0:TT * P], ACT.Copy).then_inc(gp_ok, 1)

            with act.Fori(0, last_step) as t:
                expert_step(t, False)
            expert_step(last_step, True)
            for t in range(TT):
                act.wait_ge(fin, 2 * t + 2)
                act.dma_start(out[0, t * P:(t + 1) * P, BANK:D], xres[:, t, BANK:D]).then_inc(stored, 16)

        @block.vector
        def _(dve):
            dve.wait_ge(sq1, TT)
            dve.tensor_scalar(stat[:, 1, :], stat[:, 0, :], 1.0 / D, EPS, ALU.mult, ALU.add).then_inc(var1, 1)
            dve.wait_ge(std1, 1)
            dve.reciprocal(stat[:, 3, :], stat[:, 2, :]).then_inc(rstd1, 1)
            dve.wait_ge(rstd1, 1)
            for t in range(TT):
                dve.wait_ge(consts, 13)
                dve.tensor_scalar(h[:, t, :], xres[:, t, :], stat[:, 3, t:t + 1], None, ALU.mult).then_inc(h_ok, 1)
            dve.wait_ge(g1_in, 16)
            dve.wait_ge(h_ok, TT)
            for i in range(4):
                t, half = i // 2, i % 2
                dve.wait_ge(hT_ps, i + 1)
                dve.tensor_tensor(hT[:, 4 * half:4 * half + 4, t * P:(t + 1) * P],
                                  bank(i).rearrange("p (k s) -> p k s", k=4),
                                  g1[:, 4 * half:4 * half + 4].unsqueeze(2).to_broadcast([P, 4, P]),
                                  ALU.mult).then_inc(hT_raw, 1)
            dve.wait_ge(landed[home(0)[0]], home(0)[1])
            ks = slice(KB // 2, KB)
            dve.tensor_copy(chunk_of(ring_r[rounded(0)], 0)[:, ks, :], chunk_of(ring[home(0)[0]], 0)[:, ks, :]).then_inc(
                w0_tail, 1)
            for i in range(4):
                t, half = i // 2, i % 2
                dve.wait_ge(hT_hi_ok, i + 1)
                q = (slice(None), slice(4 * half, 4 * half + 4), slice(t * P, (t + 1) * P))
                dve.tensor_tensor(hT_lo[q], hT[q], hT_hi[q], ALU.subtract).then_inc(hT_lo_ok, 1)

            def rest_of_chunk(c):
                if c >= SPLIT_POOL:
                    return
                s = home(c)[0]
                dve.wait_ge(w_hi, c + 1)
                if c == 0:
                    dve.wait_ge(w0_tail, 1)
                dve.tensor_tensor(chunk_of(ring_r[s], c), chunk_of(ring[s], c), chunk_of(ring_r[rounded(c)], c),
                                  ALU.subtract).then_inc(w_lo, 1)

            rest_of_chunk(0)
            rest_of_chunk(1)
            dve.wait_ge(rel_ps, 1)
            dve.tensor_tensor(rrow, bank(4)[0:AH, 0:TOEP], rmask, ALU.add).then_inc(rel_ok, 1)
            for c in range(GATE0):
                dve.wait_ge(proj, 2 * c + 2)
                for s0, w, kind, d0 in IN_CHUNKS[c][2]:
                    dst = {"qk": qk, "v": vals, "f": fz}[kind]
                    last = dve.tensor_copy(dst[:, 1, d0:d0 + w], bank((2 * c + 1) % 4)[:, s0:s0 + w])
                last.then_inc(ev_dve, 1)
                rest_of_chunk(c + 2)
                if c == 1:
                    dve.wait_ge(small_in, 16 * NSMALL)
                    dve.wait_ge(bcol_ps, 1)
                    dve.tensor_copy(bcol[:, :], bank(5)[:, 0:NGB + KB]).then_inc(bcol_ok, 1)
                    dve.wait_ge(bcol_ok, 1)
                    dve.tensor_tensor(wr[:, :, :], wr[:, :, :], bcol[:, NGB:NGB + KB].unsqueeze(2).to_broadcast([P, KB, NE]),
                                      ALU.mult).then_inc(wr_ok, 1)
                    for i in (0, 2):
                        dve.tensor_scalar(gain[:, i:i + 1], gain[:, i:i + 1], HD ** -0.5, None, ALU.mult).then_inc(gain_ok, 1)
                if 1 <= c <= NQK:
                    s0, w, _, d0 = [x for x in IN_CHUNKS[c - 1][2] if x[2] == "qk"][0]
                    for t in range(TT):
                        dve.wait_ge(qsq, TT * (c - 1) + t + 1)
                        dve.tensor_reduce(qstat[:, 0, t, d0 // HD:(d0 + w) // HD],
                                          sq[:, t, 0:w].rearrange("p (h d) -> p h d", d=HD), AX_X,
                                          ALU.add).then_inc(qsum, 1)
                if c == NQK:
                    dve.wait_ge(qsum, TT * NQK)
                    dve.tensor_scalar(qstat[:, 0, :, :], qstat[:, 0, :, :], 1.0 / HD, EPS, ALU.mult,
                                      ALU.add).then_inc(qvar, 1)
            dve.wait_ge(qstd, 1)
            dve.reciprocal(qstat[:, 0, :, :], qstat[:, 1, :, :]).then_inc(qrstd, 1)
            dve.wait_ge(qrstd, 1)
            dve.wait_ge(gain_ok, 2)
            for i in range(len(QK_BATCHES) * TT):
                t, (b0, nb, gi) = i // len(QK_BATCHES), QK_BATCHES[i % len(QK_BATCHES)]
                if i % len(QK_BATCHES) == 0:
                    q = qk[:, t, :].rearrange("p (h d) -> p h d", d=HD)
                    dve.tensor_tensor(q, q, qstat[:, 0, t, :].unsqueeze(2).to_broadcast([P, QKW // HD, HD]),
                                      ALU.mult).then_inc(qn, 1)
                dve.wait_ge(qT_ps, i + 1)
                dve.tensor_scalar(qkT[:, b0:b0 + nb, t * P:(t + 1) * P],
                                  bank(i % 4)[:, 0:nb * P].rearrange("p (k s) -> p k s", k=nb),
                                  gain[:, gi:gi + 1], None, ALU.mult).then_inc(qT_ok, 1)
                if i == len(QK_BATCHES):
                    dve.wait_ge(ev_act, GATE0)
                    dve.wait_ge(ev_dve, GATE0)
                    dve.tensor_tensor(fz[:, :, :], fz[:, :, :], fbias[:, :].unsqueeze(1).to_broadcast([P, TT, FH]),
                                      ALU.add).then_inc(fstep, 1)
                    dve.wait_ge(fstep, 1)
                    dve.scalar_tensor_tensor(out=fw[:, 0, :, :], in0=fz[:, :, :], scalar=-1.0, in1=fz[:, :, :],
                                             op0=ALU.mult, op1=ALU.min).then_inc(fstep, 1)
                if i == len(QK_BATCHES) + 2:
                    dve.wait_ge(fexp, 1)
                    dve.tensor_scalar(fw[:, 1, :, :], fw[:, 1, :, :], 1.0, None, ALU.add).then_inc(fstep, 1)
            dve.wait_ge(fln, 1)
            dve.scalar_tensor_tensor(out=logf[:, :, :], in0=fz[:, :, :], scalar=0.0, in1=fw[:, 2, :, :], op0=ALU.min,
                                     op1=ALU.subtract).then_inc(logf_ok, 1)
            dve.wait_ge(consts, 13)

            def attn_out(n, u0, u1, src, dst):
                dve.wait_ge(pr_ok, u1)
                dve.reciprocal(rden[:, u0:u1], den[:, u0:u1]).then_inc(rden_ok, 1)
                dve.wait_ge(rden_ok, n)
                dve.wait_ge(pv, 1 + max(i for i, (p, _) in enumerate(PIECES) if 2 * p < u1))
                dve.tensor_tensor(dst.rearrange("p (u d) -> p u d", d=HD), src.rearrange("p (u d) -> p u d", d=HD),
                                  rden[:, u0:u1].unsqueeze(2).to_broadcast([P, u1 - u0, HD]), ALU.mult).then_inc(o_ok, 1)

            for what, p in ATTENTION:
                if what != "scores":
                    continue
                kind, t, s0 = PAIRS[p]
                nk = keys(p)
                dve.wait_ge(sc_ps, p + 1)
                if p >= 2:
                    dve.wait_ge(pT_ps, 1 + max(i for i, (v, _) in enumerate(PIECES) if v == p - 2))
                if p == 0:
                    dve.wait_ge(flip_ok, AH // 2)
                if p == NPA:
                    dve.wait_ge(cum_ok, 2)
                for i in range(2):
                    if kind == "a":
                        dve.tensor_tensor(probs[p % 2][:, i, 0:3 * nk].rearrange("p (g c) -> p g c", g=3),
                                          ps[i][:, 0:3 * SEQ].rearrange("p (g c) -> p g c", g=3)[:, :, 0:nk],
                                          toep[:, :, :].rearrange("p (g s) c -> p g s c", g=3)[:, :, s0 + i, SEQ - nk:SEQ],
                                          ALU.add).then_inc(sc_add, 1)
                    else:
                        dve.scalar_tensor_tensor(out=probs[p % 2][:, i, 0:nk], in0=bank(2 * i + p % 2)[:, 0:nk],
                                                 scalar=cum[:, t, s0 + i:s0 + i + 1], in1=causal[:, SEQ - nk:SEQ],
                                                 op0=ALU.add, op1=ALU.add).then_inc(sc_add, 1)
                dve.wait_ge(sc_add, 2 * p + 2)
                dve.tensor_reduce(amax[:, 2 * p:2 * p + 2], probs[p % 2][:, :, 0:width(p)], AX_X, ALU.max).then_inc(mx, 1)
                dve.wait_ge(mx, p + 1)
                dve.tensor_scalar(nmax[:, 2 * p:2 * p + 2], amax[:, 2 * p:2 * p + 2], -1.0, None, ALU.mult).then_inc(nmx, 1)
                if p == 0:
                    dve.wait_ge(cum_ps, 1)
                    dve.tensor_copy(cum[:, :, :], bank(6)[:, 0:TT * FH].rearrange("p (t h) -> p t h", t=TT)).then_inc(cum_ok, 1)
                    dve.tensor_scalar(negcT[:, :], bank(7)[0:FH, 0:SEQ], -1.0, None, ALU.mult).then_inc(cum_ok, 1)
                    dve.tensor_copy(ck_sel[0:FH, :], ident[0:FH, 0:FH]).then_inc(ck_ok, 1)
                    dve.wait_ge(cum_ok, 2)
                    dve.tensor_copy(ck[0], negcT[:, :]).then_inc(ck_ok, 1)
                    dve.wait_ge(ck_ok, 2)
                    dve.tensor_tensor(ck[1], negcT[:, :], ck[0], ALU.subtract).then_inc(ck_ok, 1)
                if p == NPA + 1:
                    attn_out(1, 0, NUA, bank(6), o_a.rearrange("p t d -> p (t d)"))
                if p == NPA + FH // 2 + 1:
                    attn_out(2, NUA, NUA + FH, bank(7), o_b[:, 0, :])
            attn_out(3, NUA + FH, NU, bank(6), o_b[:, 1, :])
            dve.memset(bgu[:, :], 0.0).then_inc(zero_ok, 1)
            dve.wait_ge(oT_ps, 2)
            dve.tensor_copy(oT[:, :, P:SEQ], ps[1][:, 0:6 * P].rearrange("p (k s) -> p k s", k=6)).then_inc(oT_dve, 1)
            for j in range(KB):
                dve.wait_ge(br_ps, j + 1)
                dve.wait_ge(gate_ok, j + 1)
                if j >= 2:
                    dve.wait_ge(mT_ok, j - 1)
                dve.tensor_tensor(prod[:, j % 2, :, :], bank(4 + j % 4).rearrange("p (b s) -> p b s", b=2),
                                  gates[:, :, :].rearrange("p (b j) s -> p j b s", b=2)[:, j, :, :],
                                  ALU.mult).then_inc(br_mul, 1)
            dve.wait_ge(x2_in, 16 * TT)
            for i in range(2 * TT):
                t, n = i // 2, i % 2
                dve.wait_ge(wo_ps, i + 1)
                xs = xres[:, t, n * BANK:(n + 1) * BANK]
                dve.tensor_tensor(xs, bank(i), xs, ALU.add).then_inc(x1_ok, 1)
                if n:
                    dve.wait_ge(x1T_ps, i + 1)
                    dve.tensor_copy(x1T[:, 4:8, t * P:(t + 1) * P],
                                    bank(4 + i).rearrange("p (k s) -> p k s", k=4)).then_inc(x1T_dve, 1)
            dve.wait_ge(sq2, 2 * TT)
            dve.tensor_tensor(stat[:, 0, :], ssq[:, :, 0], ssq[:, :, 1], ALU.add).then_inc(norm2, 1)
            dve.wait_ge(norm2, 1)
            dve.tensor_scalar(stat[:, 1, :], stat[:, 0, :], 1.0 / D, EPS, ALU.mult, ALU.add).then_inc(norm2, 1)
            dve.wait_ge(std2, 1)
            dve.reciprocal(stat[:, 3, :], stat[:, 2, :]).then_inc(norm2, 1)
            dve.wait_ge(norm2, 3)
            dve.wait_ge(lg_ps, TT)
            for t in range(TT):
                dve.scalar_tensor_tensor(out=logits[:, t, :], in0=bank(0)[:, t * NE:(t + 1) * NE],
                                         scalar=stat[:, 3, t:t + 1], in1=rbias[:, :], op0=ALU.mult,
                                         op1=ALU.add).then_inc(lg_ok, 1)
            dve.wait_ge(lg_ok, TT)
            for t in range(TT):
                dve.max(top[:, t, :], logits[:, t, :]).then_inc(tops, 1)
            dve.wait_ge(tops, TT)
            for t in range(TT):
                dve.max_index(topi[:, t, :], top[:, t, :], logits[:, t, :]).then_inc(tops, 1)
            dve.tensor_scalar(ntop[:, :], top[:, :, 0], -1.0, None, ALU.mult).then_inc(topm, 1)
            dve.wait_ge(tops, 2 * TT)
            dve.tensor_copy(topf[:, :, :], topi[:, :, 0:TOPK]).then_inc(rt, 1)
            dve.wait_ge(rt, 1)
            hs = [P, TT, TOPK, NE]
            dve.tensor_tensor(hit, exp_no[:, :].unsqueeze(1).unsqueeze(1).to_broadcast(hs),
                              topf[:, :, :].unsqueeze(3).to_broadcast(hs), ALU.is_equal).then_inc(rt, 1)
            dve.wait_ge(rt, 2)
            dve.tensor_reduce(mask[:, :, :], hit.rearrange("p t k e -> p t e k"), AX_X,
                              ALU.add).then_inc(mask_ok, 1)
            dve.wait_ge(gexp2, TT)
            dve.reciprocal(ersum[:, :], esum[:, :]).then_inc(rt, 1)
            dve.wait_ge(rt, 3)
            dve.tensor_tensor(egate[:, :, :], egate[:, :, :], ersum[:, :].unsqueeze(2).to_broadcast([P, TT, TOPK]),
                              ALU.mult).then_inc(rt, 1)
            dve.wait_ge(rt, 4)
            dve.tensor_tensor(ghit, hit, egate[:, :, :].unsqueeze(3).to_broadcast(hs),
                              ALU.mult).then_inc(rt, 1)
            dve.wait_ge(rt, 5)
            dve.tensor_reduce(G[:, :, :], ghit.rearrange("p t k e -> p t e k"), AX_X,
                              ALU.add).then_inc(rt, 1)
            dve.wait_ge(pos_ps, 1)
            dve.scalar_tensor_tensor(out=posm[:, :, :], in0=mask[:, :, :], scalar=-BIG,
                                     in1=bank(4)[:, 0:TT * NE].rearrange("p (t e) -> p t e", t=TT), op0=ALU.mult,
                                     op1=ALU.add).then_inc(rt, 1)
            dve.wait_ge(rt, 7)
            for q in range(MAXPASS):
                rows = table[:, q * NE:(q + 1) * NE, :].rearrange("p e c -> p c e")
                dve.tensor_scalar(rows[:, 0:TT, :], posm[:, :, :], BIG - SLOTS * q, None, ALU.add)
                dve.tensor_copy(rows[:, TT:2 * TT, :], G[:, :, :])
                dve.tensor_copy(rows[:, 2 * TT, :], ident[:, 0:NE]).then_inc(tab_ok, 1)
            dve.memset(table[:, MAXPASS * NE, :], BIG).then_inc(tab_ok, 1)
            dve.wait_ge(tot_ps, 1)
            dve.tensor_reduce(cmax[:, :], bank(5)[:, 0:NE], AX_X, ALU.max).then_inc(cnt_ok, 1)
            dve.wait_ge(cnt_ok, 1)
            dve.tensor_scalar(over[:, :], thr[:, :], cmax[:, 0:1], None, ALU.is_lt).then_inc(rt, 1)
            dve.wait_ge(rt, 8)
            dve.tensor_reduce(more[:, :], over[:, :], AX_X, ALU.add).then_inc(rt, 1)
            dve.wait_ge(rt, 9)
            dve.tensor_scalar(counts[:, 0:1], more[:, :], float(NE), NE - 1.0, ALU.mult, ALU.add).then_inc(cnt_ok, 1)
            dve.tensor_scalar(counts[:, 1:2], more[:, :], 1.0, None, ALU.add).then_inc(cnt_ok, 1)
            dve.tensor_scalar(counts[:, 2:3], more[:, :], NE / 2, NE / 2, ALU.mult, ALU.add).then_inc(cnt_ok, 1)
            dve.tensor_scalar(counts[:, 3:4], more[:, :], NE / 2, NE / 2 - 1, ALU.mult, ALU.add).then_inc(cnt_ok, 1)

            def gathered(t):
                dve.wait_ge(xg_ps, t + 1)
                dve.tensor_tensor(xT, bank(4).rearrange("p (k s) -> p k s", k=KB),
                                  g2[:, :].unsqueeze(2).to_broadcast([P, KB, SLOTS]), ALU.mult).then_inc(xg_ok, 1)

            dve.wait_ge(cnt_ok, 5)
            last_step = dve.value_load(counts[0:1, 0:1], min_val=NE - 1, max_val=MAXPASS * NE - 1)
            gathered(0)

            def activations(t):
                for j in range(2):
                    dve.wait_ge(gu_ps, 2 * t + j + 1)
                    if j:
                        dve.wait_ge(mid_ok, 2 * t + 1)
                    dve.tensor_scalar(glu_g, bank(4 + j)[:, 0:2 * P], LIMIT, None, ALU.min).then_inc(g_ok, 1)
                    dve.tensor_scalar(glu_u, bank(4 + j)[:, 2 * P:4 * P], LIMIT, -LIMIT, ALU.min, ALU.max).then_inc(u_ok, 1)
                    dve.wait_ge(u_ok, 2 * t + j + 1)
                    dve.wait_ge(g_ok, 2 * t + j + 1)
                    dve.scalar_tensor_tensor(out=glu_u, in0=glu_u, scalar=1.0, in1=glu_g, op0=ALU.add,
                                             op1=ALU.mult).then_inc(ug_ok, 1)
                    dve.wait_ge(ug_ok, 2 * t + j + 1)
                    dve.wait_ge(sig_ok, 2 * t + j + 1)
                    if j:
                        dve.wait_ge(midT_ps, 2 * t + 1)
                    dve.tensor_tensor(mid, glu_u, glu_s, ALU.mult).then_inc(mid_ok, 1)

            with dve.Fori(0, last_step) as t:
                activations(t)
                gathered(t + 1)
            activations(last_step)
            for i in range(2 * TT):
                dve.wait_ge(scat[i], last_step + 1)
                t, n = i // 2, i % 2
                xs = xres[:, t, n * BANK:(n + 1) * BANK]
                dve.tensor_tensor(xs, bank(i), xs, ALU.add).then_inc(fin, 1)

        @block.tensor
        def _(pe):
            dma_done = lambda n: pe.wait_ge(landed[home(n)[0]], home(n)[1])
            def keep_warm(n):
                for _ in range(n):
                    pe.matmul(bank(6)[:, 0:P], ident[:, :], ones[:, :], start=True, stop=True)

            pe.wait_ge(consts, 3)
            keep_warm(16)
            for i in range(4):
                t, half = i // 2, i % 2
                pe.wait_ge(h_ok, t + 1)
                for k in range(4):
                    last = pe.transpose(bank(i)[:, k * P:(k + 1) * P],
                                        h[:, t, :].rearrange("p (q k) -> p k q", k=KB)[:, 4 * half + k, :], ident[:, :])
                last.then_inc(hT_ps, 1)
            def turn_rows():
                pe.wait_ge(small_in, 16 * NSMALL)
                pe.transpose(bank(5)[:, 0:NGB + KB], brow[:, :], ident[0:NGB + KB, 0:NGB + KB]).then_inc(bcol_ps, 1)

            def split_done(c, i):
                if c >= SPLIT_POOL:
                    if i == 0:
                        pe.wait_ge(pool_lo, c - SPLIT_POOL + 1)
                elif i == 0:
                    pe.wait_ge(w_hi, c + 1)
                    if c == 0:
                        pe.wait_ge(w0_tail, 1)
                elif i == 2:
                    pe.wait_ge(w_lo, c + 1)
                if c == 0 and i == 1:
                    pe.wait_ge(hT_lo_ok, 4)

            def operands(c, i):
                x = hT_lo if i == 1 else hT_hi
                return x, chunk_of(ring_r[home(c)[0] if i == 2 else rounded(c)], c)

            def project(c):
                w = IN_CHUNKS[c][1]
                order = [(t, i) for i in range(3) for t in range(TT)] if c == 0 else [
                    (t, i) for t in range(TT) for i in range(3)]
                for t, i in order:
                    if c >= 2 and i == 0:
                        pe.wait_ge((ev_act, ev_dve)[t], c - 1)
                    if t == 0:
                        split_done(c, i)
                    x, wt = operands(c, i)
                    for k in range(KB):
                        last = pe.matmul(bank((2 * c + t) % 4)[:, 0:w], x[:, k, t * P:(t + 1) * P], wt[:, k, :],
                                         start=(i == 0 and k == 0), stop=(i == 2 and k == KB - 1))
                    if i == 2:
                        last.then_inc(proj, 1)

            def fill(n):
                j, m = n // PER_GB, n % PER_GB
                c, b = GATE0 + j // 4, j % 4
                i, k = m // KB, m % KB
                if m == 0 and j % 2 == 0 and j:
                    pe.wait_ge(gate_raw, j // 2)
                if b == 0 and k == 0:
                    split_done(c, i)
                x, wt = operands(c, i)
                mm = pe.matmul(bank(5)[:, (j % 2) * SEQ:(j % 2 + 1) * SEQ], wt[:, k, b * P:(b + 1) * P], x[:, k, :],
                               start=(m == 0), stop=(m == PER_GB - 1))
                if m == PER_GB - 1 and j % 2:
                    mm.then_inc(gate_ps, 1)

            keep_warm(12)
            pe.wait_ge(hT_hi_ok, 4)
            for c in range(GATE0):
                project(c)
                if c == 0:
                    pe.wait_ge(rel_op_in, 48)
                    pe.matmul(bank(4)[0:AH, 0:TOEP], rel, onehot, start=True, stop=True).then_inc(rel_ps, 1)
                if c == FLIP_AT - 1:
                    turn_rows()
                if c == FLIP_AT:
                    pe.wait_ge(bcol_ok, 1)
                    pe.wait_ge(rel_in, 16)
                    pe.wait_ge(consts, 13)
                    for i in range(AH // 2):
                        if i >= 4:
                            pe.wait_ge(flip_ok, i - 3)
                        pe.matmul(bank(4 + i % 4), anti[:, :], reg_r[:, i * BANK:(i + 1) * BANK], start=True,
                                  stop=True).then_inc(flip_ps, 1)
            pe.wait_ge(flip_ok, AH // 2)
            for i in range(len(QK_BATCHES) * TT):
                t, (b0, nb, _) = i // len(QK_BATCHES), QK_BATCHES[i % len(QK_BATCHES)]
                if i % len(QK_BATCHES) == 0:
                    for n in range(t * 2 * PER_GB, (t + 1) * 2 * PER_GB):
                        fill(n)
                pe.wait_ge(qn, t + 1)
                if i >= 4:
                    pe.wait_ge(qT_ok, i - 3)
                for k in range(nb):
                    last = pe.transpose(bank(i % 4)[:, k * P:(k + 1) * P], qk[:, t, (b0 + k) * P:(b0 + k + 1) * P],
                                        ident[:, :])
                last.then_inc(qT_ps, 1)

            def cumulate():
                pe.wait_ge(logf_ok, 1)
                pe.wait_ge(consts, 13)
                pe.matmul(bank(6)[:, 0:FH], tri_le[:, :], logf[:, 0, :], start=True, stop=True)
                pe.matmul(bank(6)[:, FH:2 * FH], ones[:, :], logf[:, 0, :], start=True, stop=False)
                pe.matmul(bank(6)[:, FH:2 * FH], tri_le[:, :], logf[:, 1, :], start=False, stop=True)
                pe.matmul(bank(7)[0:FH, 0:P], logf[:, 0, :], tri_le[:, :], start=True, stop=True)
                pe.matmul(bank(7)[0:FH, P:SEQ], logf[:, 0, :], ones[:, :], start=True, stop=False)
                pe.matmul(bank(7)[0:FH, P:SEQ], logf[:, 1, :], tri_le[:, :], start=False, stop=True).then_inc(cum_ps, 1)

            def scores(p):
                kind, t, s0 = PAIRS[p]
                nk = keys(p)
                if p:
                    pe.wait_ge(sc_add, 2 * (p if p <= NPA else p - 1))
                out = [ps[i][:, :] if kind == "a" else bank(2 * i + p % 2) for i in range(2)]
                if kind == "b":
                    if p == NPA:
                        pe.wait_ge(ck_ok, 3)
                    for i in range(2):
                        for part in ck:
                            pe.matmul(out[i][:, 0:nk], ck_sel[0:FH, s0 + i:s0 + i + 1].to_broadcast([FH, P]),
                                      part[:, 0:nk], start=(part is ck[0]), stop=False)
                for g in range(GROUPS if kind == "a" else 1):
                    for i in range(2):
                        hd = g * SLOTHEADS + s0 + i if kind == "a" else s0 + i
                        qb, kb = (hd // 2, AH // 2 + hd // 2) if kind == "a" else (AH + hd // 2, AH + FH // 2 + hd // 2)
                        last = pe.matmul(out[i][:, g * SEQ:g * SEQ + nk], qkT[i * HD:(i + 1) * HD, qb, t * P:(t + 1) * P],
                                         qkT[i * HD:(i + 1) * HD, kb, 0:nk], start=(kind == "a"), stop=True)
                last.then_inc(sc_ps, 1)

            def turn(n):
                p, bs = PIECES[n]
                pe.wait_ge(pr_ok, 2 * p + 2)
                if n:
                    pe.wait_ge(pT_ok, n)
                for m, (i, g, k) in enumerate(bs):
                    o = g * keys(p) + k * P
                    last = pe.transpose(bank(4)[:, m * P:(m + 1) * P], probs[p % 2][:, i, o:o + P], ident[:, :])
                last.then_inc(pT_ps, 1)

            def values(n):
                p, bs = PIECES[n]
                kind, t, s0 = PAIRS[p]
                pe.wait_ge(pT_ok, n + 1)
                if p == NPA + FH // 2:
                    pe.wait_ge(o_ok, 1)
                ob = bank(6) if kind == "a" or t == 1 else bank(7)
                for m, (i, g, k) in enumerate(bs):
                    o = (t * SLOTHEADS + s0 + i if kind == "a" else s0 + i) * HD
                    v0 = (g * SLOTHEADS + s0 + i) * HD if kind == "a" else AW + (s0 + i) * HD
                    last = pe.matmul(ob[:, o:o + HD], probsT[n % 4][:, m * P:(m + 1) * P], vals[:, k, v0:v0 + HD],
                                     start=((i, g, k) == (i, 0, 0)),
                                     stop=(k == t and g == (GROUPS - 1 if kind == "a" else 0)))
                last.then_inc(pv, 1)

            keep_warm(9)
            pe.wait_ge(qT_ok, len(QK_BATCHES) * TT)
            for what, n in ATTENTION:
                if what == "fill" and n >= 4 * PER_GB:
                    fill(n)
                if what == "scores":
                    scores(n)
                    if n == 0:
                        cumulate()
                if (what, n) == ("values", 0):
                    pe.wait_ge(cum_ok, 2)
                if what == "turn":
                    turn(n)
                if what == "values":
                    values(n)
            pe.wait_ge(o_ok, 3)
            for t in range(TT):
                for b in range(6):
                    src = o_a[:, t, b * P:(b + 1) * P] if b < 2 else o_b[:, t, (b - 2) * P:(b - 1) * P]
                    last = pe.transpose(ps[t][:, b * P:(b + 1) * P], src, ident[:, :])
                last.then_inc(oT_ps, 1)
            for n in range(FILLS - LATE, FILLS):
                fill(n)
            dma_done(NIN)
            dma_done(NIN + 1)
            pe.wait_ge(oT_act, 1)
            pe.wait_ge(oT_dve, 1)
            for j in range(KB):
                if j == 1:
                    pe.wait_ge(gate_raw, NGB // 2)
                if j >= 4:
                    pe.wait_ge(br_mul, j - 3)
                for b, ks in ((0, range(0, 2)), (1, range(2, 6))):
                    for k in ks:
                        w = ring[home(NIN + k // 4)[0]]
                        last = pe.matmul(bank(4 + j % 4)[:, b * SEQ:(b + 1) * SEQ],
                                         w[:, (k % 4) * D + j * P:(k % 4) * D + (j + 1) * P], oT[:, k, :],
                                         start=(k == ks[0]), stop=(k == ks[-1]))
                last.then_inc(br_ps, 1)
            def turn_x1(i):
                t, half = i // 2, i % 2
                pe.wait_ge(x1_ok, i + 1)
                for k in range(4):
                    b = 4 * half + k
                    last = pe.transpose(bank(4 + i)[:, k * P:(k + 1) * P], xres[:, t, b * P:(b + 1) * P], ident[:, :])
                last.then_inc(x1T_ps, 1)

            def route(t):
                if t == 0:
                    pe.wait_ge(wr_ok, 1)
                for k in range(KB):
                    if k % 4 == 0:
                        pe.wait_ge((x1T_act, x1T_dve)[k // 4], t + 1)
                    last = pe.matmul(bank(0)[:, t * NE:(t + 1) * NE], x1T[:, k, t * P:(t + 1) * P], wr[:, k, :],
                                     start=(k == 0), stop=(k == KB - 1))
                last.then_inc(lg_ps, 1)

            dma_done(NIN + 2)
            dma_done(NIN + 3)
            for i in range(2 * TT):
                t, n = i // 2, i % 2
                for k in range(KB):
                    if i == 0:
                        pe.wait_ge(mT_ok, k + 1)
                    if i == 2 * TT - 1 and k == KB // 2:
                        route(0)
                    w = ring[home(NIN + 2 + k // 4)[0]]
                    last = pe.matmul(bank(i), mT[:, k, t * P:(t + 1) * P],
                                     w[:, (k % 4) * D + n * BANK:(k % 4) * D + (n + 1) * BANK],
                                     start=(k == 0), stop=(k == KB - 1))
                last.then_inc(wo_ps, 1)
                if i:
                    turn_x1(i - 1)
            turn_x1(2 * TT - 1)
            route(1)
            keep_warm(11)
            pe.wait_ge(mask_ok, 1)
            pe.matmul(bank(4)[:, 0:NE], tri_lt[:, :], mask[:, 0, :], start=True, stop=True)
            pe.matmul(bank(4)[:, NE:2 * NE], ones[:, :], mask[:, 0, :], start=True, stop=False)
            pe.matmul(bank(4)[:, NE:2 * NE], tri_lt[:, :], mask[:, 1, :], start=False, stop=True).then_inc(pos_ps, 1)
            pe.matmul(bank(5)[:, 0:NE], ones[:, :], mask[:, 0, :], start=True, stop=False)
            pe.matmul(bank(5)[:, 0:NE], ones[:, :], mask[:, 1, :], start=False, stop=True).then_inc(tot_ps, 1)
            keep_warm(9)

            def add_biases(t):
                pe.wait_ge(GT_ok, 1)
                for n in range(2):
                    pe.matmul(bank(2 * t + n), GT[:, t * P:(t + 1) * P], bdown[0:NE, n * BANK:(n + 1) * BANK],
                              start=False, stop=False, skip_group_check=True)

            def gather(t):
                pe.wait_ge(pick_ok, t + 1)
                for k in range(KB):
                    for tt in range(TT):
                        last = pe.matmul(bank(4)[:, k * SLOTS:(k + 1) * SLOTS],
                                         hn[:, tt, :].rearrange("p (q k) -> p k q", k=KB)[:, k, :], pick[:, tt, :],
                                         start=(tt == 0), stop=(tt == TT - 1))
                last.then_inc(xg_ps, 1)

            def turn_gates(t):
                pe.wait_ge(gpick_ok, t + 1)
                for tt in range(TT):
                    last = pe.transpose(bank(7)[:, tt * P:(tt + 1) * P], gpick[:, tt, :], ident[:, :])
                last.then_inc(gp_ps, 1)

            def turn_mid(t, j):
                pe.wait_ge(mid_ok, t * 2 + (j + 1))
                if j:
                    pe.wait_ge(midT_ok, t * 2 + 1)
                for b in range(2):
                    last = pe.transpose(bank(7)[:, (2 * j + b) * P:(2 * j + b + 1) * P], mid[:, b * P:(b + 1) * P],
                                        ident[:, :])
                last.then_inc(midT_ps, 1)

            def chunk(i, u, c):
                s = eslot(c, u == 1)
                uses = i + 1 if c < EXTRA else i * 2 + (u + 1)
                pe.wait_ge(landed[s], uses * eland(c) + pre_land[s])

            def down(i, u, half):
                if half:
                    pe.wait_ge(landed_half, i * 32 + (16 * u + 16))
                else:
                    chunk(i, u, 4)
                pe.wait_ge(midT_ok, i * 4 + (2 * u + half + 1))
                w = slots[eslot(4 + half, u == 1)]
                for k in range(4):
                    if half and k == 2:
                        chunk(i, u, 5)
                    for n in range(2):
                        last = pe.matmul(bank(6)[n * SLOTS:(n + 1) * SLOTS, :],
                                         midT[:, half, k % 2, (k // 2) * SLOTS:(k // 2 + 1) * SLOTS],
                                         w[:, k * D + n * BANK:k * D + (n + 1) * BANK],
                                         start=(half == 0 and k == 0), stop=(half == 1 and k == 3))
                last.then_inc((used, dn_ps)[half], 1)

            pe.wait_ge(ebias_in, 32)
            pe.wait_ge(hn_ok, TT)
            gather(0)
            turn_gates(0)
            pe.wait_ge(rt, 6)
            for t in range(TT):
                last = pe.transpose(bank(6)[0:NE, t * P:(t + 1) * P], G[:, t, :], ident[:, :])
            last.then_inc(GT_ps, 1)

            def step_pair(i, first=False, last=False):
                for u in range(2):
                    t = i * 2 + u
                    pe.wait_ge(xg_ok, t + 1)
                    for j in range(2):
                        gu = bank(4 + j)
                        for kh in range(2):
                            chunk(i, u, 2 * j + kh)
                            w = slots[eslot(2 * j + kh, u == 1)].rearrange("p (k w n c) -> p k w n c", k=4, w=2, n=2)
                            for k in range(4):
                                for n in range(2):
                                    mm = pe.matmul(gu[n * SLOTS:(n + 1) * SLOTS, :], xT[:, 4 * kh + k, :],
                                                   w[:, k, :, n, :], start=(kh == 0 and k == 0),
                                                   stop=(kh == 1 and k == 3))
                            if kh == 0:
                                mm.then_inc(used, 1)
                                for n in range(2):
                                    pe.matmul(gu[n * SLOTS:(n + 1) * SLOTS, :], sel_e[:, u, :],
                                              bgu.rearrange("p (w j n c) -> p w j n c", w=2, j=2, n=2)[:, :, j, n, :],
                                              start=False, stop=False)
                        mm.then_inc(gu_ps, 1)
                    pe.wait_ge(gp_ok, t + 1)
                    turn_mid(t, 0)
                    more = not (last and u == 1)
                    if more:
                        gather(t + 1)
                    else:
                        add_biases(1)
                        down(i, u, 0)
                    turn_mid(t, 1)
                    if more:
                        down(i, u, 0)
                    down(i, u, 1)
                    if more:
                        turn_gates(t + 1)
                    if last and u == 0:
                        add_biases(0)
                    pe.wait_ge(yb_ok, t + 1)
                    for tt in range(TT):
                        for n in range(2):
                            pe.matmul(bank(2 * tt + n), gpickT[n * SLOTS:(n + 1) * SLOTS, tt * P:(tt + 1) * P],
                                      yb[n * SLOTS:(n + 1) * SLOTS, :], start=(first and u == 0), stop=False,
                                      skip_group_check=True).then_inc(scat[2 * tt + n], 1)

            step_pair(0, first=True)
            pe.wait_ge(cnt_ok, 5)
            last_pair = pe.value_load(counts[0:1, 3:4], min_val=NE // 2 - 1, max_val=MAXPASS * NE // 2 - 1)
            with pe.Fori(1, last_pair) as i:
                step_pair(i)
            step_pair(last_pair, last=True)


def _tables():
    max_exact, max_distance = NB // 2, 2048
    dist = 2 * P - 1 - np.arange(TOEP)
    n = np.maximum(dist, 0)
    large = max_exact + (np.log(np.maximum(n, 1).astype(np.float64) / max_exact) / np.log(max_distance / max_exact)
                         * (NB - max_exact)).astype(np.int64)
    bucket = np.where(n < max_exact, n, np.minimum(large, NB - 1))
    onehot = ((np.arange(NB)[:, None] == bucket[None, :]) & (dist >= 0)[None, :]).astype(np.float32)
    reach = np.zeros((AH, TOEP), np.float32)
    for g, (window, dilation) in enumerate(((128, 1), (512, 4), (2048, 16))):
        ok = (dist >= 0) & (dist % dilation == 0) & (dist <= window)
        reach[g * SLOTHEADS:(g + 1) * SLOTHEADS] = np.where(ok, 0.0, NEG)
    return onehot, reach


_INS = ["x", "ln1_g", "w_in", "b_forget", "b_gate", "q_norm_a", "k_norm_a", "q_norm_b", "k_norm_b", "rel_bias",
        "w_branch_a", "w_branch_b", "w_out", "ln2_g", "w_router", "b_router", "w_gate_up", "b_gate_up", "w_down",
        "b_down"]


def kernel(**inputs):
    import numpy as _np
    import concourse.bacc as _bacc
    from concourse import mybir as _mybir
    from concourse.bass_utils import run_bass_kernel_spmd as _run

    nc = _bacc.Bacc("TRN2", target_bir_lowering=False, num_devices=1)
    arrays, args = {}, {}
    given = {n: _np.ascontiguousarray(inputs[n]) for n in _INS}
    given["bucket_onehot"], given["reach_mask"] = _tables()
    for name, v in given.items():
        arrays[f"in_{name}"] = v
        args[name] = nc.dram_tensor(f"in_{name}", v.shape, _mybir.dt.from_np(v.dtype), kind="ExternalInput").ap()
    out = nc.dram_tensor("out_0", (1, SEQ, D), F32, kind="ExternalOutput").ap()
    build(nc, args, out)
    r = _run(nc, [arrays], core_ids=[0])
    return r.results[0]["out_0"]
```
